# Optimizing a Trainium2 kernel written in Bass

```python
import jax
import jax.numpy as jnp
from jax import lax
import numpy as np

D_MODEL = 2048
BATCH = 1
SEQ = 512
DEPTH = 1

N_META = 16
POOL_GROUPS = 4
POOL_WINDOWS = (2, 4, 8, 16)
POOL_WIDTH = D_MODEL // 2
POOL_GROUP_DIM = POOL_WIDTH // POOL_GROUPS
DN_HEADS = 16
DN_HEAD_DIM = 128
DN_WIDTH = DN_HEADS * DN_HEAD_DIM
CONV_WIDTH = 4
CHUNK = 64
NORM_EPS = 1e-6
IN_SPLIT_SIZES = (POOL_WIDTH, POOL_WIDTH, DN_WIDTH, DN_WIDTH, DN_WIDTH, DN_WIDTH, DN_HEADS, DN_HEADS, D_MODEL, D_MODEL)
IN_COLS = 2 * POOL_WIDTH + 4 * DN_WIDTH + 2 * DN_HEADS + 2 * D_MODEL

kernel_name = "hybrid_pool_gated_deltanet_block"

def rmsnorm(x, w):
    xf = x.astype(jnp.float32)
    y = xf * lax.rsqrt(jnp.mean(xf * xf, axis=-1, keepdims=True) + NORM_EPS)
    return (y * w.astype(jnp.float32)).astype(x.dtype)

def l2norm(x):
    return x * lax.rsqrt(jnp.sum(x * x, axis=-1, keepdims=True) + NORM_EPS)

def causal_multiscale_pool(u, mix_w, scale):
    Bsz, L, _ = u.shape
    uf = u.astype(jnp.float32)
    csum = jnp.concatenate([jnp.zeros((Bsz, 1, POOL_WIDTH), jnp.float32), jnp.cumsum(uf, axis=1)], axis=1)
    t = jnp.arange(1, L + 1)
    pooled = []
    for gi, w in enumerate(POOL_WINDOWS):
        c = csum[..., gi * POOL_GROUP_DIM:(gi + 1) * POOL_GROUP_DIM]
        lag = jnp.pad(c, ((0, 0), (w, 0), (0, 0)))[:, :L + 1]
        cnt = jnp.minimum(t, w).astype(jnp.float32)[None, :, None]
        pooled.append((c[:, 1:] - lag[:, 1:]) / cnt)
    pooled = jnp.concatenate(pooled, axis=-1) - uf
    pooled = pooled.reshape(Bsz, L, POOL_GROUPS, POOL_GROUP_DIM)
    mixed = jnp.einsum('blgc,gcd->blgd', pooled, mix_w.astype(jnp.float32)).reshape(Bsz, L, POOL_WIDTH)
    return mixed * scale.astype(jnp.float32)

def causal_depthwise_conv_silu(x, w):
    K = w.shape[0]
    L = x.shape[1]
    xp = jnp.pad(x, ((0, 0), (K - 1, 0), (0, 0)))
    y = xp[:, K - 1:K - 1 + L] * w[K - 1]
    for kk in range(K - 1):
        y = y + xp[:, kk:kk + L] * w[kk]
    return jax.nn.silu(y)

def chunk_gated_delta_rule(q, k, v, beta, g):
    Bsz, Lp, H, Dk = q.shape
    Dv = v.shape[-1]
    N = Lp // CHUNK

    def to_chunks(t):
        return jnp.moveaxis(t.reshape((Bsz, N, CHUNK) + t.shape[2:]), 3, 1)

    q, k, v, beta, g = to_chunks(q), to_chunks(k), to_chunks(v), to_chunks(beta), to_chunks(g)
    gcum = jnp.cumsum(g, axis=-1)
    causal = jnp.tril(jnp.ones((CHUNK, CHUNK), bool))
    strict = jnp.tril(jnp.ones((CHUNK, CHUNK), bool), -1)
    diff = gcum[..., :, None] - gcum[..., None, :]
    decay = jnp.where(causal, jnp.exp(jnp.where(causal, diff, 0.0)), 0.0)
    k_beta = k * beta[..., None]
    v_beta = v * beta[..., None]
    lmat = jnp.where(strict, jnp.einsum('bhncd,bhnsd->bhncs', k_beta, k) * decay, 0.0)
    eye = jnp.eye(CHUNK, dtype=jnp.float32)
    tmat = lax.linalg.triangular_solve(eye + lmat, jnp.broadcast_to(eye, lmat.shape), left_side=True, lower=True)
    u_c = jnp.einsum('bhncs,bhnsd->bhncd', tmat, v_beta)
    w_c = jnp.einsum('bhncs,bhnsd->bhncd', tmat, k_beta * jnp.exp(gcum)[..., None])
    qk = jnp.where(causal, jnp.einsum('bhncd,bhnsd->bhncs', q, k) * decay, 0.0)
    q_dec = q * jnp.exp(gcum)[..., None]
    k_dec = k * jnp.exp(gcum[..., -1:] - gcum)[..., None]
    g_last = jnp.exp(gcum[..., -1])

    def step(S, xs):
        u_i, w_i, q_i, k_i, qk_i, gl_i = xs
        v_new = u_i - jnp.einsum('bhcd,bhde->bhce', w_i, S)
        o_i = jnp.einsum('bhcd,bhde->bhce', q_i, S) + jnp.einsum('bhcs,bhse->bhce', qk_i, v_new)
        S = S * gl_i[..., None, None] + jnp.einsum('bhcd,bhce->bhde', k_i, v_new)
        return S, o_i

    xs = tuple(jnp.moveaxis(t, 2, 0) for t in (u_c, w_c, q_dec, k_dec, qk, g_last))
    S0 = jnp.zeros((Bsz, H, Dk, Dv), jnp.float32)
    _, o = lax.scan(step, S0, xs)
    o = jnp.transpose(o, (1, 0, 3, 2, 4))
    return o.reshape(Bsz, Lp, H, Dv)

def gated_deltanet_branch(q, k, v, z, b, a, conv_w, A_log, dt_bias, norm_w):
    Bsz, L, _ = q.shape
    qkv = causal_depthwise_conv_silu(jnp.concatenate([q, k, v], axis=-1), conv_w)
    q, k, v = jnp.split(qkv.astype(jnp.float32), 3, axis=-1)
    heads = lambda t: t.reshape(Bsz, L, DN_HEADS, DN_HEAD_DIM)
    q = l2norm(heads(q)) * (DN_HEAD_DIM ** -0.5)
    k = l2norm(heads(k))
    v = heads(v)
    beta = jax.nn.sigmoid(b.astype(jnp.float32))
    g = -jnp.exp(A_log.astype(jnp.float32)) * jax.nn.softplus(a.astype(jnp.float32) + dt_bias.astype(jnp.float32))
    pad = (-N_META) % CHUNK
    front = lambda t: jnp.pad(t, ((0, 0), (pad, 0)) + ((0, 0),) * (t.ndim - 2))
    o = chunk_gated_delta_rule(front(q), front(k), front(v), front(beta), front(g))[:, pad:]
    o = rmsnorm(o, norm_w) * jax.nn.silu(heads(z.astype(jnp.float32)))
    return o.reshape(Bsz, L, DN_WIDTH)

def hybrid_layer(h, norm_w, w_in, conv_w, A_log, dt_bias, pool_mix, pool_scale, dn_norm_w, w_pool_out, w_dn_out, w_o):
    xn = rmsnorm(h, norm_w)
    proj = xn @ w_in
    splits = np.cumsum(IN_SPLIT_SIZES[:-1]).tolist()
    u_pool, z_pool, q, k, v, z_dn, b, a, gate_pool, gate_dn = jnp.split(proj, splits, axis=-1)
    y_pool = (causal_multiscale_pool(u_pool, pool_mix, pool_scale) * jax.nn.silu(z_pool.astype(jnp.float32))).astype(h.dtype)
    y_dn = gated_deltanet_branch(q, k, v, z_dn, b, a, conv_w, A_log, dt_bias, dn_norm_w).astype(h.dtype)
    merged = jax.nn.sigmoid(gate_pool) * (y_pool @ w_pool_out) + jax.nn.sigmoid(gate_dn) * (y_dn @ w_dn_out)
    return h + merged @ w_o

def setup_inputs(seed: int = 0) -> dict:
    key = jax.random.key(seed)
    ks = jax.random.split(key, 14)
    nrm = jax.random.normal
    x = nrm(ks[0], (BATCH, SEQ, D_MODEL), jnp.float32)
    meta_tokens = nrm(ks[1], (N_META, D_MODEL), jnp.float32)
    norm_w = 1.0 + 0.02 * nrm(ks[2], (DEPTH, D_MODEL), jnp.float32)
    w_in = nrm(ks[3], (DEPTH, D_MODEL, IN_COLS), jnp.float32) * D_MODEL ** -0.5
    conv_w = nrm(ks[4], (DEPTH, CONV_WIDTH, 3 * DN_WIDTH), jnp.float32) * CONV_WIDTH ** -0.5
    A_log = jnp.log(jax.random.uniform(ks[5], (DEPTH, DN_HEADS), jnp.float32, minval=1.0, maxval=16.0))
    dt = jnp.exp(jax.random.uniform(ks[6], (DEPTH, DN_HEADS), jnp.float32, minval=float(np.log(1e-3)), maxval=float(np.log(1e-1))))
    dt_bias = dt + jnp.log(-jnp.expm1(-dt))
    pool_mix = nrm(ks[7], (DEPTH, POOL_GROUPS, POOL_GROUP_DIM, POOL_GROUP_DIM), jnp.float32) * POOL_GROUP_DIM ** -0.5
    pool_scale = 1.0 + 0.02 * nrm(ks[8], (DEPTH, POOL_WIDTH), jnp.float32)
    dn_norm_w = 1.0 + 0.02 * nrm(ks[9], (DEPTH, DN_HEAD_DIM), jnp.float32)
    w_pool_out = nrm(ks[10], (DEPTH, POOL_WIDTH, D_MODEL), jnp.float32) * POOL_WIDTH ** -0.5
    w_dn_out = nrm(ks[11], (DEPTH, DN_WIDTH, D_MODEL), jnp.float32) * DN_WIDTH ** -0.5
    w_o = nrm(ks[12], (DEPTH, D_MODEL, D_MODEL), jnp.float32) * D_MODEL ** -0.5
    final_norm_w = 1.0 + 0.02 * nrm(ks[13], (D_MODEL,), jnp.float32)
    return {"x": x, "meta_tokens": meta_tokens, "norm_w": norm_w, "w_in": w_in, "conv_w": conv_w,
            "A_log": A_log, "dt_bias": dt_bias, "pool_mix": pool_mix, "pool_scale": pool_scale,
            "dn_norm_w": dn_norm_w, "w_pool_out": w_pool_out, "w_dn_out": w_dn_out, "w_o": w_o,
            "final_norm_w": final_norm_w}

def reference(x, meta_tokens, norm_w, w_in, conv_w, A_log, dt_bias, pool_mix, pool_scale, dn_norm_w, w_pool_out, w_dn_out, w_o, final_norm_w):
    Bsz = x.shape[0]
    meta = jnp.broadcast_to(meta_tokens.astype(x.dtype)[None], (Bsz, N_META, D_MODEL))
    h = jnp.concatenate([meta, x], axis=1)
    for i in range(DEPTH):
        h = hybrid_layer(h, norm_w[i], w_in[i], conv_w[i], A_log[i], dt_bias[i], pool_mix[i], pool_scale[i],
                         dn_norm_w[i], w_pool_out[i], w_dn_out[i], w_o[i])
    return rmsnorm(h[:, N_META:], final_norm_w)


_drawn_inputs = setup_inputs


def setup_inputs(seed=0):
    import zlib

    import numpy as np

    out = dict(_drawn_inputs(seed))
    spreads = {}
    factors = {'norm_w': 4.377, 'pool_scale': 8.0, 'dn_norm_w': 8.0, 'final_norm_w': 2.777}
    for name, (base, spread) in spreads.items():
        noise = np.random.default_rng([zlib.crc32(name.encode()), seed]).standard_normal(out[name].shape)
        drawn = base * np.exp(spread * noise) if base else spread * noise
        out[name] = jnp.asarray(drawn.astype(out[name].dtype))
    for name, factor in factors.items():
        out[name] = (out[name] * factor).astype(out[name].dtype)
    return out
```

```python
from contextlib import ExitStack

import concourse.bass as bass
from concourse import mybir

F32 = mybir.dt.float32
F32R = mybir.dt.float32r
ALU = mybir.AluOpType
ACT = mybir.ActivationFunctionType
AX_X = mybir.AxisListType.X

P = 128
D = 2048
SEQ = 512
META = 16
T = SEQ + META
HALF = T // 2
KT = D // P
PW = 1024
GROUPS = 4
GD = PW // GROUPS
WINDOWS = (2, 4, 8, 16)
HEADS = 16
PAIRS = HEADS // 2
HD = 128
DNW = HEADS * HD
TAPS = 4
C = 64
PAD = C - META
NCH = (T + PAD) // C
LEVELS = 6
GC = 3
NG = NCH // GC
EPS = 1e-6
NEG = -3.0e4

COL_U, COL_ZP = 0, PW
COL_Q, COL_K, COL_V, COL_Z = 2 * PW, 2 * PW + DNW, 2 * PW + 2 * DNW, 2 * PW + 3 * DNW
COL_BA = 2 * PW + 4 * DNW
COL_GATE = COL_BA + 2 * HEADS
CW = 256
UK = 8
CP_PAIR0 = 2 * GROUPS
CP_GATE0 = CP_PAIR0 + 4 * PAIRS
NGATE = 2 * D // CW
NCP = CP_GATE0 + NGATE

CI, CI2, CMUP = 0, 128, 192
CLEV = 256
CEPS = CLEV + C * LEVELS
NCONST = CEPS + 1
CU, CONES, CHA, CHB = (NCONST + P * i for i in range(4))
NTILE_CONV = 3 * HEADS
ROW_NORM, ROW_PS, ROW_DN = 2 * NTILE_CONV, 2 * NTILE_CONV + KT, 2 * NTILE_CONV + KT + PW // P
NROW_A, NROW_B = ROW_DN + 1, 2 * NTILE_CONV
BETA, GCUM, NBEG, EG, EDEC, GLA, GLB = range(7)
NKIND = 7


def constants():
    import numpy as np

    c = np.zeros((P, CHB + P), np.float32)
    c[:, CI:CI + P] = np.eye(P)
    s = np.arange(P) % C
    half = np.arange(P) // C
    col = np.arange(C)
    c[:, CI2:CI2 + C] = s[:, None] == col[None]
    c[:, CMUP:CMUP + C] = np.where(s[:, None] <= col[None], 0.0, NEG)
    for lv in range(LEVELS):
        a, b = s[:, None] >> lv, col[None] >> lv
        c[:, CLEV + C * lv:CLEV + C * (lv + 1)] = (a % 2 == 0) & (b == a + 1)
    same = half[:, None] == half[None]
    c[:, CU:CU + P] = same & (s[:, None] <= s[None])
    c[:, CONES:CONES + P] = same
    c[:, CHA:CHA + P] = (half == 0)[:, None]
    c[:, CHB:CHB + P] = (half == 1)[:, None]
    c[:, CEPS] = EPS
    return c


def need(engine, semaphore, value):
    if isinstance(value, int) and value < 1:
        return
    engine.wait_ge(semaphore, value)


def build(nc, x, meta_tokens, norm_w, w_in, conv_w, A_log, dt_bias, pool_mix, pool_scale, dn_norm_w,
          w_pool_out, w_dn_out, w_o, final_norm_w, consts, out):
    gates_d = nc.dram_tensor("gates_scratch", (2 * D, SEQ), F32, kind="Internal").ap()
    y_d = nc.dram_tensor("branch_scratch", (PW + DNW, SEQ), F32, kind="Internal").ap()

    outer = ExitStack()
    with outer:
        def tensors(stack):
            def sb(name, shape, dt=F32):
                return stack.enter_context(nc.sbuf_tensor(name, shape, dt))
            return sb

        def sem(name):
            return outer.enter_context(nc.semaphore(name))

        sb = tensors(outer)
        cst = sb("cst", [P, NCONST])
        vcol = sb("vcol", [P, NROW_A - ROW_NORM])
        convc = sb("convc", [P, TAPS, 3, HEADS])
        table = sb("table", [P, PAIRS, NKIND, NCH])
        ident = cst[:, CI:CI + P]
        eps = cst[:, CEPS:CEPS + 1]
        normw = vcol[:, 0:KT]
        pscale = vcol[:, KT:KT + PW // P]
        dnw = vcol[:, KT + PW // P:KT + PW // P + 1]

        WORK = 24 * SEQ + 3 * UK * CW

        class Layout:

            def __init__(self):
                self.stack, self.at = ExitStack(), 0

            def tensor(self, name, shape, dt=F32):
                n = 1
                for k in shape:
                    n *= k
                self.at += n
                return self.stack.enter_context(nc.sbuf_tensor(name, [P] + list(shape), dt))

            def skip_to(self, column):
                assert column >= self.at, (column, self.at)
                if column > self.at:
                    self.tensor(f"skip{self.stack_id}_{self.at}", [column - self.at])

            def close(self):
                self.stack.close()

        def layout(number):
            made = Layout()
            made.stack_id = number
            return made

        lay = layout(0)
        kq = lay.tensor("kq", [2, NCH, 2, C])
        vch = lay.tensor("vch", [NCH, 2, C])
        sz = lay.tensor("sz", [2, SEQ])
        dec = lay.tensor("dec", [NCH, C])
        mq = lay.tensor("mq", [NCH, 2, C])
        ts = lay.tensor("ts", [NCH, 2, C])
        xm = lay.tensor("xm", [NCH, C])
        bm = lay.tensor("bm", [NG, 2, GC, C])
        ktok = lay.tensor("ktok", [NCH, HD])
        oo = lay.tensor("oo", [NCH - 1, HD])
        gates_at = lay.at
        stg = lay.tensor("stg", [3, 2, T])
        vtok = lay.tensor("vtok", [NCH, HD])
        xin = lay.tensor("xin", [TAPS - 1 + T])
        zst = lay.tensor("zst", [2, SEQ])
        convcur = lay.tensor("convcur", [TAPS, 3, 2])
        cur = lay.tensor("cur", [NKIND, NCH])
        state = lay.tensor("state", [2, HD])
        rr = lay.tensor("rr", [HD])
        vn = lay.tensor("vn", [HD])
        junk = lay.tensor("junk", [HD])
        norms = lay.tensor("norms", [NCH, 2])
        rkq = lay.tensor("rkq", [NCH, 2])
        sc = lay.tensor("sc", [4, NCH])
        oss = lay.tensor("oss", [4, NCH - 1])
        lay.skip_to(WORK)
        raw = lay.tensor("raw", [4, UK, CW])
        xh = lay.tensor("xh", [KT, T], F32R)
        xl = lay.tensor("xl", [KT, T], F32R)
        wh = lay.tensor("wh", [4, UK, P], F32R)
        wl = lay.tensor("wl", [4, UK, P], F32R)
        lay.close()
        assert gates_at == 22 * SEQ
        gates_sb = [stg[:, 0, :, :].rearrange("p a t -> p (a t)")[:, i * SEQ:(i + 1) * SEQ] for i in range(2)]

        lay = layout(1)
        prow = lay.tensor("prow", [2, P])
        al = lay.tensor("al", [2, HEADS])
        wba = lay.tensor("wba", [KT, 2 * HEADS])
        sums = lay.tensor("sums", [4, P])
        at_xt = lay.at
        xt = lay.tensor("xt", [5, D])
        fst = lay.tensor("fst", [4, 4, P])
        stat = lay.tensor("stat", [3, 5])
        at_square = lay.at
        xsquare = lay.tensor("xsquare", [D])
        lay.close()
        lay = layout(2)
        lay.skip_to(at_xt)
        ba = lay.tensor("ba", [NCH * C])
        ba2 = lay.tensor("ba2", [NCH, 2, C])
        tb = lay.tensor("tb", [2, PAIRS, NCH])
        tq = lay.tensor("tq", [8, PAIRS, NCH])
        mixcur = lay.tensor("mixcur", [2, GD])
        ub = lay.tensor("ub", [2, T])
        pa = lay.tensor("pa", [2, T])
        pooled = lay.tensor("pooled", [2, SEQ])
        szp = lay.tensor("szp", [2, SEQ])
        yps = lay.tensor("yps", [2, SEQ])
        lay.skip_to(at_square)
        wbh = lay.tensor("wbh", [KT, P], F32R)
        wbl = lay.tensor("wbl", [KT, P], F32R)
        assert lay.at <= WORK
        lay.close()

        lay = layout(3)
        yraw = lay.tensor("yraw", [24, SEQ])
        rawb = lay.tensor("rawb", [3, UK, CW])
        yh = lay.tensor("yh", [24, SEQ], F32R)
        yl = lay.tensor("yl", [24, SEQ], F32R)
        bwh = lay.tensor("bwh", [3, UK, P], F32R)
        bwl = lay.tensor("bwl", [3, UK, P], F32R)
        lay.close()
        lay = layout(4)
        merged = lay.tensor("merged", [KT, SEQ])
        gst = lay.tensor("gst", [2, 2, SEQ])
        rawc3 = lay.tensor("rawc3", [UK, CW])
        lay.close()
        lay = layout(5)
        xres = lay.tensor("xres", [4, D])
        fnw = lay.tensor("fnw", [D])
        lay.skip_to(WORK)
        mh = lay.tensor("mh", [KT, SEQ], F32R)
        ml = lay.tensor("ml", [KT, SEQ], F32R)
        res = lay.tensor("res", [4, D])
        cwh = lay.tensor("cwh", [4, UK, P], F32R)
        cwl = lay.tensor("cwl", [4, UK, P], F32R)
        ot = lay.tensor("ot", [SEQ])
        lay.close()
        rawc = [rawb[:, 0], rawb[:, 1], rawb[:, 2], rawc3[:, :, :]]
        spare = table[:, :, :, :].rearrange("p a k n -> p (a k n)")
        ssp = spare[:, 0:4 * KT].rearrange("p (n k) -> p n k", n=4)
        fin = spare[:, 4 * KT:4 * KT + 12].rearrange("p (a n) -> p a n", a=3)

        pj = [outer.enter_context(nc.psum_tensor(f"pj{i}", [P, 2, 512], F32)) for i in range(2)]
        pg = [outer.enter_context(nc.psum_tensor(f"pg{i}", [P, 512], F32)) for i in range(NG)]
        pt = outer.enter_context(nc.psum_tensor("pt", [P, 512], F32))
        banks = [pj[0][:, 0, :], pj[0][:, 1, :], pj[1][:, 0, :], pj[1][:, 1, :]]

        cst_loaded, par_loaded, ba_loaded = sem("cst_loaded"), sem("par_loaded"), sem("ba_loaded")
        mix_loaded = sem("mix_loaded")
        xt_loaded = [sem(f"xt_loaded{i}") for i in range(5)]
        raw_loaded = [sem(f"raw_loaded{i}") for i in range(4)]
        rawb_loaded = [sem(f"rawb_loaded{i}") for i in range(3)]
        rawc_loaded = [sem(f"rawc_loaded{i}") for i in range(4)]
        par_tr, par_cols = sem("par_tr"), sem("par_cols")
        x_sq, x_rms, x_rstd, x_scaled = sem("x_sq"), sem("x_rms"), sem("x_rstd"), sem("x_scaled")
        x_tr, x_f, x_hi, x_lo = sem("x_tr"), sem("x_f"), sem("x_hi"), sem("x_lo")
        ba_zero, ba_hi, ba_lo, ba_mm, ba_row = sem("ba_zero"), sem("ba_hi"), sem("ba_lo"), sem("ba_mm"), sem("ba_row")
        ba_tr, ba_tok = sem("ba_tr"), sem("ba_tok")
        tab_act, tab_dve, tab_mid, tab_mm = sem("tab_act"), sem("tab_dve"), sem("tab_mid"), sem("tab_mm")
        zeroed = sem("zeroed")
        hi_done, lo_done, pe_piece, proj_evac = sem("hi_done"), sem("lo_done"), sem("pe_piece"), sem("proj_evac")
        pool_add, pool_step, mix_mm, yp_done, yp_stored = sem("pool_add"), sem("pool_step"), sem("mix_mm"), sem("yp_done"), sem("yp_stored")
        conv_cur, conv_step = sem("conv_cur"), sem("conv_step")
        gate_stored = [sem("gate_stored0"), sem("gate_stored1")]
        silu_done, cur_ready = sem("silu_done"), sem("cur_ready")
        gram_mm, gram_read, gram_sum = sem("gram_mm"), sem("gram_read"), sem("gram_sum")
        norm_sqrt, rkq_ready, decay_exp = sem("norm_sqrt"), sem("rkq_ready"), sem("decay_exp")
        scale_ready, decay_scaled, mq_ready = sem("scale_ready"), sem("decay_scaled"), sem("mq_ready")
        ts_init, b_masked = sem("ts_init"), sem("b_masked")
        vk_tr, vk_tok = sem("vk_tr"), sem("vk_tok")
        x_mm, x_evac, ts_mm, ts_upd = sem("x_mm"), sem("x_evac"), sem("ts_mm"), sem("ts_upd")
        ks_mm, qs_mm, r_ready, tr_mm, vn_ready = sem("ks_mm"), sem("qs_mm"), sem("r_ready"), sem("tr_mm"), sem("vn_ready")
        st_mm, st_upd, qkv_mm, o_inter, o_ready = sem("st_mm"), sem("st_upd"), sem("qkv_mm"), sem("o_inter"), sem("o_ready")
        o_ssq, o_var, o_sqrt, o_rstd, o_fac = sem("o_ssq"), sem("o_var"), sem("o_sqrt"), sem("o_rstd"), sem("o_fac")
        o_scaled, o_tr, y_ready, y_stored = sem("o_scaled"), sem("o_tr"), sem("y_ready"), sem("y_stored")
        work_free = sem("work_free")
        pe_gate = sem("pe_gate")
        yraw_tail, yraw_loaded, y_hi, y_lo = sem("yraw_tail"), sem("yraw_loaded"), sem("y_hi"), sem("y_lo")
        hib, lob, peb = sem("hib"), sem("lob"), sem("peb")
        gate_loaded = [sem("gate_loaded0"), sem("gate_loaded1")]
        mg_step, mg_done = sem("mg_step"), sem("mg_done")
        m_hi, m_lo = sem("m_hi"), sem("m_lo")
        hic, loc, pec, c_evac, c_tr, res_done = sem("hic"), sem("loc"), sem("pec"), sem("c_evac"), sem("c_tr"), sem("res_done")
        xres_loaded, fnw_loaded, c_ssq = sem("xres_loaded"), sem("fnw_loaded"), sem("c_ssq")
        fin_sum, fin_sqrt, fin_rstd, fin_done, out_stored = (
            sem("fin_sum"), sem("fin_sqrt"), sem("fin_rstd"), sem("fin_done"), sem("out_stored"))

        TILE_ROWS = [META] + [P] * 4
        TILE_COL = [0] + [META + P * i for i in range(4)]

        def chunk(t, n):
            return t[:, n * C:(n + 1) * C]

        def bc(ap, n):
            return ap.unsqueeze(2).broadcast_to([ap.shape[0], ap.shape[1], n])

        def group(g):
            return slice(GC * g, GC * (g + 1))

        block = outer.enter_context(nc.Block())

        @block.sync
        def _(sp):
            sp.dma_start(cst[:, :], consts[:, 0:NCONST]).then_inc(cst_loaded, 16)
            for i in range(5):
                src = meta_tokens if i == 0 else x[0, (i - 1) * P:i * P, :]
                sp.dma_start(xt[0:TILE_ROWS[i], i, :], src).then_inc(xt_loaded[i], 16)
                if i == 1:
                    cv = conv_w[0].rearrange("t (n c) -> t n c", c=P)
                    n = NTILE_CONV
                    sp.dma_start(prow[0:n, 0, :], cv[0]).then_inc(par_loaded, 16)
                    sp.dma_start(prow[n:2 * n, 0, :], cv[1]).then_inc(par_loaded, 16)
                    sp.dma_start(prow[0:n, 1, :], cv[2]).then_inc(par_loaded, 16)
                    sp.dma_start(prow[n:2 * n, 1, :], cv[3]).then_inc(par_loaded, 16)
                    sp.dma_start(prow[ROW_NORM:ROW_PS, 0, :], norm_w[0].rearrange("(k p) -> k p", p=P)).then_inc(par_loaded, 16)
                    sp.dma_start(prow[ROW_PS:ROW_DN, 0, :], pool_scale[0].rearrange("(k p) -> k p", p=P)).then_inc(par_loaded, 16)
                    sp.dma_start(prow[ROW_DN:ROW_DN + 1, 0, :], dn_norm_w).then_inc(par_loaded, 16)
            sp.dma_start(wba[:, :, :], w_in[0, :, COL_BA:COL_GATE].rearrange("(k p) c -> p k c", p=P)).then_inc(ba_loaded, 16)
            sp.dma_start(sums[:, :, :], consts[:, CU:CU + 4 * P].rearrange("p (i c) -> p i c", i=4)).then_inc(ba_loaded, 16)
            sp.dma_start(al[:, 0, :], A_log.broadcast_to([P, HEADS])).then_inc(ba_loaded, 16)
            sp.dma_start(al[:, 1, :], dt_bias.broadcast_to([P, HEADS])).then_inc(ba_loaded, 16)

            def load_cp(cp, par, col):
                for h in range(2):
                    need(sp, lo_done, 16 * cp + 4 * h - 20)
                    sp.dma_start(raw[:, 2 * par + h, :, :],
                                 w_in[0, h * UK * P:(h + 1) * UK * P, bass.ds(col, CW)].rearrange("(k p) c -> p k c", p=P)
                                 ).then_inc(raw_loaded[2 * par + h], 16)

            load_cp(0, 0, COL_U)
            load_cp(1, 1, COL_ZP)
            with sp.Fori(1, GROUPS) as g:
                load_cp(2 * g, 0, COL_U + g * CW)
                load_cp(2 * g + 1, 1, COL_ZP + g * CW)
            with sp.Fori(0, PAIRS) as p:
                for k, col in enumerate((COL_K, COL_Q, COL_V, COL_Z)):
                    load_cp(CP_PAIR0 + 4 * p + k, k % 2, col + p * CW)
            with sp.Fori(0, NGATE // 2) as i:
                load_cp(CP_GATE0 + 2 * i, 0, COL_GATE + i * (2 * CW))
                load_cp(CP_GATE0 + 2 * i + 1, 1, COL_GATE + CW + i * (2 * CW))

            sp.wait_ge(y_stored, 16 * PAIRS)
            sp.wait_ge(yp_stored, 16 * GROUPS)
            y_rows = y_d.rearrange("(k p) t -> p k t", p=P)
            sp.dma_start(yraw[:, 0:22, :], y_rows[:, 0:22, :]).then_inc(yraw_loaded, 16)

            def load_b(jp, first):
                for u in range(3):
                    if not first:
                        need(sp, lob, 24 * jp + 4 * u - 8)
                    w = w_pool_out if u == 0 else w_dn_out
                    r = 0 if u < 2 else UK * P
                    sp.dma_start(rawb[:, u, :, :],
                                 w[0, r:r + UK * P, bass.ds(jp * CW, CW)].rearrange("(k p) c -> p k c", p=P)
                                 ).then_inc(rawb_loaded[u], 16)

            load_b(0, True)
            for c in range(2):
                sp.wait_ge(gate_stored[c], 16 * NGATE)
            sp.dma_start(yraw[:, 22:24, :], y_rows[:, 22:24, :]).then_inc(yraw_tail, 16)
            with sp.Fori(1, D // CW) as jp:
                load_b(jp, False)

            def load_c(cp, par, first):
                for h in range(2):
                    slot = 2 * par + h
                    if first:
                        if slot < 3:
                            sp.wait_ge(lob, 24 * (D // CW) + 4 * slot - 8)
                        else:
                            sp.wait_ge(y_lo, 24)
                    else:
                        need(sp, loc, 16 * cp + 4 * h - 20)
                    sp.dma_start(rawc[slot],
                                 w_o[0, h * UK * P:(h + 1) * UK * P, bass.ds(cp * CW, CW)].rearrange("(k p) c -> p k c", p=P)
                                 ).then_inc(rawc_loaded[slot], 16)

            load_c(0, 0, True)
            load_c(1, 1, True)
            sp.wait_ge(m_hi, KT)
            sp.wait_ge(m_lo, KT)
            sp.dma_start(xres[:, :, :], x[0].rearrange("(n p) d -> p n d", p=P)).then_inc(xres_loaded, 16)
            sp.dma_start(fnw[:, :], final_norm_w.unsqueeze(0).broadcast_to([P, D])).then_inc(fnw_loaded, 16)
            with sp.Fori(1, D // CW // 2) as i:
                load_c(2 * i, 0, False)
                load_c(2 * i + 1, 1, False)
            for n in range(4):
                for hf in range(2):
                    sp.wait_ge(fin_done, 2 * n + hf + 1)
                    sp.dma_start(out[0, n * P:(n + 1) * P, hf * 1024:(hf + 1) * 1024],
                                 res[:, n, hf * 1024:(hf + 1) * 1024]).then_inc(out_stored, 16)
            sp.wait_ge(out_stored, 16 * 8)

        @block.tensor
        def _(pe):
            def product(dst, lhs, rhs, start, stop):
                return pe.matmul(dst, lhs, rhs, start=start, stop=stop)

            def window(cp, c, h, full, hook):
                pe.wait_ge(lo_done, 16 * cp + 8 * c + 4 * h + 4)
                if h == 0:
                    need(pe, proj_evac, 2 * cp + c - 1)
                halves = [(pj[c][:, i, 0:HALF], i * HALF, HALF) for i in range(2)] if full else \
                    [(pj[c][:, 0, 0:SEQ], META, SEQ)]
                slot = 2 * c + h
                for k in range(UK):
                    kt = h * UK + k
                    for w, xx, first, last in ((wh, xh, True, False), (wh, xl, False, False), (wl, xh, False, True)):
                        for dst, c0, n in halves:
                            mm = product(dst, w[:, slot, k, :], xx[:, kt, c0:c0 + n],
                                         first and kt == 0, last and kt == KT - 1)
                    if k == UK - 1:
                        mm.then_inc(pe_piece, 1)
                    if k % 2 == 1:
                        hook(k // 2)

            pe.wait_ge(cst_loaded, 16)
            pe.wait_ge(par_loaded, 16 * 7)
            pe.transpose(pt[:, 0:NROW_A], prow[0:NROW_A, 0, :], cst[0:NROW_A, CI:CI + NROW_A])
            pe.transpose(pt[:, 128:128 + NROW_B], prow[0:NROW_B, 1, :], cst[0:NROW_B, CI:CI + NROW_B]).then_inc(par_tr, 1)
            for i in range(5):
                r = TILE_ROWS[i]
                pe.wait_ge(x_scaled, i + 1)
                for b in range(4):
                    n = 4 * i + b
                    if n >= 4:
                        pe.wait_ge(x_f, n - 3)
                    for k in range(4):
                        kt = 4 * b + k
                        mm = pe.transpose(banks[n % 4][:, k * P:k * P + r], xt[0:r, i, kt * P:(kt + 1) * P],
                                          cst[0:r, CI:CI + r])
                    mm.then_inc(x_tr, 1)
            pe.wait_ge(x_lo, 20)
            pe.wait_ge(ba_lo, 2)
            for kt in range(KT):
                for w, xx, first, last in ((wbh, xh, True, False), (wbh, xl, False, False), (wbl, xh, False, True)):
                    for i in range(2):
                        mm = product(pg[i][:, 0:HALF], w[:, kt, :], xx[:, kt, i * HALF:(i + 1) * HALF],
                                     first and kt == 0, last and kt == KT - 1)
            mm.then_inc(ba_mm, 1)

            def no_hook(q):
                return None

            def table_steps(cp, j, q):
                if (cp, j, q) == (0, 1, 0):
                    pe.wait_ge(ba_row, 4)
                    for n in range(NCH):
                        lhs = ba2[0:48, n, :, :].rearrange("p a c -> p (a c)")
                        mm = pe.transpose(pg[2][:, 48 * n:48 * (n + 1)], lhs, cst[0:48, CI:CI + 48])
                    mm.then_inc(ba_tr, 1)
                if (cp, j, q) == (0, 3, 0):
                    pe.wait_ge(tab_dve, 3)
                    g = tq[:, 5, :, :].rearrange("p a n -> p (a n)")
                    w = PAIRS * NCH
                    pe.wait_ge(ba_loaded, 64)
                    for i in range(4):
                        mm = product(pg[2][:, i * w:(i + 1) * w], sums[:, i, :], g, True, True)
                    mm.then_inc(tab_mm, 1)

            def pool_windows(g, first):
                for z in range(2):
                    for j in range(4):
                        def hook(q, z=z, j=j):
                            if first:
                                table_steps(z, j, q)
                            if (z, j, q) == (1, 2, 3):
                                pe.wait_ge(mix_loaded, 16 * g + 16)
                                pe.wait_ge(pool_step, 2 * g + 2)
                                need(pe, yp_done, 2 * g)
                                for d in range(2):
                                    for cc in range(2):
                                        mm = product(pg[d][:, 0:SEQ], mixcur[:, cc, d * P:(d + 1) * P],
                                                     pooled[:, cc, :], cc == 0, cc == 1)
                                mm.then_inc(mix_mm, 1)
                        window(2 * g + z, j // 2, j % 2, z == 0, hook)

            pool_windows(0, True)
            with pe.Fori(1, GROUPS) as g:
                pool_windows(g, False)

            def delta(d, m):
                def wait(semaphore, per_pair, count):
                    need(pe, semaphore, d * per_pair + count)

                def alone():
                    pe.sem_inc(pe_gate, 1)

                if 2 <= m <= 4:
                    g = m - 2
                    if g == 0:
                        wait(silu_done, 4, 2)
                        wait(cur_ready, 1, 1)
                        pe.wait_ge(yp_done, 2 * GROUPS)
                        pe.wait_ge(tab_dve, 6)
                    else:
                        wait(gram_read, NG, g)
                    alone()
                    for i in range(GC):
                        n = GC * g + i
                        for hd in range(2):
                            ph = slice(64 * hd, 64 * hd + 64)
                            kk, qq = kq[:, 0, n, hd, :], kq[:, 1, n, hd, :]
                            product(pg[g][ph, 128 * i:128 * (i + 1)].rearrange("p (a c) -> p a c", a=2), kk,
                                    kq[:, :, n, hd, :], True, True)
                            product(pt[ph, C * i:C * (i + 1)], qq, qq, True, True)
                            mm = product(pt[ph, 256 + C * i:256 + C * (i + 1)],
                                         cur[ph, GCUM, n:n + 1].broadcast_to([64, 64]), cst[ph, CI2:CI2 + C], True, True)
                    mm.then_inc(gram_mm, 1)
                if 7 <= m <= 11:
                    rd = m - 7
                    if rd == 0:
                        wait(silu_done, 4, 3)
                        wait(gram_read, NG, NG)
                    else:
                        wait(vk_tok, 2 * NCH, 4 * rd)
                    for i in range(4 * rd, min(4 * rd + 4, 2 * NCH)):
                        src = (vch[:, i] if i < NCH else kq[:, 0, i - NCH]).rearrange("p h c -> p (h c)")
                        mm = pe.transpose(pt[:, (i % 4) * P:(i % 4 + 1) * P], src, ident)
                    mm.then_inc(vk_tr, 1)
                if 9 <= m < 9 + 2 * LEVELS:
                    lv, second = (m - 9) // 2, (m - 9) % 2
                    for g in range(NG):
                        if not second:
                            wait(b_masked, NG * LEVELS, NG * lv + g + 1)
                            if lv == 0:
                                wait(mq_ready, NG, g + 1)
                                wait(ts_init, 1, 1)
                            else:
                                wait(ts_upd, NG * LEVELS, NG * (lv - 1) + g + 1)
                            alone()
                            for i in range(GC):
                                for hd in range(2):
                                    ph = slice(64 * hd, 64 * hd + 64)
                                    mm = product(pg[g][ph, C * i:C * (i + 1)], bm[ph, g, lv % 2, i, :],
                                                 ts[ph, GC * g + i, 0, :], True, True)
                            mm.then_inc(x_mm, 1)
                        else:
                            wait(x_evac, NG * LEVELS, NG * lv + g + 1)
                            alone()
                            for i in range(GC):
                                n = GC * g + i
                                for hd in range(2):
                                    ph = slice(64 * hd, 64 * hd + 64)
                                    product(pg[g][ph, 128 * i:128 * i + C], ts[ph, n, 1, :], xm[ph, n, :], True, True)
                                    mm = product(pg[g][ph, 128 * i + C:128 * (i + 1)], xm[ph, n, :], ts[ph, n, 1, :], True, True)
                            mm.then_inc(ts_mm, 1)
                R0 = 9 + 2 * LEVELS
                if R0 <= m < R0 + 3 * NCH:
                    n, stage = (m - R0) // 3, (m - R0) % 3
                    if stage == 0 and n > 0:
                        wait(st_upd, 2 * (NCH - 1), 2 * n)
                        if n == 1:
                            wait(vn_ready, NCH, 1)
                        for hd in range(2):
                            mm = product(pg[0][64 * hd:64 * hd + 64, 0:HD], kq[:, 0, n, hd, :], state[:, hd, :], True, True)
                        mm.then_inc(ks_mm, 1)
                        if n > 1:
                            wait(o_ready, NCH - 1, n - 1)
                        else:
                            wait(vk_tok, 2 * NCH, 2 * NCH)
                        for hd in range(2):
                            mm = product(pt[64 * hd:64 * hd + 64, 0:HD], kq[:, 1, n, hd, :], state[:, hd, :], True, True)
                        mm.then_inc(qs_mm, 1)
                    if stage == 1:
                        if n == 0:
                            wait(ts_upd, NG * LEVELS, NG * LEVELS)
                            wait(vk_tok, 2 * NCH, NCH)
                            rhs = vtok[:, 0, :]
                        else:
                            wait(r_ready, NCH - 1, n)
                            rhs = rr[:, :]
                        alone()
                        for hd in range(2):
                            ph = slice(64 * hd, 64 * hd + 64)
                            mm = product(pg[0][ph, 128:128 + HD], ts[ph, n, 1, :], rhs[ph, :], True, True)
                        mm.then_inc(tr_mm, 1)
                    if stage == 2:
                        wait(vn_ready, NCH, n + 1)
                        if n == 0:
                            wait(vk_tok, 2 * NCH, NCH + 1)
                        if n < NCH - 1:
                            for hd in range(2):
                                ph = slice(64 * hd, 64 * hd + 64)
                                mm = product(pg[1 + hd][:, 0:HD], ktok[ph, n, :], vn[ph, :], True, True)
                            mm.then_inc(st_mm, 1)
                        if n > 0:
                            wait(o_inter, NCH - 1, n)
                            alone()
                            for hd in range(2):
                                ph = slice(64 * hd, 64 * hd + 64)
                                mm = product(pt[ph, 128:128 + HD], mq[ph, n, 1, :], vn[ph, :], True, True)
                            mm.then_inc(qkv_mm, 1)
                for b in range(2):
                    if m == 52 + 2 * b:
                        wait(o_scaled, 2, b + 1)
                        if b == 0:
                            wait(o_ready, NCH - 1, NCH - 1)
                        for i in range(4):
                            mm = pe.transpose((pt if b == 0 else pg[0])[:, i * P:(i + 1) * P], oo[:, 4 * b + i, :], ident)
                        mm.then_inc(o_tr, 1)

            def pair_windows(p, d):
                for k in range(4):
                    for j in range(4):
                        def hook(q, k=k, j=j):
                            if d is not None:
                                delta(d, 16 * k + 4 * j + q)
                        window(CP_PAIR0 + 4 * p + k, j // 2, j % 2, k < 3, hook)

            pair_windows(0, None)
            with pe.Fori(1, PAIRS) as p:
                pair_windows(p, p - 1)
            for k in range(4):
                for j in range(4):
                    window(CP_GATE0 + k, j // 2, j % 2, False, lambda q, k=k, j=j: delta(PAIRS - 1, 16 * k + 4 * j + q))
            with pe.Fori(2, NGATE // 2) as i:
                for k in range(2):
                    for j in range(4):
                        window(CP_GATE0 + 2 * i + k, j // 2, j % 2, False, no_hook)

            def window_b(jp, c, u, first):
                pe.wait_ge(lob, 24 * jp + 12 * c + 4 * u + 4)
                if u == 0:
                    if first:
                        pe.wait_ge(proj_evac, 2 * NCP - 1 + c)
                    else:
                        pe.wait_ge(mg_done, 2 * jp + c - 1)
                dst = pj[c][:, 0 if u == 0 else 1, :]
                for k in range(UK):
                    kt = u * UK + k
                    if first and c == 0:
                        pe.wait_ge(y_lo, kt + 1)
                    for w, yy, one, last in ((bwh, yh, True, False), (bwh, yl, False, False), (bwl, yh, False, True)):
                        mm = product(dst, w[:, u, k, :], yy[:, kt, :], one and k == 0 and u < 2,
                                     last and k == UK - 1 and u != 1)
                mm.then_inc(peb, 1)

            for c in range(2):
                for u in range(3):
                    window_b(0, c, u, True)
            with pe.Fori(1, D // CW) as jp:
                for c in range(2):
                    for u in range(3):
                        window_b(jp, c, u, False)

            def back(count):
                pe.wait_ge(c_evac, count)
                need(pe, c_ssq, 4 * (count - 1))
                for n in range(4):
                    mm = pe.transpose(pg[0][:, n * P:(n + 1) * P], ot[:, n * P:(n + 1) * P], ident)
                mm.then_inc(c_tr, 1)

            def window_c(cp, c, h, first):
                pe.wait_ge(loc, 16 * cp + 8 * c + 4 * h + 4)
                if h == 0:
                    if first and c == 0 and isinstance(cp, int) and cp == 0:
                        pe.wait_ge(mg_done, KT)
                    else:
                        need(pe, c_evac, 2 * cp + c - 1)
                for k in range(UK):
                    kt = h * UK + k
                    if first and c == 0:
                        pe.wait_ge(m_lo, kt + 1)
                    for w, yy, one, last in ((cwh, mh, True, False), (cwh, ml, False, False), (cwl, mh, False, True)):
                        mm = product(pj[c][:, 0, :], w[:, 2 * c + h, k, :], yy[:, kt, :], one and kt == 0, last and kt == KT - 1)
                mm.then_inc(pec, 1)

            def pair_c(cp, first):
                for j in range(4):
                    window_c(cp, j // 2, j % 2, first)
                    if j == 0 and not first:
                        back(2 * cp)
                    if j == 2:
                        back(2 * cp + 1)

            pair_c(0, True)
            pair_c(1, False)
            with pe.Fori(1, D // CW // 2) as i:
                pair_c(2 * i, False)
                pair_c(2 * i + 1, False)
            back(2 * (D // CW))

        def target(cp, par, j):
            return (cp, par, j + 2) if j < 2 else (cp + 1, 1 - par, j - 2)

        @block.scalar
        def _(act):
            def copy(dst, src):
                return act.activation(dst, src, ACT.Copy)

            def split_hi(cp, par, j, q):
                c, h = j // 2, j % 2
                if q == 0:
                    if c == 0:
                        act.wait_ge(raw_loaded[2 * par + h], 8 * cp + 16 - 8 * par)
                    need(act, pe_piece, 4 * cp + j - 3)
                copy(wh[:, j, 2 * q:2 * q + 2, :],
                     raw[:, 2 * par + h, 2 * q:2 * q + 2, c * P:(c + 1) * P]).then_inc(hi_done, 1)

            def window(cp, par, j, hook, evac, last=False):
                for q in range(4):
                    if not (last and j >= 2):
                        split_hi(*target(cp, par, j), q)
                    hook(q)
                if j % 2 == 1:
                    act.wait_ge(pe_piece, 4 * cp + j + 1)
                    evac(j // 2)

            def x_hi_part(i):
                r, c0 = TILE_ROWS[i], TILE_COL[i]
                for b in range(4):
                    n = 4 * i + b
                    act.wait_ge(x_f, n + 1)
                    copy(xh[:, 4 * b:4 * b + 4, c0:c0 + r], fst[:, n % 4, :, 0:r]).then_inc(x_hi, 1)

            act.wait_ge(cst_loaded, 16)
            for i in range(5):
                r = TILE_ROWS[i]
                act.wait_ge(xt_loaded[i], 16)
                act.activation(xsquare[0:r, :], xt[0:r, i, :], ACT.Square, accum_out=stat[0:r, 0, i:i + 1]).then_inc(x_sq, 1)
                act.wait_ge(x_sq, i + 1)
                act.activation(stat[0:r, 1, i:i + 1], stat[0:r, 0, i:i + 1], ACT.Sqrt, bias=eps[0:r, :], scale=1.0 / D).then_inc(x_rms, 1)
                if i >= 1:
                    x_hi_part(i - 1)
            x_hi_part(4)

            for j in range(2):
                for q in range(4):
                    split_hi(0, 0, j, q)

            def nothing(q):
                return None

            def table_acts(z, j, q):
                if (z, j, q) == (0, 1, 3):
                    act.wait_ge(tab_dve, 2)
                    act.activation(tq[:, 1], tq[:, 0], ACT.Abs).then_inc(tab_act, 1)
                    act.wait_ge(tab_act, 1)
                    act.activation(tq[:, 2], tq[:, 1], ACT.Exp, scale=-1.0).then_inc(tab_act, 1)
                    act.wait_ge(tab_act, 2)
                    act.activation(tq[:, 3], tq[:, 2], ACT.Ln, bias=1.0).then_inc(tab_act, 1)
                    act.activation(al[:, 0, :], al[:, 0, :], ACT.Exp).then_inc(tab_act, 1)
                    act.activation(table[:, :, BETA, :], tb[:, 0], ACT.Sigmoid).then_inc(tab_act, 1)
                if (z, j, q) == (1, 0, 0):
                    act.wait_ge(tab_dve, 5)
                    act.activation(table[:, :, EG, :], table[:, :, GCUM, :], ACT.Exp).then_inc(tab_act, 1)
                    act.activation(table[:, :, EDEC, :], tq[:, 4], ACT.Exp).then_inc(tab_act, 1)
                    act.activation(table[:, :, GLA, :], tq[:, 6], ACT.Exp).then_inc(tab_act, 1)
                    act.activation(table[:, :, GLB, :], tq[:, 7], ACT.Exp).then_inc(tab_act, 1)

            def pool_windows(g, first):
                for z in range(2):
                    def evac(c, z=z):
                        if z == 0:
                            need(act, pool_step, 2 * g)
                            copy(ub[:, c, :].rearrange("p (a t) -> p a t", a=2), pj[c][:, :, 0:HALF]).then_inc(proj_evac, 1)
                        else:
                            need(act, yp_done, 2 * g)
                            act.activation(szp[:, c, :], pj[c][:, 0, :], ACT.Silu).then_inc(proj_evac, 1)
                    for j in range(4):
                        hook = (lambda q, z=z, j=j: table_acts(z, j, q)) if first else nothing
                        window(2 * g + z, z, j, hook, evac)

            pool_windows(0, True)
            with act.Fori(1, GROUPS) as g:
                pool_windows(g, False)

            def silu_chunks(dst, src):
                act.activation(dst[:, 0, :, PAD:], src[:, :, 0:META], ACT.Silu)
                act.activation(dst[:, 1:NCH].rearrange("p n h c -> p h n c"),
                               src[:, :, META:T].rearrange("p h (n c) -> p h n c", c=C), ACT.Silu).then_inc(silu_done, 1)

            def delta(d, m):
                def wait(semaphore, per_pair, count):
                    need(act, semaphore, d * per_pair + count)

                if m == 0:
                    wait(conv_step, 4 * 6, 4 * 6)
                    wait(work_free, 1, 1)
                    for kk in range(2):
                        silu_chunks(kq[:, kk], stg[:, kk])
                if m == 1:
                    silu_chunks(vch, stg[:, 2])
                    act.wait_ge(proj_evac, 2 * CP_PAIR0 + 8 * d + 8)
                    act.activation(sz[:, :, :], zst[:, :, :], ACT.Silu).then_inc(silu_done, 1)
                if m == 5:
                    wait(gram_sum, 1, 1)
                    act.activation(rkq[:, :, :], norms[:, :, :], ACT.Sqrt, bias=eps).then_inc(norm_sqrt, 1)
                if m == 6:
                    act.activation(dec[:, :, :], dec[:, :, :], ACT.Exp).then_inc(decay_exp, 1)
                if 7 <= m <= 11:
                    rd = m - 7
                    if rd == 0:
                        wait(scale_ready, 1, 1)
                    wait(vk_tr, 5, rd + 1)
                    for i in range(4 * rd, min(4 * rd + 4, 2 * NCH)):
                        src = pt[:, (i % 4) * P:(i % 4 + 1) * P]
                        if i < NCH:
                            act.activation(vtok[:, i, :], src, ACT.Copy, scale=cur[:, BETA, i:i + 1]).then_inc(vk_tok, 1)
                        else:
                            act.activation(ktok[:, i - NCH, :], src, ACT.Copy, scale=sc[:, 2, i - NCH:i - NCH + 1]).then_inc(vk_tok, 1)
                R0 = 9 + 2 * LEVELS
                if R0 <= m < R0 + 3 * NCH:
                    n, stage = (m - R0) // 3, (m - R0) % 3
                    if stage == 0 and n > 0:
                        wait(qs_mm, NCH - 1, n)
                        act.activation(oo[:, n - 1, :], pt[:, 0:HD], ACT.Copy, scale=cur[:, EG, n:n + 1]).then_inc(o_inter, 1)
                    if stage == 1:
                        wait(tr_mm, NCH, n + 1)
                        copy(vn[:, :], pg[0][:, 128:128 + HD]).then_inc(vn_ready, 1)
                    if stage == 1 and n > 1:
                        wait(o_ready, NCH - 1, n - 1)
                        act.activation(junk[:, :], oo[:, n - 2, :], ACT.Square, accum_out=oss[:, 0, n - 2:n - 1]).then_inc(o_ssq, 1)
                if m == 48:
                    wait(o_ready, NCH - 1, NCH - 1)
                    act.activation(junk[:, :], oo[:, NCH - 2, :], ACT.Square, accum_out=oss[:, 0, NCH - 2:NCH - 1]).then_inc(o_ssq, 1)
                if m == 49:
                    wait(o_var, 2, 2)
                    act.activation(oss[:, 2, :], oss[:, 1, :], ACT.Sqrt, bias=eps, scale=1.0 / HD).then_inc(o_sqrt, 1)

            def pair_windows(p, d):
                for k in range(4):
                    def evac(c, k=k):
                        if k < 3:
                            need(act, conv_step, (p * 6 + 2 * k + c) * 4)
                            if k == 0 and c == 0 and isinstance(p, int) and p == 0:
                                act.wait_ge(zeroed, 3)
                            copy(xin[:, TAPS - 1:].rearrange("p (a t) -> p a t", a=2), pj[c][:, :, 0:HALF]).then_inc(proj_evac, 1)
                        else:
                            copy(zst[:, c, :], pj[c][:, 0, :]).then_inc(proj_evac, 1)
                    for j in range(4):
                        hook = nothing if d is None else (lambda q, k=k, j=j: delta(d, 16 * k + 4 * j + q))
                        window(CP_PAIR0 + 4 * p + k, k % 2, j, hook, evac)

            pair_windows(0, None)
            with act.Fori(1, PAIRS) as p:
                pair_windows(p, p - 1)

            def gate_evac(i):
                def evac(c):
                    need(act, gate_stored[c], 16 * i)
                    act.activation(gates_sb[c], pj[c][:, 0, :], ACT.Sigmoid).then_inc(proj_evac, 1)
                    act.wait_ge(proj_evac, 2 * CP_GATE0 + 2 * i + c + 1)
                    act.dma_start(gates_d[bass.ds((2 * i + c) * P, P), :], gates_sb[c]).then_inc(gate_stored[c], 16)
                return evac

            for k in range(4):
                for j in range(4):
                    window(CP_GATE0 + k, k % 2, j, lambda q, k=k, j=j: delta(PAIRS - 1, 16 * k + 4 * j + q), gate_evac(k))
            with act.Fori(2, NGATE // 2 - 1) as i:
                for k in range(2):
                    for j in range(4):
                        window(CP_GATE0 + 2 * i + k, k, j, nothing, gate_evac(2 * i + k))
            for k in range(2):
                for j in range(4):
                    window(NCP - 2 + k, k, j, nothing, gate_evac(NGATE - 2 + k), last=(k == 1))

            def split_b(jp, j, q):
                c, u = j // 3, j % 3
                if q == 0:
                    if c == 0:
                        act.wait_ge(rawb_loaded[u], 16 * jp + 16)
                    need(act, peb, 6 * jp + j - 2)
                copy(bwh[:, u, 2 * q:2 * q + 2, :], rawb[:, u, 2 * q:2 * q + 2, c * P:(c + 1) * P]).then_inc(hib, 1)

            def y_hi_part(k):
                copy(yh[:, k, :], yraw[:, k, :]).then_inc(y_hi, 1)

            act.wait_ge(pe_piece, 4 * NCP)
            act.wait_ge(yraw_loaded, 16)
            for j in range(2):
                for q in range(4):
                    split_b(0, j, q)
                    y_hi_part(8 * j + 2 * q)
                    y_hi_part(8 * j + 2 * q + 1)

            def window_b(jp, j, first, last):
                for q in range(4):
                    if j < 4:
                        split_b(jp, j + 2, q)
                    elif not last:
                        split_b(jp + 1, j - 4, q)
                    if first and j == 0:
                        if q == 3:
                            act.wait_ge(yraw_tail, 16)
                        y_hi_part(16 + 2 * q)
                        y_hi_part(16 + 2 * q + 1)

            for j in range(6):
                window_b(0, j, True, False)
            with act.Fori(1, D // CW - 1) as jp:
                for j in range(6):
                    window_b(jp, j, False, False)
            for j in range(6):
                window_b(D // CW - 1, j, False, True)

            def split_c(cp, par, j, q):
                c, h = j // 2, j % 2
                if q == 0:
                    if c == 0:
                        act.wait_ge(rawc_loaded[2 * par + h], 8 * cp + 16 - 8 * par)
                    need(act, pec, 4 * cp + j - 3)
                copy(cwh[:, j, 2 * q:2 * q + 2, :], rawc[2 * par + h][:, 2 * q:2 * q + 2, c * P:(c + 1) * P]).then_inc(hic, 1)

            act.wait_ge(peb, 6 * (D // CW))
            act.wait_ge(mg_done, KT)
            for j in range(2):
                for q in range(4):
                    split_c(0, 0, j, q)
                    for k in (8 * j + 2 * q, 8 * j + 2 * q + 1):
                        copy(mh[:, k, :], merged[:, k, :]).then_inc(m_hi, 1)

            def squares(count):
                act.wait_ge(res_done, count)
                need(act, c_ssq, 4 * (count - 1))
                for n in range(4):
                    col = (count - 1) * P
                    act.activation(pt[:, n * P:(n + 1) * P], res[:, n, bass.ds(col, P)], ACT.Square,
                                   accum_out=ssp[:, n, bass.ds(count - 1, 1)]).then_inc(c_ssq, 1)

            def pair_c(cp, par, first, last=False):
                for j in range(4):
                    for q in range(4):
                        if not (last and j >= 2):
                            split_c(*target(cp, par, j), q)
                        if q == 3 and j == 0 and not first:
                            squares(2 * cp)
                        if q == 3 and j == 2:
                            squares(2 * cp + 1)
                    if j % 2 == 1:
                        act.wait_ge(pec, 4 * cp + j + 1)
                        need(act, c_tr, 2 * cp + j // 2)
                        copy(ot[:, :], pj[j // 2][:, 0, :]).then_inc(c_evac, 1)

            pair_c(0, 0, True)
            pair_c(1, 1, False)
            with act.Fori(1, D // CW // 2 - 1) as i:
                pair_c(2 * i, 0, False)
                pair_c(2 * i + 1, 1, False)
            pair_c(D // CW - 2, 0, False)
            pair_c(D // CW - 1, 1, False, last=True)
            squares(KT)
            act.wait_ge(fin_sum, 1)
            act.activation(fin[:, 1, :], fin[:, 0, :], ACT.Sqrt, bias=eps, scale=1.0 / D).then_inc(fin_sqrt, 1)
            for n in range(2, 4):
                act.wait_ge(fin_rstd, 1)
                act.activation(res[:, n, :], res[:, n, :], ACT.Copy, scale=fin[:, 2, n:n + 1]).then_inc(fin_sqrt, 1)

        @block.vector
        def _(dve):
            tt = dve.tensor_tensor

            def split_lo(cp, par, j, q):
                c, h = j // 2, j % 2
                dve.wait_ge(hi_done, 16 * cp + 4 * j + q + 1)
                tt(wl[:, j, 2 * q:2 * q + 2, :], raw[:, 2 * par + h, 2 * q:2 * q + 2, c * P:(c + 1) * P],
                   wh[:, j, 2 * q:2 * q + 2, :].bitcast(F32), ALU.subtract).then_inc(lo_done, 1)

            def window(cp, par, j, hook, last=False):
                for q in range(4):
                    if not (last and j >= 2):
                        split_lo(*target(cp, par, j), q)
                    hook(q)

            dve.wait_ge(par_tr, 1)
            dve.tensor_copy(convc[:, 0:2, :, :].rearrange("p a b c -> p (a b c)"), pt[:, 0:2 * NTILE_CONV]).then_inc(par_cols, 1)
            dve.tensor_copy(vcol[:, :], pt[:, ROW_NORM:NROW_A]).then_inc(par_cols, 1)
            dve.tensor_copy(convc[:, 2:4, :, :].rearrange("p a b c -> p (a b c)"), pt[:, 128:128 + NROW_B]).then_inc(par_cols, 1)
            dve.wait_ge(par_cols, 3)

            def x_f_part(i):
                r = TILE_ROWS[i]
                for b in range(4):
                    n = 4 * i + b
                    dve.wait_ge(x_tr, n + 1)
                    if n >= 4:
                        dve.wait_ge(x_lo, n - 3)
                    tt(fst[:, n % 4, :, 0:r], banks[n % 4].rearrange("p (k t) -> p k t", k=4)[:, :, 0:r],
                       bc(normw[:, 4 * b:4 * b + 4], r), ALU.mult).then_inc(x_f, 1)

            for i in range(5):
                r = TILE_ROWS[i]
                dve.wait_ge(x_rms, i + 1)
                dve.reciprocal(stat[0:r, 2, i:i + 1], stat[0:r, 1, i:i + 1]).then_inc(x_rstd, 1)
                dve.wait_ge(x_rstd, i + 1)
                dve.tensor_scalar(xt[0:r, i, :], xt[0:r, i, :], stat[0:r, 2, i:i + 1], None, ALU.mult).then_inc(x_scaled, 1)
                if i >= 1:
                    x_f_part(i - 1)
            x_f_part(4)
            dve.wait_ge(ba_loaded, 64)
            dve.wait_ge(ba_zero, 2)

            def parity(t, e):
                return t[:, :, 32 * e:32 * e + 16].rearrange("p k (b h) -> p k b h", b=2)

            for e in range(2):
                src = wba[:, :, :].rearrange("p k (b h e) -> p k b h e", b=2, e=2)[:, :, :, :, e]
                dve.tensor_copy(parity(wbh, e), src).then_inc(ba_hi, 1)
            dve.wait_ge(ba_hi, 2)
            for e in range(2):
                src = wba[:, :, :].rearrange("p k (b h e) -> p k b h e", b=2, e=2)[:, :, :, :, e]
                tt(parity(wbl, e), src, parity(wbh, e).bitcast(F32), ALU.subtract).then_inc(ba_lo, 1)
            for j in range(2):
                for q in range(4):
                    split_lo(0, 0, j, q)
            dve.memset(ba[0:48, 0:PAD], 0.0).then_inc(ba_row, 1)
            dve.wait_ge(ba_mm, 1)
            for i in range(2):
                dve.tensor_copy(ba[0:48, PAD + i * HALF:PAD + (i + 1) * HALF], pg[i][0:48, 0:HALF]).then_inc(ba_row, 1)
            dve.wait_ge(ba_row, 3)
            dve.tensor_copy(ba2[0:48], ba[0:48].rearrange("p (n c) -> p n c", c=C).unsqueeze(2).broadcast_to([48, NCH, 2, C])).then_inc(ba_row, 1)

            def table_dves(z, j, q):
                if (z, j, q) == (0, 1, 0):
                    dve.wait_ge(ba_tr, 1)
                    for e in range(2):
                        ph = slice(64 * e, 64 * e + 64)
                        src = pg[2][ph, 0:48 * NCH].rearrange("p (n r) -> p n r", r=48)[:, :, 32 * e:32 * e + 16]
                        dst = tb[ph, :, :, :].rearrange("p b a n -> p n (b a)")
                        ins = dve.tensor_copy(dst, src)
                    ins.then_inc(tab_dve, 1)
                    dve.wait_ge(tab_dve, 1)
                    for e in range(2):
                        ph = slice(64 * e, 64 * e + 64)
                        dtb = al[ph, 1, :].rearrange("p (h e) -> p h e", e=2)[:, :, e]
                        ins = tt(tq[ph, 0], tb[ph, 1], bc(dtb, NCH), ALU.add)
                    ins.then_inc(tab_dve, 1)
                if (z, j, q) == (0, 2, 0):
                    dve.wait_ge(tab_act, 5)
                    dve.scalar_tensor_tensor(tq[:, 4].rearrange("p a n -> p (a n)"), tq[:, 0].rearrange("p a n -> p (a n)"), 0.0,
                                             tq[:, 3].rearrange("p a n -> p (a n)"), ALU.max, ALU.add).then_inc(tab_mid, 1)
                    dve.wait_ge(tab_mid, 1)
                    for e in range(2):
                        ph = slice(64 * e, 64 * e + 64)
                        ea = al[ph, 0, :].rearrange("p (h e) -> p h e", e=2)[:, :, e]
                        ins = dve.scalar_tensor_tensor(tq[ph, 5], tq[ph, 4], -1.0, bc(ea, NCH), ALU.mult, ALU.mult)
                    ins.then_inc(tab_dve, 1)
                if (z, j, q) == (0, 3, 1):
                    dve.wait_ge(tab_mm, 1)
                    w = PAIRS * NCH
                    sums = pg[2][:, 0:4 * w].rearrange("p (i a n) -> p i a n", i=4, a=PAIRS)
                    dve.tensor_copy(table[:, :, GCUM, :], sums[:, 0]).then_inc(tab_mid, 1)
                    dve.tensor_copy(tq[:, 6:8], sums[:, 2:4]).then_inc(tab_dve, 1)
                    dve.wait_ge(tab_mid, 2)
                    tt(tq[:, 4], sums[:, 1], table[:, :, GCUM, :], ALU.subtract).then_inc(tab_dve, 1)
                if (z, j, q) == (1, 0, 3):
                    dve.wait_ge(tab_act, 9)
                    dve.scalar_tensor_tensor(table[:, :, NBEG, :], table[:, :, BETA, :], -1.0, table[:, :, EG, :],
                                             ALU.mult, ALU.mult).then_inc(tab_dve, 1)

            steps = [0]

            def pooling(g, c):
                dve.wait_ge(proj_evac, 4 * g + c + 1)
                need(dve, mix_mm, g)
                need(dve, pool_step, 2 * g + c)
                src, lag, n = ub[:, c, :], 1, 0
                while lag < WINDOWS[g]:
                    if n:
                        dve.wait_ge(pool_add, steps[0])
                    lo = 2 * lag - 1
                    tt(pa[:, n % 2, lo:T], src[:, lo:T], src[:, lo - lag:T - lag], ALU.add).then_inc(pool_add, 1)
                    steps[0] += 1
                    src, lag, n = pa[:, n % 2, :], 2 * lag, n + 1
                dve.wait_ge(pool_add, steps[0])
                dve.scalar_tensor_tensor(pooled[:, c, :], src[:, META:T], 1.0 / WINDOWS[g], ub[:, c, META:T],
                                         ALU.mult, ALU.subtract).then_inc(pool_step, 1)

            for g in range(GROUPS):
                for z in range(2):
                    for j in range(4):
                        def hook(q, z=z, j=j):
                            if g == 0:
                                table_dves(z, j, q)
                            if q == 0 and (z, j) == (0, 2):
                                pooling(g, 0)
                            if q == 0 and (z, j) == (1, 0):
                                pooling(g, 1)
                        window(2 * g + z, z, j, hook)
                dve.wait_ge(mix_mm, g + 1)
                dve.wait_ge(proj_evac, 4 * g + 4)
                need(dve, yp_stored, 16 * g)
                for d in range(2):
                    dve.scalar_tensor_tensor(yps[:, d, :], pg[d][:, :], pscale[:, 2 * g + d:2 * g + d + 1], szp[:, d, :],
                                             ALU.mult, ALU.mult).then_inc(yp_done, 1)

            def convolve(p, k, c, tap):
                n = (p * 6 + 2 * k + c) * 4
                which = (1, 0, 2)[k]
                acc = stg[:, k, c, :]
                src_tap = (3, 0, 1, 2)[tap]
                w = convcur[:, src_tap, which, c:c + 1]
                if tap == 0:
                    dve.wait_ge(proj_evac, 2 * CP_PAIR0 + 8 * p + 2 * k + c + 1)
                    need(dve, silu_done, p * 4 if k == 2 else p * 4 - 2)
                    dve.wait_ge(conv_cur, p + 1)
                    dve.tensor_scalar(acc, xin[:, src_tap:src_tap + T], w, None, ALU.mult).then_inc(conv_step, 1)
                else:
                    dve.wait_ge(conv_step, n + tap)
                    dve.scalar_tensor_tensor(acc, xin[:, src_tap:src_tap + T], w, acc, ALU.mult, ALU.add).then_inc(conv_step, 1)

            def delta(d, m):
                def wait(semaphore, per_pair, count):
                    need(dve, semaphore, d * per_pair + count)

                if m == 0:
                    wait(silu_done, 4, 1)
                    dve.tensor_copy(cur[:, :, :], table[:, bass.ds(d, 1), :, :].rearrange("p a k n -> p (a k) n")).then_inc(cur_ready, 1)
                if 2 <= m <= 4:
                    g = m - 2
                    if g == 0:
                        wait(cur_ready, 1, 1)
                    wait(gram_mm, NG, g + 1)
                    gram = pt[:, 0:GC * C].rearrange("p (n c) -> p n c", c=C)
                    rowg = pt[:, 256:256 + GC * C].rearrange("p (n c) -> p n c", c=C)
                    eye = cst[:, CI2:CI2 + C].unsqueeze(1).broadcast_to([P, GC, C])
                    kk = pg[g][:, 0:GC * 2 * C].rearrange("p (n a c) -> p n a c", a=2, c=C)[:, :, 0, :]
                    tt(ts[:, group(g), 1, :], gram, eye, ALU.mult)
                    tt(ts[:, group(g), 0, :], kk, eye, ALU.mult)
                    tt(dec[:, group(g), :], rowg, bc(cur[:, GCUM, group(g)], C), ALU.subtract).then_inc(gram_read, 1)
                if m == 5:
                    wait(gram_read, NG, NG)
                    mup = cst[:, CMUP:CMUP + C].unsqueeze(1).broadcast_to([P, NCH, C])
                    dve.tensor_reduce(norms[:, :, :], ts[:, :, :, :], AX_X, ALU.add)
                    tt(dec[:, :, :], dec[:, :, :], mup, ALU.min).then_inc(gram_sum, 1)
                if m == 6:
                    wait(norm_sqrt, 1, 1)
                    dve.reciprocal(rkq[:, :, :], rkq[:, :, :]).then_inc(rkq_ready, 1)
                    wait(rkq_ready, 1, 1)
                    rk = rkq[:, :, 0]
                    tt(sc[:, 0, :], cur[:, BETA, :], rk, ALU.mult)
                    tt(sc[:, 1, :], cur[:, NBEG, :], rk, ALU.mult)
                    tt(sc[:, 2, :], cur[:, EDEC, :], rk, ALU.mult)
                    dve.tensor_scalar(sc[:, 3, :], rkq[:, :, 1], HD ** -0.5, None, ALU.mult).then_inc(scale_ready, 1)
                if m == 7:
                    wait(decay_exp, 1, 1)
                    tt(dec[:, :, :], dec[:, :, :], bc(rkq[:, :, 0], C), ALU.mult).then_inc(decay_scaled, 1)
                if m == 8:
                    wait(decay_scaled, 1, 1)
                    for g in range(NG):
                        both = dec[:, group(g), :].unsqueeze(2).broadcast_to([P, GC, 2, C])
                        tt(mq[:, group(g), :, :], pg[g][:, 0:GC * 2 * C].rearrange("p (n a c) -> p n a c", a=2, c=C),
                           both, ALU.mult).then_inc(mq_ready, 1)
                if 9 <= m < 9 + 2 * LEVELS:
                    lv, second = (m - 9) // 2, (m - 9) % 2
                    for g in range(NG):
                        if not second:
                            wait(x_mm, NG * LEVELS, NG * lv + g + 1)
                            if lv == 0 and g == 0:
                                wait(scale_ready, 1, 1)
                            tt(xm[:, group(g), :], pg[g][:, 0:GC * C].rearrange("p (n c) -> p n c", c=C),
                               bc(sc[:, 0, group(g)], C), ALU.mult).then_inc(x_evac, 1)
                        else:
                            wait(ts_mm, NG * LEVELS, NG * lv + g + 1)
                            flat = ts[:, group(g), :, :].rearrange("p n a c -> p (n a c)")
                            if lv > 0:
                                wait(ts_upd, NG * LEVELS, NG * (lv - 1) + g + 1)
                            tt(flat, flat, pg[g][:, 0:GC * 2 * C], ALU.subtract).then_inc(ts_upd, 1)
                R0 = 9 + 2 * LEVELS
                if R0 <= m < R0 + 3 * NCH:
                    n, stage = (m - R0) // 3, (m - R0) % 3
                    if stage == 0 and n > 0:
                        wait(ks_mm, NCH - 1, n)
                        if n == 1:
                            wait(vk_tok, 2 * NCH, 2 * NCH)
                        dve.scalar_tensor_tensor(rr[:, :], pg[0][:, 0:HD], sc[:, 1, n:n + 1], vtok[:, n, :],
                                                 ALU.mult, ALU.add).then_inc(r_ready, 1)
                    if stage == 2:
                        if n < NCH - 1:
                            wait(st_mm, NCH - 1, n + 1)
                            if n > 0:
                                wait(st_upd, 2 * (NCH - 1), 2 * n)
                            for hd in range(2):
                                if n == 0:
                                    dve.tensor_copy(state[:, hd, :], pg[1 + hd][:, 0:HD]).then_inc(st_upd, 1)
                                else:
                                    dve.scalar_tensor_tensor(state[:, hd, :], state[:, hd, :], cur[:, GLA + hd, n:n + 1],
                                                             pg[1 + hd][:, 0:HD], ALU.mult, ALU.add).then_inc(st_upd, 1)
                        if n > 0:
                            wait(qkv_mm, NCH - 1, n)
                            wait(o_inter, NCH - 1, n)
                            tt(oo[:, n - 1, :], oo[:, n - 1, :], pt[:, 128:128 + HD], ALU.add).then_inc(o_ready, 1)
                if m == 49:
                    rqs = sc[:, 3, 1:NCH]
                    wait(o_ssq, NCH - 1, NCH - 1)
                    tt(oss[:, 1, :], oss[:, 0, :], rqs, ALU.mult).then_inc(o_var, 1)
                    wait(o_var, 2, 1)
                    tt(oss[:, 1, :], oss[:, 1, :], rqs, ALU.mult).then_inc(o_var, 1)
                if m == 50:
                    wait(o_sqrt, 1, 1)
                    dve.reciprocal(oss[:, 3, :], oss[:, 2, :]).then_inc(o_rstd, 1)
                    wait(o_rstd, 1, 1)
                    tt(oss[:, 1, :], oss[:, 3, :], sc[:, 3, 1:NCH], ALU.mult).then_inc(o_fac, 1)
                    wait(o_fac, 1, 1)
                    tt(oo[:, 0:4, :], oo[:, 0:4, :], bc(oss[:, 1, 0:4], HD), ALU.mult).then_inc(o_scaled, 1)
                if m == 51:
                    tt(oo[:, 4:8, :], oo[:, 4:8, :], bc(oss[:, 1, 4:8], HD), ALU.mult).then_inc(o_scaled, 1)
                for b in range(2):
                    if m == 53 + 2 * b:
                        wait(o_tr, 2, b + 1)
                        if b == 0:
                            wait(silu_done, 4, 4)
                        src = (pt if b == 0 else pg[0])[:, :].rearrange("p (n h c) -> p n h c", h=2, c=C)
                        for hd in range(2):
                            part = sz[:, hd, 256 * b:256 * (b + 1)].rearrange("p (n c) -> p n c", c=C)
                            dve.scalar_tensor_tensor(part, src[:, :, hd, :], dnw, part, ALU.mult, ALU.mult).then_inc(y_ready, 1)

            def pair_windows(p, d):
                for k in range(4):
                    for j in range(4):
                        def hook(q, k=k, j=j):
                            if k == 0 and j == 0 and q == 0:
                                dve.tensor_copy(convcur[:, :, :, :].rearrange("p t k h -> p (t k) h"),
                                                convc[:, :, :, bass.ds(2 * p, 2)].rearrange("p t k h -> p (t k) h")).then_inc(conv_cur, 1)
                            if d is not None:
                                delta(d, 16 * k + 4 * j + q)
                            if k < 3 and j == 2:
                                convolve(p, k, 0, q)
                            if k > 0 and j == 0:
                                convolve(p, k - 1, 1, q)
                        window(CP_PAIR0 + 4 * p + k, k % 2, j, hook)

            pair_windows(0, None)
            with dve.Fori(1, PAIRS) as p:
                pair_windows(p, p - 1)
            for k in range(4):
                for j in range(4):
                    window(CP_GATE0 + k, k % 2, j, lambda q, k=k, j=j: delta(PAIRS - 1, 16 * k + 4 * j + q))
            with dve.Fori(2, NGATE // 2 - 1) as i:
                for k in range(2):
                    for j in range(4):
                        window(CP_GATE0 + 2 * i + k, k, j, lambda q: None)
            for k in range(2):
                for j in range(4):
                    window(NCP - 2 + k, k, j, lambda q: None, last=(k == 1))

            def split_b(jp, j, q):
                c, u = j // 3, j % 3
                dve.wait_ge(hib, 24 * jp + 4 * j + q + 1)
                tt(bwl[:, u, 2 * q:2 * q + 2, :], rawb[:, u, 2 * q:2 * q + 2, c * P:(c + 1) * P],
                   bwh[:, u, 2 * q:2 * q + 2, :].bitcast(F32), ALU.subtract).then_inc(lob, 1)

            def y_lo_part(k):
                dve.wait_ge(y_hi, k + 1)
                tt(yl[:, k, :], yraw[:, k, :], yh[:, k, :].bitcast(F32), ALU.subtract).then_inc(y_lo, 1)

            for j in range(2):
                for q in range(4):
                    split_b(0, j, q)
                    y_lo_part(8 * j + 2 * q)
                    y_lo_part(8 * j + 2 * q + 1)

            def merge(jp, c):
                dve.wait_ge(peb, 6 * jp + 3 * c + 3)
                dve.wait_ge(gate_loaded[c], 32 * jp + 32)
                for i in range(2):
                    tt(gst[:, c, i, :], gst[:, c, i, :], pj[c][:, i, :], ALU.mult).then_inc(mg_step, 1)
                dve.wait_ge(mg_step, 4 * jp + 2 * c + 2)
                tt(merged[:, bass.ds(2 * jp + c, 1), :].rearrange("p a t -> p (a t)"), gst[:, c, 0, :], gst[:, c, 1, :],
                   ALU.add).then_inc(mg_done, 1)

            def window_b(jp, j, first, last):
                for q in range(4):
                    if j < 4:
                        split_b(jp, j + 2, q)
                    elif not last:
                        split_b(jp + 1, j - 4, q)
                    if first and j == 0:
                        y_lo_part(16 + 2 * q)
                        y_lo_part(16 + 2 * q + 1)
                if j % 3 == 2:
                    merge(jp, j // 3)

            for j in range(6):
                window_b(0, j, True, False)
            with dve.Fori(1, D // CW - 1) as jp:
                for j in range(6):
                    window_b(jp, j, False, False)
            for j in range(6):
                window_b(D // CW - 1, j, False, True)

            def split_c(cp, par, j, q):
                c, h = j // 2, j % 2
                dve.wait_ge(hic, 16 * cp + 4 * j + q + 1)
                tt(cwl[:, j, 2 * q:2 * q + 2, :], rawc[2 * par + h][:, 2 * q:2 * q + 2, c * P:(c + 1) * P],
                   cwh[:, j, 2 * q:2 * q + 2, :].bitcast(F32), ALU.subtract).then_inc(loc, 1)

            for j in range(2):
                for q in range(4):
                    split_c(0, 0, j, q)
                    for k in (8 * j + 2 * q, 8 * j + 2 * q + 1):
                        dve.wait_ge(m_hi, k + 1)
                        tt(ml[:, k, :], merged[:, k, :], mh[:, k, :].bitcast(F32), ALU.subtract).then_inc(m_lo, 1)

            def residual(count):
                dve.wait_ge(c_tr, count)
                if isinstance(count, int) and count == 1:
                    dve.wait_ge(xres_loaded, 16)
                col = (count - 1) * P
                tt(res[:, :, bass.ds(col, P)], pg[0][:, :].rearrange("p (n c) -> p n c", n=4),
                   xres[:, :, bass.ds(col, P)], ALU.add).then_inc(res_done, 1)

            def pair_c(cp, par, first, last=False):
                for j in range(4):
                    for q in range(4):
                        if not (last and j >= 2):
                            split_c(*target(cp, par, j), q)
                        if q == 3 and j == 0 and not first:
                            residual(2 * cp)
                        if q == 3 and j == 2:
                            residual(2 * cp + 1)

            pair_c(0, 0, True)
            pair_c(1, 1, False)
            with dve.Fori(1, D // CW // 2 - 1) as i:
                pair_c(2 * i, 0, False)
                pair_c(2 * i + 1, 1, False)
            pair_c(D // CW - 2, 0, False)
            pair_c(D // CW - 1, 1, False, last=True)
            residual(KT)
            dve.wait_ge(c_ssq, 4 * KT)
            dve.wait_ge(fnw_loaded, 16)
            dve.tensor_reduce(fin[:, 0, :], ssp[:, :, :], AX_X, ALU.add).then_inc(fin_sum, 1)
            dve.wait_ge(fin_sqrt, 1)
            dve.reciprocal(fin[:, 2, :], fin[:, 1, :]).then_inc(fin_rstd, 1)
            dve.wait_ge(fin_rstd, 1)
            for n in range(4):
                if n >= 2:
                    dve.wait_ge(fin_sqrt, n)
                for hf in range(2):
                    part = slice(hf * 1024, (hf + 1) * 1024)
                    if n < 2:
                        dve.scalar_tensor_tensor(res[:, n, part], res[:, n, part], fin[:, 2, n:n + 1], fnw[:, part],
                                                 ALU.mult, ALU.mult).then_inc(fin_done, 1)
                    else:
                        tt(res[:, n, part], res[:, n, part], fnw[:, part], ALU.mult).then_inc(fin_done, 1)

        @block.gpsimd
        def _(pool):
            def mix_load(g):
                need(pool, mix_mm, g)
                pool.dma_start(mixcur[:, :, :], pool_mix[0, bass.ds(g, 1), :, :].rearrange("g (c p) d -> p (g c) d", p=P)
                               ).then_inc(mix_loaded, 16)

            def branch_store(g):
                pool.wait_ge(yp_done, 2 * g + 2)
                pool.dma_start(y_d[bass.ds(g * GD, GD), :].rearrange("(c p) t -> p c t", p=P), yps[:, :, :]).then_inc(yp_stored, 16)

            for i in range(5):
                r, c0 = TILE_ROWS[i], TILE_COL[i]
                for b in range(4):
                    n = 4 * i + b
                    pool.wait_ge(x_hi, n + 1)
                    pool.tensor_tensor(xl[:, 4 * b:4 * b + 4, c0:c0 + r], fst[:, n % 4, :, 0:r],
                                       xh[:, 4 * b:4 * b + 4, c0:c0 + r].bitcast(F32), ALU.subtract).then_inc(x_lo, 1)
                if i == 3:
                    pool.wait_ge(x_sq, 5)
                    pool.memset(wbh[:, :, :].bitcast(F32), 0.0).then_inc(ba_zero, 1)
                    pool.memset(wbl[:, :, :].bitcast(F32), 0.0).then_inc(ba_zero, 1)
            pool.wait_ge(x_tr, 20)
            mix_load(0)
            branch_store(0)
            with pool.Fori(1, GROUPS) as g:
                mix_load(g)
                branch_store(g)
            pool.wait_ge(yp_stored, 16 * GROUPS)
            pool.wait_ge(proj_evac, 4 * GROUPS)
            pool.memset(xin[:, 0:TAPS - 1], 0.0).then_inc(zeroed, 1)
            pool.memset(kq[:, :, 0, :, 0:PAD], 0.0).then_inc(zeroed, 1)
            pool.memset(vch[:, 0, :, 0:PAD], 0.0).then_inc(zeroed, 1)

            pool.sem_inc(work_free, 1)
            with pool.Fori(0, PAIRS) as d:
                pool.wait_ge(gram_sum, d + 1)
                eye = cst[:, CI2:CI2 + C].unsqueeze(1).broadcast_to([P, 2 * NCH, C])
                pool.tensor_tensor(ts[:, :, :, :].rearrange("p n a c -> p (n a) c"), eye, eye, ALU.mult).then_inc(ts_init, 1)
                for lv in range(LEVELS):
                    for g in range(NG):
                        if lv == 0:
                            pool.wait_ge(mq_ready, d * NG + g + 1)
                        if lv >= 2:
                            pool.wait_ge(x_mm, d * (NG * LEVELS) + NG * (lv - 2) + g + 1)
                        mask = cst[:, CLEV + C * lv:CLEV + C * (lv + 1)].unsqueeze(1).broadcast_to([P, GC, C])
                        pool.tensor_tensor(bm[:, g, lv % 2], mq[:, group(g), 0, :], mask, ALU.mult).then_inc(b_masked, 1)
                pool.wait_ge(y_ready, 4 * d + 4)
                pool.dma_start(y_d[bass.ds(PW + CW * d, CW), :].rearrange("(h e) t -> e h t", e=P), sz[:, :, :]).then_inc(y_stored, 16)
                pool.wait_ge(y_stored, 16 * d + 16)
                pool.sem_inc(work_free, 1)

            def gate_load(jp, c, first):
                if first:
                    pool.wait_ge(y_lo, 24)
                    pool.wait_ge(gate_stored[0], 16 * NGATE)
                    pool.wait_ge(gate_stored[1], 16 * NGATE)
                else:
                    pool.wait_ge(mg_done, 2 * jp + c - 1)
                for i in range(2):
                    pool.dma_start(gst[:, c, i, :], gates_d[bass.ds(jp * CW + c * P + i * D, P), :]).then_inc(gate_loaded[c], 16)

            for c in range(2):
                gate_load(0, c, True)
            with pool.Fori(1, D // CW) as jp:
                for c in range(2):
                    gate_load(jp, c, False)


_INS = ["x", "meta_tokens", "norm_w", "w_in", "conv_w", "A_log", "dt_bias", "pool_mix", "pool_scale", "dn_norm_w",
        "w_pool_out", "w_dn_out", "w_o", "final_norm_w"]


def kernel(**inputs):
    import numpy as np
    import concourse.bacc as bacc
    from concourse.bass_utils import run_bass_kernel_spmd

    nc = bacc.Bacc("TRN2", target_bir_lowering=False, num_devices=1)
    arrays = {f"in_{n}": np.ascontiguousarray(inputs[n]) for n in _INS}
    arrays["in_consts"] = constants()
    args = [nc.dram_tensor(n, a.shape, mybir.dt.from_np(a.dtype), kind="ExternalInput").ap() for n, a in arrays.items()]
    out = nc.dram_tensor("out", (1, SEQ, D), F32, kind="ExternalOutput").ap()
    build(nc, *args, out)
    return run_bass_kernel_spmd(nc, [arrays], core_ids=[0]).results[0]["out"]
```

```python
from contextlib import ExitStack

import concourse.bass as bass
from concourse import mybir

F32 = mybir.dt.float32
F32R = mybir.dt.float32r
ALU = mybir.AluOpType
ACT = mybir.ActivationFunctionType
AX_X = mybir.AxisListType.X

P = 128
D = 2048
SEQ = 512
META = 16
T = SEQ + META
HALF = T // 2
KT = D // P
PW = 1024
GROUPS = 4
GD = PW // GROUPS
WINDOWS = (2, 4, 8, 16)
HEADS = 16
PAIRS = HEADS // 2
HD = 128
DNW = HEADS * HD
TAPS = 4
C = 64
PAD = C - META
NCH = (T + PAD) // C
LEVELS = 6
SHORT = 4
GC = 3
NG = NCH // GC
EPS = 1e-6
NEG = -3.0e4

COL_U, COL_ZP = 0, PW
COL_Q, COL_K, COL_V, COL_Z = 2 * PW, 2 * PW + DNW, 2 * PW + 2 * DNW, 2 * PW + 3 * DNW
COL_BA = 2 * PW + 4 * DNW
COL_GATE = COL_BA + 2 * HEADS
CW = 256
UK = 8
CP_PAIR0 = 2 * GROUPS
CP_GATE0 = CP_PAIR0 + 4 * PAIRS
NGATE = 2 * D // CW
NCP = CP_GATE0 + NGATE

CI, CI2 = 0, 128
CUP = 192
CHALF = 320
CPAIR = 322
CEPS = 386
NCONST = CEPS + 1
CU, CONES, CHA, CHB = (NCONST + P * i for i in range(4))
CLEV = CHB + P
NCOLS = CLEV + P * LEVELS
NTILE_CONV = 3 * HEADS
ROW_NORM, ROW_PS, ROW_DN = 2 * NTILE_CONV, 2 * NTILE_CONV + KT, 2 * NTILE_CONV + KT + PW // P
NROW_A, NROW_B = ROW_DN + 1, 2 * NTILE_CONV
BETA, GCUM, NEG_EG, EG, EDEC, GLA, GLB = range(7)
NKIND = 7


def constants():
    import numpy as np

    c = np.zeros((P, NCOLS), np.float32)
    c[:, CI:CI + P] = np.eye(P)
    s = np.arange(P) % C
    half = np.arange(P) // C
    col = np.arange(C)
    c[:, CI2:CI2 + C] = s[:, None] == col[None]
    c[:, CUP:CUP + P] = np.where((s[:, None] <= s[None]) & (half[:, None] == half[None]), 0.0, NEG)
    c[:, CPAIR:CPAIR + C] = (s[:, None] % 2 == 0) & (col[None] == s[:, None] + 1)
    for h in range(2):
        c[:, CHALF + h] = half == h
    for lv in range(LEVELS):
        a, b = s[:, None] >> lv, s[None] >> lv
        c[:, CLEV + P * lv:CLEV + P * (lv + 1)] = (b % 2 == 0) & (a == b + 1) & (half[:, None] == half[None])
    same = half[:, None] == half[None]
    c[:, CU:CU + P] = same & (s[:, None] <= s[None])
    c[:, CONES:CONES + P] = same
    c[:, CHA:CHA + P] = (half == 0)[:, None]
    c[:, CHB:CHB + P] = (half == 1)[:, None]
    c[:, CEPS] = EPS
    return c


def need(engine, semaphore, value):
    if isinstance(value, int) and value < 1:
        return
    engine.wait_ge(semaphore, value)


def build(nc, x, meta_tokens, norm_w, w_in, conv_w, A_log, dt_bias, pool_mix, pool_scale, dn_norm_w,
          w_pool_out, w_dn_out, w_o, final_norm_w, consts, out):
    gates_d = nc.dram_tensor("gates_scratch", (2 * D, SEQ), F32, kind="Internal").ap()
    y_d = nc.dram_tensor("branch_scratch", (PW + DNW, SEQ), F32, kind="Internal").ap()
    g_d = nc.dram_tensor("gate_sum_scratch", (PAIRS, 2, NCH, C), F32, kind="Internal").ap()

    outer = ExitStack()
    with outer:
        def tensors(stack):
            def sb(name, shape, dt=F32):
                return stack.enter_context(nc.sbuf_tensor(name, shape, dt))
            return sb

        def sem(name):
            return outer.enter_context(nc.semaphore(name))

        sb = tensors(outer)
        cst = sb("cst", [P, NCONST])
        vcol = sb("vcol", [P, NROW_A - ROW_NORM])
        convc = sb("convc", [P, TAPS, 3, HEADS])
        table = sb("table", [P, PAIRS, NKIND, NCH])
        ident = cst[:, CI:CI + P]
        eps = cst[:, CEPS:CEPS + 1]
        normw = vcol[:, 0:KT]
        pscale = vcol[:, KT:KT + PW // P]
        dnw = vcol[:, KT + PW // P:KT + PW // P + 1]

        WORK = 24 * SEQ + 3 * UK * CW + 320

        class Layout:

            def __init__(self):
                self.stack, self.at = ExitStack(), 0

            def tensor(self, name, shape, dt=F32):
                n = 1
                for k in shape:
                    n *= k
                self.at += n
                return self.stack.enter_context(nc.sbuf_tensor(name, [P] + list(shape), dt))

            def skip_to(self, column):
                assert column >= self.at, (column, self.at)
                if column > self.at:
                    self.tensor(f"skip{self.stack_id}_{self.at}", [column - self.at])

            def close(self):
                self.stack.close()

        def layout(number):
            made = Layout()
            made.stack_id = number
            return made

        lay = layout(0)
        kq = lay.tensor("kq", [2, NCH, 2, C])
        vch = lay.tensor("vch", [NCH, 2, C])
        sz = lay.tensor("sz", [2, SEQ])
        dec = lay.tensor("dec", [NCH, 2, C])
        mt = lay.tensor("mt", [NCH, 2, C])
        qk = lay.tensor("qk", [NCH, C])
        st = lay.tensor("st", [NCH, C])
        sq = lay.tensor("sq", [NCH, 2, C])
        ktok = lay.tensor("ktok", [NCH, HD])
        oo = lay.tensor("oo", [NCH - 1, HD])
        tm = oo[:, :, :].rearrange("p n e -> p (n e)")[:, 0:NCH * C].rearrange("p (n c) -> p n c", c=C)
        gates_at = lay.at
        stg = lay.tensor("stg", [3, 2, T])
        vtok = lay.tensor("vtok", [NCH, HD])
        pw, px = (vtok[:, :, i * C:(i + 1) * C] for i in range(2))
        xin = lay.tensor("xin", [TAPS - 1 + T])
        zst = lay.tensor("zst", [2, SEQ])
        convcur = lay.tensor("convcur", [TAPS, 3, 2])
        cur = lay.tensor("cur", [NKIND, NCH])
        state = lay.tensor("state", [2, HD])
        rr = lay.tensor("rr", [HD])
        vn = lay.tensor("vn", [HD])
        junk = lay.tensor("junk", [HD])
        norms = lay.tensor("norms", [2, NCH])
        rk = lay.tensor("rk", [2, NCH])
        qd = lay.tensor("qd", [3, NCH])
        lvm = lay.tensor("lvm", [LEVELS, 2, C])
        oss = lay.tensor("oss", [4, NCH - 1])
        lay.skip_to(WORK)
        raw = lay.tensor("raw", [4, UK, CW])
        xh = lay.tensor("xh", [KT, T], F32R)
        xl = lay.tensor("xl", [KT, T], F32R)
        wh = lay.tensor("wh", [4, UK, P], F32R)
        wl = lay.tensor("wl", [4, UK, P], F32R)
        lay.close()
        assert gates_at == 22 * SEQ
        gates_sb = [stg[:, 0, :, :].rearrange("p a t -> p (a t)")[:, i * SEQ:(i + 1) * SEQ] for i in range(2)]

        lay = layout(1)
        prow = lay.tensor("prow", [2, P])
        al = lay.tensor("al", [2, HEADS])
        wba = lay.tensor("wba", [KT, 2 * HEADS])
        sums = lay.tensor("sums", [4, P])
        at_xt = lay.at
        xt = lay.tensor("xt", [5, D])
        fst = lay.tensor("fst", [4, 4, P])
        stat = lay.tensor("stat", [3, 5])
        at_square = lay.at
        xsquare = lay.tensor("xsquare", [D])
        lay.close()
        lay = layout(2)
        lay.skip_to(at_xt)
        ba = lay.tensor("ba", [NCH * C])
        ba2 = lay.tensor("ba2", [NCH, 2, C])
        tb = lay.tensor("tb", [2, PAIRS, NCH])
        tq = lay.tensor("tq", [8, PAIRS, NCH])
        grow = lay.tensor("grow", [P])
        mixcur = lay.tensor("mixcur", [2, GD])
        ub = lay.tensor("ub", [2, T])
        pa = lay.tensor("pa", [2, T])
        pooled = lay.tensor("pooled", [2, SEQ])
        szp = lay.tensor("szp", [2, SEQ])
        yps = lay.tensor("yps", [2, SEQ])
        lay.skip_to(at_square)
        wbh = lay.tensor("wbh", [KT, P], F32R)
        wbl = lay.tensor("wbl", [KT, P], F32R)
        assert lay.at <= WORK
        lay.close()

        lay = layout(3)
        yraw = lay.tensor("yraw", [24, SEQ])
        rawb = lay.tensor("rawb", [3, UK, CW])
        yh = lay.tensor("yh", [24, SEQ], F32R)
        yl = lay.tensor("yl", [24, SEQ], F32R)
        bwh = lay.tensor("bwh", [3, UK, P], F32R)
        bwl = lay.tensor("bwl", [3, UK, P], F32R)
        lay.close()
        lay = layout(4)
        merged = lay.tensor("merged", [KT, SEQ])
        gst = lay.tensor("gst", [2, 2, SEQ])
        rawc3 = lay.tensor("rawc3", [UK, CW])
        lay.close()
        lay = layout(5)
        xres = lay.tensor("xres", [4, D])
        fnw = lay.tensor("fnw", [D])
        lay.skip_to(WORK)
        mh = lay.tensor("mh", [KT, SEQ], F32R)
        ml = lay.tensor("ml", [KT, SEQ], F32R)
        res = lay.tensor("res", [4, D])
        cwh = lay.tensor("cwh", [4, UK, P], F32R)
        cwl = lay.tensor("cwl", [4, UK, P], F32R)
        ot = lay.tensor("ot", [SEQ])
        lay.close()
        rawc = [rawb[:, 0], rawb[:, 1], rawb[:, 2], rawc3[:, :, :]]
        spare = table[:, :, :, :].rearrange("p a k n -> p (a k n)")
        ssp = spare[:, 0:4 * KT].rearrange("p (n k) -> p n k", n=4)
        fin = spare[:, 4 * KT:4 * KT + 12].rearrange("p (a n) -> p a n", a=3)

        pj = [outer.enter_context(nc.psum_tensor(f"pj{i}", [P, 2, 512], F32)) for i in range(2)]
        pg = [outer.enter_context(nc.psum_tensor(f"pg{i}", [P, 512], F32)) for i in range(NG)]
        pt = outer.enter_context(nc.psum_tensor("pt", [P, 512], F32))
        banks = [pj[0][:, 0, :], pj[0][:, 1, :], pj[1][:, 0, :], pj[1][:, 1, :]]

        cst_loaded, par_loaded, ba_loaded = sem("cst_loaded"), sem("par_loaded"), sem("ba_loaded")
        mix_loaded = sem("mix_loaded")
        xt_loaded = [sem(f"xt_loaded{i}") for i in range(5)]
        raw_loaded = [sem(f"raw_loaded{i}") for i in range(4)]
        rawb_loaded = [sem(f"rawb_loaded{i}") for i in range(3)]
        rawc_loaded = [sem(f"rawc_loaded{i}") for i in range(4)]
        par_tr, par_cols = sem("par_tr"), sem("par_cols")
        x_sq, x_rms, x_rstd, x_scaled = sem("x_sq"), sem("x_rms"), sem("x_rstd"), sem("x_scaled")
        x_tr, x_f, x_hi, x_lo = sem("x_tr"), sem("x_f"), sem("x_hi"), sem("x_lo")
        ba_zero, ba_hi, ba_lo, ba_mm, ba_row = sem("ba_zero"), sem("ba_hi"), sem("ba_lo"), sem("ba_mm"), sem("ba_row")
        ba_tr, ba_tok = sem("ba_tr"), sem("ba_tok")
        tab_act, tab_dve, tab_mid, tab_mm = sem("tab_act"), sem("tab_dve"), sem("tab_mid"), sem("tab_mm")
        zeroed = sem("zeroed")
        hi_done, lo_done, pe_piece, proj_evac = sem("hi_done"), sem("lo_done"), sem("pe_piece"), sem("proj_evac")
        pool_add, pool_step, mix_mm, yp_done, yp_stored = sem("pool_add"), sem("pool_step"), sem("mix_mm"), sem("yp_done"), sem("yp_stored")
        conv_cur, conv_step = sem("conv_cur"), sem("conv_step")
        gate_stored = [sem("gate_stored0"), sem("gate_stored1")]
        silu_done, cur_ready = sem("silu_done"), sem("cur_ready")
        gsum_tr, gsum_row, gsum_stored, rowg_loaded = sem("gsum_tr"), sem("gsum_row"), sem("gsum_stored"), sem("rowg_loaded")
        masks_loaded = sem("masks_loaded")
        dec_diff, dec_arg, decay_exp, dec_packed = sem("dec_diff"), sem("dec_arg"), sem("decay_exp"), sem("dec_packed")
        gram_mm, gram_diag, norm_sum, norm_sqrt = sem("gram_mm"), sem("gram_diag"), sem("norm_sum"), sem("norm_sqrt")
        rk_ready, qd_ready, s_init, mt_ready, qk_ready = sem("rk_ready"), sem("qd_ready"), sem("s_init"), sem("mt_ready"), sem("qk_ready")
        qd_shift, qd_pair, pair_dec, pair_fac, pair_x = sem("qd_shift"), sem("qd_pair"), sem("pair_dec"), sem("pair_fac"), sem("pair_x")
        tok_tr, tok_done, q_norm = sem("tok_tr"), sem("tok_done"), sem("q_norm")
        x_mm, x_ready, y_mm, s_ready = sem("x_mm"), sem("x_ready"), sem("y_mm"), sem("s_ready")
        t_tr, t_ready = sem("t_tr"), sem("t_ready")
        sq_pool, sq_act = sem("sq_pool"), sem("sq_act")
        ks_mm, qs_mm, r_ready, tr_mm, vn_ready = sem("ks_mm"), sem("qs_mm"), sem("r_ready"), sem("tr_mm"), sem("vn_ready")
        st_mm, st_upd, qkv_mm, o_inter, o_ready = sem("st_mm"), sem("st_upd"), sem("qkv_mm"), sem("o_inter"), sem("o_ready")
        o_ssq, o_var, o_sqrt, o_rstd, o_fac = sem("o_ssq"), sem("o_var"), sem("o_sqrt"), sem("o_rstd"), sem("o_fac")
        o_scaled, o_tr, y_ready, y_stored = sem("o_scaled"), sem("o_tr"), sem("y_ready"), sem("y_stored")
        work_free = sem("work_free")
        pe_gate = sem("pe_gate")
        yraw_tail, yraw_loaded, y_hi, y_lo = sem("yraw_tail"), sem("yraw_loaded"), sem("y_hi"), sem("y_lo")
        hib, lob, peb = sem("hib"), sem("lob"), sem("peb")
        gate_loaded = [sem("gate_loaded0"), sem("gate_loaded1")]
        mg_step, mg_done = sem("mg_step"), sem("mg_done")
        m_hi, m_lo = sem("m_hi"), sem("m_lo")
        hic, loc, pec, c_evac, c_tr, res_done = sem("hic"), sem("loc"), sem("pec"), sem("c_evac"), sem("c_tr"), sem("res_done")
        xres_loaded, fnw_loaded, c_ssq = sem("xres_loaded"), sem("fnw_loaded"), sem("c_ssq")
        fin_sum, fin_sqrt, fin_rstd, fin_done, out_stored = (
            sem("fin_sum"), sem("fin_sqrt"), sem("fin_rstd"), sem("fin_done"), sem("out_stored"))

        TILE_ROWS = [META] + [P] * 4
        TILE_COL = [0] + [META + P * i for i in range(4)]

        def chunk(t, n):
            return t[:, n * C:(n + 1) * C]

        def bc(ap, n):
            return ap.unsqueeze(2).broadcast_to([ap.shape[0], ap.shape[1], n])

        def group(g, lv=0):
            return slice(GC * g + (1 if g == 0 and lv >= SHORT else 0), GC * (g + 1))

        G0 = 3
        F0 = G0 + GC
        L0 = F0 + 7
        TOK_ROUNDS = {G0: [("k", n) for n in range(0, 4)], G0 + 1: [("k", n) for n in range(4, 8)], G0 + 2: [("k", 8)]}
        for i in range(3):
            TOK_ROUNDS[L0 + 3 * i] = [("v", n) for n in range(3 * i, 3 * i + 3)]
            TOK_ROUNDS[L0 + 9 + 3 * i] = [("q", n) for n in range(3 * i + 1, min(3 * i + 4, NCH))]
        TOK_STEPS = sorted(TOK_ROUNDS)
        K_TOK, V_TOK, ALL_TOK = NCH, 2 * NCH, 3 * NCH - 1

        def tok_before(m):
            return sum(len(TOK_ROUNDS[i]) for i in TOK_STEPS if i < m)

        def level_step(m):
            return ((m - L0 + 2) // 3, (m - L0 + 2) % 3) if L0 <= m < R0 else (None, None)

        R0 = L0 + 3 * LEVELS - 3
        O0 = R0 + 3 * NCH

        block = outer.enter_context(nc.Block())

        @block.sync
        def _(sp):
            sp.dma_start(cst[:, :], consts[:, 0:NCONST]).then_inc(cst_loaded, 16)
            for i in range(5):
                src = meta_tokens if i == 0 else x[0, (i - 1) * P:i * P, :]
                sp.dma_start(xt[0:TILE_ROWS[i], i, :], src).then_inc(xt_loaded[i], 16)
                if i == 1:
                    cv = conv_w[0].rearrange("t (n c) -> t n c", c=P)
                    n = NTILE_CONV
                    sp.dma_start(prow[0:n, 0, :], cv[0]).then_inc(par_loaded, 16)
                    sp.dma_start(prow[n:2 * n, 0, :], cv[1]).then_inc(par_loaded, 16)
                    sp.dma_start(prow[0:n, 1, :], cv[2]).then_inc(par_loaded, 16)
                    sp.dma_start(prow[n:2 * n, 1, :], cv[3]).then_inc(par_loaded, 16)
                    sp.dma_start(prow[ROW_NORM:ROW_PS, 0, :], norm_w[0].rearrange("(k p) -> k p", p=P)).then_inc(par_loaded, 16)
                    sp.dma_start(prow[ROW_PS:ROW_DN, 0, :], pool_scale[0].rearrange("(k p) -> k p", p=P)).then_inc(par_loaded, 16)
                    sp.dma_start(prow[ROW_DN:ROW_DN + 1, 0, :], dn_norm_w).then_inc(par_loaded, 16)
            sp.dma_start(wba[:, :, :], w_in[0, :, COL_BA:COL_GATE].rearrange("(k p) c -> p k c", p=P)).then_inc(ba_loaded, 16)
            sp.dma_start(sums[:, :, :], consts[:, CU:CU + 4 * P].rearrange("p (i c) -> p i c", i=4)).then_inc(ba_loaded, 16)
            sp.dma_start(al[:, 0, :], A_log.broadcast_to([P, HEADS])).then_inc(ba_loaded, 16)
            sp.dma_start(al[:, 1, :], dt_bias.broadcast_to([P, HEADS])).then_inc(ba_loaded, 16)

            def load_cp(cp, par, col):
                for h in range(2):
                    need(sp, lo_done, 16 * cp + 4 * h - 20)
                    sp.dma_start(raw[:, 2 * par + h, :, :],
                                 w_in[0, h * UK * P:(h + 1) * UK * P, bass.ds(col, CW)].rearrange("(k p) c -> p k c", p=P)
                                 ).then_inc(raw_loaded[2 * par + h], 16)

            load_cp(0, 0, COL_U)
            load_cp(1, 1, COL_ZP)
            with sp.Fori(1, GROUPS) as g:
                load_cp(2 * g, 0, COL_U + g * CW)
                load_cp(2 * g + 1, 1, COL_ZP + g * CW)
            with sp.Fori(0, PAIRS) as p:
                for k, col in enumerate((COL_K, COL_Q, COL_V, COL_Z)):
                    load_cp(CP_PAIR0 + 4 * p + k, k % 2, col + p * CW)
            with sp.Fori(0, NGATE // 2) as i:
                load_cp(CP_GATE0 + 2 * i, 0, COL_GATE + i * (2 * CW))
                load_cp(CP_GATE0 + 2 * i + 1, 1, COL_GATE + CW + i * (2 * CW))

            sp.wait_ge(y_stored, 16 * PAIRS)
            sp.wait_ge(yp_stored, 16 * GROUPS)
            y_rows = y_d.rearrange("(k p) t -> p k t", p=P)
            sp.dma_start(yraw[:, 0:22, :], y_rows[:, 0:22, :]).then_inc(yraw_loaded, 16)

            def load_b(jp, first):
                for u in range(3):
                    if not first:
                        need(sp, lob, 24 * jp + 4 * u - 8)
                    w = w_pool_out if u == 0 else w_dn_out
                    r = 0 if u < 2 else UK * P
                    sp.dma_start(rawb[:, u, :, :],
                                 w[0, r:r + UK * P, bass.ds(jp * CW, CW)].rearrange("(k p) c -> p k c", p=P)
                                 ).then_inc(rawb_loaded[u], 16)

            load_b(0, True)
            for c in range(2):
                sp.wait_ge(gate_stored[c], 16 * NGATE)
            sp.dma_start(yraw[:, 22:24, :], y_rows[:, 22:24, :]).then_inc(yraw_tail, 16)
            with sp.Fori(1, D // CW) as jp:
                load_b(jp, False)

            def load_c(cp, par, first):
                for h in range(2):
                    slot = 2 * par + h
                    if first:
                        if slot < 3:
                            sp.wait_ge(lob, 24 * (D // CW) + 4 * slot - 8)
                        else:
                            sp.wait_ge(y_lo, 24)
                    else:
                        need(sp, loc, 16 * cp + 4 * h - 20)
                    sp.dma_start(rawc[slot],
                                 w_o[0, h * UK * P:(h + 1) * UK * P, bass.ds(cp * CW, CW)].rearrange("(k p) c -> p k c", p=P)
                                 ).then_inc(rawc_loaded[slot], 16)

            load_c(0, 0, True)
            load_c(1, 1, True)
            sp.wait_ge(m_hi, KT)
            sp.wait_ge(m_lo, KT)
            sp.dma_start(xres[:, :, :], x[0].rearrange("(n p) d -> p n d", p=P)).then_inc(xres_loaded, 16)
            sp.dma_start(fnw[:, :], final_norm_w.unsqueeze(0).broadcast_to([P, D])).then_inc(fnw_loaded, 16)
            with sp.Fori(1, D // CW // 2) as i:
                load_c(2 * i, 0, False)
                load_c(2 * i + 1, 1, False)
            for n in range(4):
                for hf in range(2):
                    sp.wait_ge(fin_done, 2 * n + hf + 1)
                    sp.dma_start(out[0, n * P:(n + 1) * P, hf * 1024:(hf + 1) * 1024],
                                 res[:, n, hf * 1024:(hf + 1) * 1024]).then_inc(out_stored, 16)
            sp.wait_ge(out_stored, 16 * 8)

        @block.tensor
        def _(pe):
            def product(dst, lhs, rhs, start, stop):
                return pe.matmul(dst, lhs, rhs, start=start, stop=stop)

            def window(cp, c, h, full, hook):
                pe.wait_ge(lo_done, 16 * cp + 8 * c + 4 * h + 4)
                if h == 0:
                    need(pe, proj_evac, 2 * cp + c - 1)
                halves = [(pj[c][:, i, 0:HALF], i * HALF, HALF) for i in range(2)] if full else \
                    [(pj[c][:, 0, 0:SEQ], META, SEQ)]
                slot = 2 * c + h
                for k in range(UK):
                    kt = h * UK + k
                    for w, xx, first, last in ((wh, xh, True, False), (wh, xl, False, False), (wl, xh, False, True)):
                        for dst, c0, n in halves:
                            mm = product(dst, w[:, slot, k, :], xx[:, kt, c0:c0 + n],
                                         first and kt == 0, last and kt == KT - 1)
                    if k == UK - 1:
                        mm.then_inc(pe_piece, 1)
                    if k % 2 == 1:
                        hook(k // 2)

            pe.wait_ge(cst_loaded, 16)
            pe.wait_ge(par_loaded, 16 * 7)
            pe.transpose(pt[:, 0:NROW_A], prow[0:NROW_A, 0, :], cst[0:NROW_A, CI:CI + NROW_A])
            pe.transpose(pt[:, 128:128 + NROW_B], prow[0:NROW_B, 1, :], cst[0:NROW_B, CI:CI + NROW_B]).then_inc(par_tr, 1)
            for i in range(5):
                r = TILE_ROWS[i]
                pe.wait_ge(x_scaled, i + 1)
                for b in range(4):
                    n = 4 * i + b
                    if n >= 4:
                        pe.wait_ge(x_f, n - 3)
                    for k in range(4):
                        kt = 4 * b + k
                        mm = pe.transpose(banks[n % 4][:, k * P:k * P + r], xt[0:r, i, kt * P:(kt + 1) * P],
                                          cst[0:r, CI:CI + r])
                    mm.then_inc(x_tr, 1)
            pe.wait_ge(x_lo, 20)
            pe.wait_ge(ba_lo, 2)
            for kt in range(KT):
                for w, xx, first, last in ((wbh, xh, True, False), (wbh, xl, False, False), (wbl, xh, False, True)):
                    for i in range(2):
                        mm = product(pg[i][:, 0:HALF], w[:, kt, :], xx[:, kt, i * HALF:(i + 1) * HALF],
                                     first and kt == 0, last and kt == KT - 1)
            mm.then_inc(ba_mm, 1)

            def no_hook(q):
                return None

            def table_steps(cp, j, q):
                if (cp, j, q) == (0, 1, 0):
                    pe.wait_ge(ba_row, 4)
                    for n in range(NCH):
                        lhs = ba2[0:48, n, :, :].rearrange("p a c -> p (a c)")
                        mm = pe.transpose(pg[2][:, 48 * n:48 * (n + 1)], lhs, cst[0:48, CI:CI + 48])
                    mm.then_inc(ba_tr, 1)
                if (cp, j, q) == (0, 3, 0):
                    pe.wait_ge(tab_dve, 3)
                    g = tq[:, 5, :, :].rearrange("p a n -> p (a n)")
                    w = PAIRS * NCH
                    pe.wait_ge(ba_loaded, 64)
                    for i in range(4):
                        mm = product(pg[2][:, i * w:(i + 1) * w], sums[:, i, :], g, True, True)
                    mm.then_inc(tab_mm, 1)
                if (cp, j, q) == (1, 0, 0):
                    pe.wait_ge(tab_dve, 5)
                    w = PAIRS * NCH
                    pe.transpose(pg[2][0:w, 0:P], tq[:, 5, :, :].rearrange("p a n -> p (a n)"), ident).then_inc(gsum_tr, 1)

            def pool_windows(g, first):
                for z in range(2):
                    for j in range(4):
                        def hook(q, z=z, j=j):
                            if first:
                                table_steps(z, j, q)
                            if (z, j, q) == (1, 2, 3):
                                pe.wait_ge(mix_loaded, 16 * g + 16)
                                pe.wait_ge(pool_step, 2 * g + 2)
                                need(pe, yp_done, 2 * g)
                                for d in range(2):
                                    for cc in range(2):
                                        mm = product(pg[d][:, 0:SEQ], mixcur[:, cc, d * P:(d + 1) * P],
                                                     pooled[:, cc, :], cc == 0, cc == 1)
                                mm.then_inc(mix_mm, 1)
                        window(2 * g + z, j // 2, j % 2, z == 0, hook)

            pool_windows(0, True)
            with pe.Fori(1, GROUPS) as g:
                pool_windows(g, False)

            def delta(d, m):
                def wait(semaphore, per_pair, count):
                    need(pe, semaphore, d * per_pair + count)

                def alone():
                    pe.sem_inc(pe_gate, 1)

                if G0 <= m < G0 + NG:
                    g = m - G0
                    if g == 0:
                        wait(silu_done, 4, 2)
                        wait(cur_ready, 1, 1)
                        pe.wait_ge(yp_done, 2 * GROUPS)
                        pe.wait_ge(tab_dve, 6)
                        alone()
                    for n in range(GC * g, GC * (g + 1)):
                        i = n - GC * g
                        for hd in range(2):
                            ph = slice(64 * hd, 64 * hd + 64)
                            mm = product(pg[g][ph, 128 * i:128 * (i + 1)].rearrange("p (a c) -> p a c", a=2),
                                         kq[:, 0, n, hd, :], kq[:, :, n, hd, :], True, True)
                    mm.then_inc(gram_mm, 1)
                if m in TOK_ROUNDS:
                    if m == TOK_STEPS[0]:
                        pass
                    else:
                        wait(tok_done, ALL_TOK, tok_before(m))
                    if TOK_ROUNDS[m][0] == ("v", 0):
                        wait(silu_done, 4, 3)
                        wait(qd_pair, 1, 1)
                    for i, (what, n) in enumerate(TOK_ROUNDS[m]):
                        src = vch[:, n] if what == "v" else kq[:, "kq".index(what), n]
                        mm = pe.transpose(pt[:, i * P:(i + 1) * P], src.rearrange("p h c -> p (h c)"), ident)
                    mm.then_inc(tok_tr, 1)
                if m == F0 + 2:
                    wait(qd_ready, 1, 1)
                    wait(tok_done, ALL_TOK, K_TOK)
                    pe.wait_ge(masks_loaded, 16)
                    alone()
                    product(pt[:, 0:NCH], lvm[:, 0, :, :].rearrange("p h c -> p (h c)"), qd[:, 1, :], True, True).then_inc(qd_shift, 1)
                lv, stage = level_step(m)
                if lv is not None:
                    for g in range(NG):
                        chunks = group(g, lv)

                        def quadrants(t, n):
                            return t[:, n, :, :].rearrange("p h c -> p (h c)")

                        if stage == 0:
                            wait(t_ready, NG * (LEVELS - 1), NG * (lv - 1) + g + 1)
                            alone()
                        if stage == 1:
                            wait(x_ready, NG * (LEVELS - 1), NG * (lv - 1) + g + 1)
                            alone()
                        if stage == 2:
                            if g == 1:
                                wait(sq_act, LEVELS, lv + 1)
                            else:
                                wait(sq_pool, 2 * LEVELS, 2 * lv + 1 + g // 2)
                            alone()
                        for n in range(chunks.start, chunks.stop):
                            i = n - GC * g
                            if stage == 0:
                                mm = product(pg[g][:, C * i:C * (i + 1)], quadrants(mt, n), tm[:, n, :], True, True)
                            if stage == 1:
                                mm = product(pg[g][:, 192 + C * i:192 + C * (i + 1)], quadrants(dec, n), st[:, n, :], True, True)
                            if stage == 2:
                                mm = pe.transpose(pg[g][:, P * i:P * (i + 1)], quadrants(sq, n), ident)
                        mm.then_inc((x_mm, y_mm, t_tr)[stage], 1)
                if R0 <= m < O0:
                    n, stage = (m - R0) // 3, (m - R0) % 3
                    if stage == 0 and n > 0:
                        wait(st_upd, 2 * (NCH - 1), 2 * n)
                        if n == 1:
                            wait(vn_ready, NCH, 1)
                        for hd in range(2):
                            mm = product(pg[0][64 * hd:64 * hd + 64, 0:HD], kq[:, 0, n, hd, :], state[:, hd, :], True, True)
                        mm.then_inc(ks_mm, 1)
                        if n > 1:
                            wait(o_ready, NCH - 1, n - 1)
                        else:
                            wait(tok_done, ALL_TOK, ALL_TOK)
                        for hd in range(2):
                            mm = product(pt[64 * hd:64 * hd + 64, 0:HD], kq[:, 1, n, hd, :], state[:, hd, :], True, True)
                        mm.then_inc(qs_mm, 1)
                    if stage == 1:
                        if n == 0:
                            wait(sq_act, LEVELS, LEVELS)
                            wait(sq_pool, 2 * LEVELS, 2 * LEVELS)
                            wait(tok_done, ALL_TOK, V_TOK)
                            rhs = vtok[:, 0, :]
                        else:
                            wait(r_ready, NCH - 1, n)
                            rhs = rr[:, :]
                        mm = product(pg[0][:, 128:128 + HD], sq[:, n, :, :].rearrange("p h c -> p (h c)"), rhs, True, True)
                        mm.then_inc(tr_mm, 1)
                    if stage == 2:
                        wait(vn_ready, NCH, n + 1)
                        if n < NCH - 1:
                            for hd in range(2):
                                ph = slice(64 * hd, 64 * hd + 64)
                                mm = product(pg[1 + hd][:, 0:HD], ktok[ph, n, :], vn[ph, :], True, True)
                            mm.then_inc(st_mm, 1)
                        if n > 0:
                            wait(o_inter, NCH - 1, n)
                            alone()
                            for hd in range(2):
                                ph = slice(64 * hd, 64 * hd + 64)
                                mm = product(pt[ph, 128:128 + HD], qk[ph, n, :], vn[ph, :], True, True)
                            mm.then_inc(qkv_mm, 1)
                for b in range(2):
                    if m == O0 + 4 + 2 * b:
                        wait(o_scaled, 2, b + 1)
                        if b == 0:
                            wait(o_ready, NCH - 1, NCH - 1)
                        for i in range(4):
                            mm = pe.transpose((pt if b == 0 else pg[0])[:, i * P:(i + 1) * P], oo[:, 4 * b + i, :], ident)
                        mm.then_inc(o_tr, 1)

            def pair_windows(p, d):
                for k in range(4):
                    for j in range(4):
                        def hook(q, k=k, j=j):
                            if d is not None:
                                delta(d, 16 * k + 4 * j + q)
                        window(CP_PAIR0 + 4 * p + k, j // 2, j % 2, k < 3, hook)

            pair_windows(0, None)
            with pe.Fori(1, PAIRS) as p:
                pair_windows(p, p - 1)
            for k in range(4):
                for j in range(4):
                    window(CP_GATE0 + k, j // 2, j % 2, False, lambda q, k=k, j=j: delta(PAIRS - 1, 16 * k + 4 * j + q))
            with pe.Fori(2, NGATE // 2) as i:
                for k in range(2):
                    for j in range(4):
                        window(CP_GATE0 + 2 * i + k, j // 2, j % 2, False, no_hook)

            def window_b(jp, c, u, first):
                pe.wait_ge(lob, 24 * jp + 12 * c + 4 * u + 4)
                if u == 0:
                    if first:
                        pe.wait_ge(proj_evac, 2 * NCP - 1 + c)
                    else:
                        pe.wait_ge(mg_done, 2 * jp + c - 1)
                dst = pj[c][:, 0 if u == 0 else 1, :]
                for k in range(UK):
                    kt = u * UK + k
                    if first and c == 0:
                        pe.wait_ge(y_lo, kt + 1)
                    for w, yy, one, last in ((bwh, yh, True, False), (bwh, yl, False, False), (bwl, yh, False, True)):
                        mm = product(dst, w[:, u, k, :], yy[:, kt, :], one and k == 0 and u < 2,
                                     last and k == UK - 1 and u != 1)
                mm.then_inc(peb, 1)

            for c in range(2):
                for u in range(3):
                    window_b(0, c, u, True)
            with pe.Fori(1, D // CW) as jp:
                for c in range(2):
                    for u in range(3):
                        window_b(jp, c, u, False)

            def back(count):
                pe.wait_ge(c_evac, count)
                need(pe, c_ssq, 4 * (count - 1))
                for n in range(4):
                    mm = pe.transpose(pg[0][:, n * P:(n + 1) * P], ot[:, n * P:(n + 1) * P], ident)
                mm.then_inc(c_tr, 1)

            def window_c(cp, c, h, first):
                pe.wait_ge(loc, 16 * cp + 8 * c + 4 * h + 4)
                if h == 0:
                    if first and c == 0 and isinstance(cp, int) and cp == 0:
                        pe.wait_ge(mg_done, KT)
                    else:
                        need(pe, c_evac, 2 * cp + c - 1)
                for k in range(UK):
                    kt = h * UK + k
                    if first and c == 0:
                        pe.wait_ge(m_lo, kt + 1)
                    for w, yy, one, last in ((cwh, mh, True, False), (cwh, ml, False, False), (cwl, mh, False, True)):
                        mm = product(pj[c][:, 0, :], w[:, 2 * c + h, k, :], yy[:, kt, :], one and kt == 0, last and kt == KT - 1)
                mm.then_inc(pec, 1)

            def pair_c(cp, first):
                for j in range(4):
                    window_c(cp, j // 2, j % 2, first)
                    if j == 0 and not first:
                        back(2 * cp)
                    if j == 2:
                        back(2 * cp + 1)

            pair_c(0, True)
            pair_c(1, False)
            with pe.Fori(1, D // CW // 2) as i:
                pair_c(2 * i, False)
                pair_c(2 * i + 1, False)
            back(2 * (D // CW))

        def target(cp, par, j):
            return (cp, par, j + 2) if j < 2 else (cp + 1, 1 - par, j - 2)

        @block.scalar
        def _(act):
            def copy(dst, src):
                return act.activation(dst, src, ACT.Copy)

            def split_hi(cp, par, j, q):
                c, h = j // 2, j % 2
                if q == 0:
                    if c == 0:
                        act.wait_ge(raw_loaded[2 * par + h], 8 * cp + 16 - 8 * par)
                    need(act, pe_piece, 4 * cp + j - 3)
                copy(wh[:, j, 2 * q:2 * q + 2, :],
                     raw[:, 2 * par + h, 2 * q:2 * q + 2, c * P:(c + 1) * P]).then_inc(hi_done, 1)

            def window(cp, par, j, hook, evac, last=False):
                for q in range(4):
                    if not (last and j >= 2):
                        split_hi(*target(cp, par, j), q)
                    hook(q)
                if j % 2 == 1:
                    act.wait_ge(pe_piece, 4 * cp + j + 1)
                    evac(j // 2)

            def x_hi_part(i):
                r, c0 = TILE_ROWS[i], TILE_COL[i]
                for b in range(4):
                    n = 4 * i + b
                    act.wait_ge(x_f, n + 1)
                    copy(xh[:, 4 * b:4 * b + 4, c0:c0 + r], fst[:, n % 4, :, 0:r]).then_inc(x_hi, 1)

            act.wait_ge(cst_loaded, 16)
            for i in range(5):
                r = TILE_ROWS[i]
                act.wait_ge(xt_loaded[i], 16)
                act.activation(xsquare[0:r, :], xt[0:r, i, :], ACT.Square, accum_out=stat[0:r, 0, i:i + 1]).then_inc(x_sq, 1)
                act.wait_ge(x_sq, i + 1)
                act.activation(stat[0:r, 1, i:i + 1], stat[0:r, 0, i:i + 1], ACT.Sqrt, bias=eps[0:r, :], scale=1.0 / D).then_inc(x_rms, 1)
                if i >= 1:
                    x_hi_part(i - 1)
            x_hi_part(4)

            for j in range(2):
                for q in range(4):
                    split_hi(0, 0, j, q)

            def nothing(q):
                return None

            def table_acts(z, j, q):
                if (z, j, q) == (0, 1, 3):
                    act.wait_ge(tab_dve, 2)
                    act.activation(tq[:, 1], tq[:, 0], ACT.Abs).then_inc(tab_act, 1)
                    act.wait_ge(tab_act, 1)
                    act.activation(tq[:, 2], tq[:, 1], ACT.Exp, scale=-1.0).then_inc(tab_act, 1)
                    act.wait_ge(tab_act, 2)
                    act.activation(tq[:, 3], tq[:, 2], ACT.Ln, bias=1.0).then_inc(tab_act, 1)
                    act.activation(al[:, 0, :], al[:, 0, :], ACT.Exp).then_inc(tab_act, 1)
                    act.activation(table[:, :, BETA, :], tb[:, 0], ACT.Sigmoid).then_inc(tab_act, 1)
                if (z, j, q) == (1, 0, 0):
                    act.wait_ge(tab_dve, 5)
                    act.activation(table[:, :, EG, :], table[:, :, GCUM, :], ACT.Exp).then_inc(tab_act, 1)
                    act.activation(table[:, :, EDEC, :], tq[:, 4], ACT.Exp).then_inc(tab_act, 1)
                    act.activation(table[:, :, GLA, :], tq[:, 6], ACT.Exp).then_inc(tab_act, 1)
                    act.activation(table[:, :, GLB, :], tq[:, 7], ACT.Exp).then_inc(tab_act, 1)

            def pool_windows(g, first):
                for z in range(2):
                    def evac(c, z=z):
                        if z == 0:
                            need(act, pool_step, 2 * g)
                            copy(ub[:, c, :].rearrange("p (a t) -> p a t", a=2), pj[c][:, :, 0:HALF]).then_inc(proj_evac, 1)
                        else:
                            need(act, yp_done, 2 * g)
                            act.activation(szp[:, c, :], pj[c][:, 0, :], ACT.Silu).then_inc(proj_evac, 1)
                    for j in range(4):
                        hook = (lambda q, z=z, j=j: table_acts(z, j, q)) if first else nothing
                        window(2 * g + z, z, j, hook, evac)

            pool_windows(0, True)
            with act.Fori(1, GROUPS) as g:
                pool_windows(g, False)

            def silu_chunks(dst, src):
                act.activation(dst[:, 0, :, PAD:], src[:, :, 0:META], ACT.Silu)
                act.activation(dst[:, 1:NCH].rearrange("p n h c -> p h n c"),
                               src[:, :, META:T].rearrange("p h (n c) -> p h n c", c=C), ACT.Silu).then_inc(silu_done, 1)

            def delta(d, m):
                def wait(semaphore, per_pair, count):
                    need(act, semaphore, d * per_pair + count)

                if m == 0:
                    wait(conv_step, 4 * 6, 4 * 6)
                    for kk in range(2):
                        silu_chunks(kq[:, kk], stg[:, kk])
                if m == 1:
                    silu_chunks(vch, stg[:, 2])
                if m == R0:
                    wait(work_free, 1, 1)
                    act.wait_ge(proj_evac, 2 * CP_PAIR0 + 8 * d + 8)
                    act.activation(sz[:, :, :], zst[:, :, :], ACT.Silu).then_inc(silu_done, 1)
                if m == F0:
                    wait(norm_sum, 1, 1)
                    act.activation(rk[:, 0, :], norms[:, 0, :], ACT.Sqrt, bias=eps).then_inc(norm_sqrt, 1)
                if m == G0 + 1:
                    wait(dec_arg, 1, 1)
                    act.activation(dec[:, :, :, :], dec[:, :, :, :], ACT.Exp).then_inc(decay_exp, 1)
                if m in TOK_ROUNDS:
                    if m == TOK_STEPS[0]:
                        wait(cur_ready, 1, 1)
                    if TOK_ROUNDS[m][0] == ("v", 0):
                        wait(norm_sqrt, 1, 1)
                        wait(s_ready, NG * LEVELS, NG)
                    wait(tok_tr, len(TOK_STEPS), TOK_STEPS.index(m) + 1)
                    for i, (what, n) in enumerate(TOK_ROUNDS[m]):
                        src = pt[:, i * P:(i + 1) * P]
                        if what == "k":
                            act.activation(ktok[:, n, :], src, ACT.Copy, scale=cur[:, EDEC, n:n + 1]).then_inc(tok_done, 1)
                        elif what == "v":
                            act.activation(vtok[:, n, :], src, ACT.Copy, scale=rk[:, 0, n:n + 1]).then_inc(tok_done, 1)
                        else:
                            act.activation(src, src, ACT.Square, accum_out=norms[:, 1, n:n + 1]).then_inc(tok_done, 1)
                lv, stage = level_step(m)
                if stage == 1 or m == L0 - 1:
                    lv = lv or 0
                    wait(s_ready, NG * LEVELS, NG * lv + 2)
                    for hd in range(2):
                        ins = act.activation(sq[:, group(1), hd, :], st[:, group(1), :], ACT.Copy, scale=cst[:, CHALF + hd:CHALF + hd + 1])
                    ins.then_inc(sq_act, 1)
                if stage == 2:
                    for g in range(NG):
                        chunks = group(g, lv)
                        wait(t_tr, NG * (LEVELS - 1), NG * lv + g + 1)
                        for hd in range(2):
                            ph = slice(64 * hd, 64 * hd + 64)
                            src = pg[g][ph, 0:GC * P].rearrange("p (n h c) -> p n h c", h=2, c=C)[:, chunks.start - GC * g:, hd, :]
                            ins = copy(tm[ph, chunks, :], src)
                        ins.then_inc(t_ready, 1)
                if R0 <= m < O0:
                    n, stage = (m - R0) // 3, (m - R0) % 3
                    if stage == 0 and n > 0:
                        wait(qs_mm, NCH - 1, n)
                        act.activation(oo[:, n - 1, :], pt[:, 0:HD], ACT.Copy, scale=cur[:, EG, n:n + 1]).then_inc(o_inter, 1)
                    if stage == 1:
                        wait(tr_mm, NCH, n + 1)
                        copy(vn[:, :], pg[0][:, 128:128 + HD]).then_inc(vn_ready, 1)
                    if stage == 1 and n > 1:
                        wait(o_ready, NCH - 1, n - 1)
                        act.activation(junk[:, :], oo[:, n - 2, :], ACT.Square, accum_out=oss[:, 0, n - 2:n - 1]).then_inc(o_ssq, 1)
                if m == O0:
                    wait(o_ready, NCH - 1, NCH - 1)
                    act.activation(junk[:, :], oo[:, NCH - 2, :], ACT.Square, accum_out=oss[:, 0, NCH - 2:NCH - 1]).then_inc(o_ssq, 1)
                if m == O0 + 1:
                    wait(o_var, 1, 1)
                    act.activation(oss[:, 2, :], oss[:, 1, :], ACT.Sqrt, bias=eps, scale=1.0 / HD).then_inc(o_sqrt, 1)

            def pair_windows(p, d):
                for k in range(4):
                    def evac(c, k=k):
                        if k < 3:
                            need(act, conv_step, (p * 6 + 2 * k + c) * 4)
                            if k == 0 and c == 0 and isinstance(p, int) and p == 0:
                                act.wait_ge(zeroed, 3)
                            copy(xin[:, TAPS - 1:].rearrange("p (a t) -> p a t", a=2), pj[c][:, :, 0:HALF]).then_inc(proj_evac, 1)
                        else:
                            copy(zst[:, c, :], pj[c][:, 0, :]).then_inc(proj_evac, 1)
                    for j in range(4):
                        hook = nothing if d is None else (lambda q, k=k, j=j: delta(d, 16 * k + 4 * j + q))
                        window(CP_PAIR0 + 4 * p + k, k % 2, j, hook, evac)

            pair_windows(0, None)
            with act.Fori(1, PAIRS) as p:
                pair_windows(p, p - 1)

            def gate_evac(i):
                def evac(c):
                    need(act, gate_stored[c], 16 * i)
                    act.activation(gates_sb[c], pj[c][:, 0, :], ACT.Sigmoid).then_inc(proj_evac, 1)
                    act.wait_ge(proj_evac, 2 * CP_GATE0 + 2 * i + c + 1)
                    act.dma_start(gates_d[bass.ds((2 * i + c) * P, P), :], gates_sb[c]).then_inc(gate_stored[c], 16)
                return evac

            for k in range(4):
                for j in range(4):
                    window(CP_GATE0 + k, k % 2, j, lambda q, k=k, j=j: delta(PAIRS - 1, 16 * k + 4 * j + q), gate_evac(k))
            with act.Fori(2, NGATE // 2 - 1) as i:
                for k in range(2):
                    for j in range(4):
                        window(CP_GATE0 + 2 * i + k, k, j, nothing, gate_evac(2 * i + k))
            for k in range(2):
                for j in range(4):
                    window(NCP - 2 + k, k, j, nothing, gate_evac(NGATE - 2 + k), last=(k == 1))

            def split_b(jp, j, q):
                c, u = j // 3, j % 3
                if q == 0:
                    if c == 0:
                        act.wait_ge(rawb_loaded[u], 16 * jp + 16)
                    need(act, peb, 6 * jp + j - 2)
                copy(bwh[:, u, 2 * q:2 * q + 2, :], rawb[:, u, 2 * q:2 * q + 2, c * P:(c + 1) * P]).then_inc(hib, 1)

            def y_hi_part(k):
                copy(yh[:, k, :], yraw[:, k, :]).then_inc(y_hi, 1)

            act.wait_ge(pe_piece, 4 * NCP)
            act.wait_ge(yraw_loaded, 16)
            for j in range(2):
                for q in range(4):
                    split_b(0, j, q)
                    y_hi_part(8 * j + 2 * q)
                    y_hi_part(8 * j + 2 * q + 1)

            def window_b(jp, j, first, last):
                for q in range(4):
                    if j < 4:
                        split_b(jp, j + 2, q)
                    elif not last:
                        split_b(jp + 1, j - 4, q)
                    if first and j == 0:
                        if q == 3:
                            act.wait_ge(yraw_tail, 16)
                        y_hi_part(16 + 2 * q)
                        y_hi_part(16 + 2 * q + 1)

            for j in range(6):
                window_b(0, j, True, False)
            with act.Fori(1, D // CW - 1) as jp:
                for j in range(6):
                    window_b(jp, j, False, False)
            for j in range(6):
                window_b(D // CW - 1, j, False, True)

            def split_c(cp, par, j, q):
                c, h = j // 2, j % 2
                if q == 0:
                    if c == 0:
                        act.wait_ge(rawc_loaded[2 * par + h], 8 * cp + 16 - 8 * par)
                    need(act, pec, 4 * cp + j - 3)
                copy(cwh[:, j, 2 * q:2 * q + 2, :], rawc[2 * par + h][:, 2 * q:2 * q + 2, c * P:(c + 1) * P]).then_inc(hic, 1)

            act.wait_ge(peb, 6 * (D // CW))
            act.wait_ge(mg_done, KT)
            for j in range(2):
                for q in range(4):
                    split_c(0, 0, j, q)
                    for k in (8 * j + 2 * q, 8 * j + 2 * q + 1):
                        copy(mh[:, k, :], merged[:, k, :]).then_inc(m_hi, 1)

            def squares(count):
                act.wait_ge(res_done, count)
                need(act, c_ssq, 4 * (count - 1))
                for n in range(4):
                    col = (count - 1) * P
                    act.activation(pt[:, n * P:(n + 1) * P], res[:, n, bass.ds(col, P)], ACT.Square,
                                   accum_out=ssp[:, n, bass.ds(count - 1, 1)]).then_inc(c_ssq, 1)

            def pair_c(cp, par, first, last=False):
                for j in range(4):
                    for q in range(4):
                        if not (last and j >= 2):
                            split_c(*target(cp, par, j), q)
                        if q == 3 and j == 0 and not first:
                            squares(2 * cp)
                        if q == 3 and j == 2:
                            squares(2 * cp + 1)
                    if j % 2 == 1:
                        act.wait_ge(pec, 4 * cp + j + 1)
                        need(act, c_tr, 2 * cp + j // 2)
                        copy(ot[:, :], pj[j // 2][:, 0, :]).then_inc(c_evac, 1)

            pair_c(0, 0, True)
            pair_c(1, 1, False)
            with act.Fori(1, D // CW // 2 - 1) as i:
                pair_c(2 * i, 0, False)
                pair_c(2 * i + 1, 1, False)
            pair_c(D // CW - 2, 0, False)
            pair_c(D // CW - 1, 1, False, last=True)
            squares(KT)
            act.wait_ge(fin_sum, 1)
            act.activation(fin[:, 1, :], fin[:, 0, :], ACT.Sqrt, bias=eps, scale=1.0 / D).then_inc(fin_sqrt, 1)
            for n in range(2, 4):
                act.wait_ge(fin_rstd, 1)
                act.activation(res[:, n, :], res[:, n, :], ACT.Copy, scale=fin[:, 2, n:n + 1]).then_inc(fin_sqrt, 1)

        @block.vector
        def _(dve):
            tt = dve.tensor_tensor

            def split_lo(cp, par, j, q):
                c, h = j // 2, j % 2
                dve.wait_ge(hi_done, 16 * cp + 4 * j + q + 1)
                tt(wl[:, j, 2 * q:2 * q + 2, :], raw[:, 2 * par + h, 2 * q:2 * q + 2, c * P:(c + 1) * P],
                   wh[:, j, 2 * q:2 * q + 2, :].bitcast(F32), ALU.subtract).then_inc(lo_done, 1)

            def window(cp, par, j, hook, last=False):
                for q in range(4):
                    if not (last and j >= 2):
                        split_lo(*target(cp, par, j), q)
                    hook(q)

            dve.wait_ge(par_tr, 1)
            dve.tensor_copy(convc[:, 0:2, :, :].rearrange("p a b c -> p (a b c)"), pt[:, 0:2 * NTILE_CONV]).then_inc(par_cols, 1)
            dve.tensor_copy(vcol[:, :], pt[:, ROW_NORM:NROW_A]).then_inc(par_cols, 1)
            dve.tensor_copy(convc[:, 2:4, :, :].rearrange("p a b c -> p (a b c)"), pt[:, 128:128 + NROW_B]).then_inc(par_cols, 1)
            dve.wait_ge(par_cols, 3)

            def x_f_part(i):
                r = TILE_ROWS[i]
                for b in range(4):
                    n = 4 * i + b
                    dve.wait_ge(x_tr, n + 1)
                    if n >= 4:
                        dve.wait_ge(x_lo, n - 3)
                    tt(fst[:, n % 4, :, 0:r], banks[n % 4].rearrange("p (k t) -> p k t", k=4)[:, :, 0:r],
                       bc(normw[:, 4 * b:4 * b + 4], r), ALU.mult).then_inc(x_f, 1)

            for i in range(5):
                r = TILE_ROWS[i]
                dve.wait_ge(x_rms, i + 1)
                dve.reciprocal(stat[0:r, 2, i:i + 1], stat[0:r, 1, i:i + 1]).then_inc(x_rstd, 1)
                dve.wait_ge(x_rstd, i + 1)
                dve.tensor_scalar(xt[0:r, i, :], xt[0:r, i, :], stat[0:r, 2, i:i + 1], None, ALU.mult).then_inc(x_scaled, 1)
                if i >= 1:
                    x_f_part(i - 1)
            x_f_part(4)
            dve.wait_ge(ba_loaded, 64)
            dve.wait_ge(ba_zero, 2)

            def parity(t, e):
                return t[:, :, 32 * e:32 * e + 16].rearrange("p k (b h) -> p k b h", b=2)

            for e in range(2):
                src = wba[:, :, :].rearrange("p k (b h e) -> p k b h e", b=2, e=2)[:, :, :, :, e]
                dve.tensor_copy(parity(wbh, e), src).then_inc(ba_hi, 1)
            dve.wait_ge(ba_hi, 2)
            for e in range(2):
                src = wba[:, :, :].rearrange("p k (b h e) -> p k b h e", b=2, e=2)[:, :, :, :, e]
                tt(parity(wbl, e), src, parity(wbh, e).bitcast(F32), ALU.subtract).then_inc(ba_lo, 1)
            for j in range(2):
                for q in range(4):
                    split_lo(0, 0, j, q)
            dve.memset(ba[0:48, 0:PAD], 0.0).then_inc(ba_row, 1)
            dve.wait_ge(ba_mm, 1)
            for i in range(2):
                dve.tensor_copy(ba[0:48, PAD + i * HALF:PAD + (i + 1) * HALF], pg[i][0:48, 0:HALF]).then_inc(ba_row, 1)
            dve.wait_ge(ba_row, 3)
            dve.tensor_copy(ba2[0:48], ba[0:48].rearrange("p (n c) -> p n c", c=C).unsqueeze(2).broadcast_to([48, NCH, 2, C])).then_inc(ba_row, 1)

            def table_dves(z, j, q):
                if (z, j, q) == (0, 1, 0):
                    dve.wait_ge(ba_tr, 1)
                    for e in range(2):
                        ph = slice(64 * e, 64 * e + 64)
                        src = pg[2][ph, 0:48 * NCH].rearrange("p (n r) -> p n r", r=48)[:, :, 32 * e:32 * e + 16]
                        dst = tb[ph, :, :, :].rearrange("p b a n -> p n (b a)")
                        ins = dve.tensor_copy(dst, src)
                    ins.then_inc(tab_dve, 1)
                    dve.wait_ge(tab_dve, 1)
                    for e in range(2):
                        ph = slice(64 * e, 64 * e + 64)
                        dtb = al[ph, 1, :].rearrange("p (h e) -> p h e", e=2)[:, :, e]
                        ins = tt(tq[ph, 0], tb[ph, 1], bc(dtb, NCH), ALU.add)
                    ins.then_inc(tab_dve, 1)
                if (z, j, q) == (0, 2, 0):
                    dve.wait_ge(tab_act, 5)
                    dve.scalar_tensor_tensor(tq[:, 4].rearrange("p a n -> p (a n)"), tq[:, 0].rearrange("p a n -> p (a n)"), 0.0,
                                             tq[:, 3].rearrange("p a n -> p (a n)"), ALU.max, ALU.add).then_inc(tab_mid, 1)
                    dve.wait_ge(tab_mid, 1)
                    for e in range(2):
                        ph = slice(64 * e, 64 * e + 64)
                        ea = al[ph, 0, :].rearrange("p (h e) -> p h e", e=2)[:, :, e]
                        ins = dve.scalar_tensor_tensor(tq[ph, 5], tq[ph, 4], -1.0, bc(ea, NCH), ALU.mult, ALU.mult)
                    ins.then_inc(tab_dve, 1)
                if (z, j, q) == (0, 3, 1):
                    dve.wait_ge(tab_mm, 1)
                    w = PAIRS * NCH
                    sums = pg[2][:, 0:4 * w].rearrange("p (i a n) -> p i a n", i=4, a=PAIRS)
                    dve.tensor_copy(table[:, :, GCUM, :], sums[:, 0]).then_inc(tab_mid, 1)
                    dve.tensor_copy(tq[:, 5], sums[:, 0])
                    dve.tensor_copy(tq[:, 6:8], sums[:, 2:4]).then_inc(tab_dve, 1)
                    dve.wait_ge(tab_mid, 2)
                    tt(tq[:, 4], sums[:, 1], table[:, :, GCUM, :], ALU.subtract).then_inc(tab_dve, 1)
                if (z, j, q) == (1, 0, 3):
                    dve.wait_ge(tab_act, 9)
                    dve.tensor_scalar(table[:, :, NEG_EG, :], table[:, :, EG, :], -1.0, None, ALU.mult).then_inc(tab_dve, 1)
                    dve.wait_ge(gsum_tr, 1)
                    dve.tensor_copy(grow[0:PAIRS * NCH, :], pg[2][0:PAIRS * NCH, 0:P]).then_inc(gsum_row, 1)

            steps = [0]

            def pooling(g, c):
                dve.wait_ge(proj_evac, 4 * g + c + 1)
                need(dve, mix_mm, g)
                need(dve, pool_step, 2 * g + c)
                src, lag, n = ub[:, c, :], 1, 0
                while lag < WINDOWS[g]:
                    if n:
                        dve.wait_ge(pool_add, steps[0])
                    lo = 2 * lag - 1
                    tt(pa[:, n % 2, lo:T], src[:, lo:T], src[:, lo - lag:T - lag], ALU.add).then_inc(pool_add, 1)
                    steps[0] += 1
                    src, lag, n = pa[:, n % 2, :], 2 * lag, n + 1
                dve.wait_ge(pool_add, steps[0])
                dve.scalar_tensor_tensor(pooled[:, c, :], src[:, META:T], 1.0 / WINDOWS[g], ub[:, c, META:T],
                                         ALU.mult, ALU.subtract).then_inc(pool_step, 1)

            for g in range(GROUPS):
                for z in range(2):
                    for j in range(4):
                        def hook(q, z=z, j=j):
                            if g == 0:
                                table_dves(z, j, q)
                            if q == 0 and (z, j) == (0, 2):
                                pooling(g, 0)
                            if q == 0 and (z, j) == (1, 0):
                                pooling(g, 1)
                        window(2 * g + z, z, j, hook)
                dve.wait_ge(mix_mm, g + 1)
                dve.wait_ge(proj_evac, 4 * g + 4)
                need(dve, yp_stored, 16 * g)
                for d in range(2):
                    dve.scalar_tensor_tensor(yps[:, d, :], pg[d][:, :], pscale[:, 2 * g + d:2 * g + d + 1], szp[:, d, :],
                                             ALU.mult, ALU.mult).then_inc(yp_done, 1)

            def convolve(p, k, c, tap):
                n = (p * 6 + 2 * k + c) * 4
                which = (1, 0, 2)[k]
                acc = stg[:, k, c, :]
                src_tap = (3, 0, 1, 2)[tap]
                w = convcur[:, src_tap, which, c:c + 1]
                if tap == 0:
                    dve.wait_ge(proj_evac, 2 * CP_PAIR0 + 8 * p + 2 * k + c + 1)
                    need(dve, silu_done, p * 4 if k == 2 else p * 4 - 2)
                    dve.wait_ge(conv_cur, p + 1)
                    dve.tensor_scalar(acc, xin[:, src_tap:src_tap + T], w, None, ALU.mult).then_inc(conv_step, 1)
                else:
                    dve.wait_ge(conv_step, n + tap)
                    dve.scalar_tensor_tensor(acc, xin[:, src_tap:src_tap + T], w, acc, ALU.mult, ALU.add).then_inc(conv_step, 1)

            def delta(d, m):
                def wait(semaphore, per_pair, count):
                    need(dve, semaphore, d * per_pair + count)

                if m == 0:
                    wait(silu_done, 4, 1)
                    dve.tensor_copy(cur[:, :, :], table[:, bass.ds(d, 1), :, :].rearrange("p a k n -> p (a k) n")).then_inc(cur_ready, 1)
                if G0 <= m < G0 + NG:
                    g = m - G0
                    wait(gram_mm, NG, g + 1)
                    kk = pg[g][:, 0:GC * 2 * C].rearrange("p (n a c) -> p n a c", a=2, c=C)[:, :, 0, :]
                    tt(st[:, group(g), :], kk, cst[:, CI2:CI2 + C].unsqueeze(1).broadcast_to([P, GC, C]), ALU.mult).then_inc(gram_diag, 1)
                if m == G0 + 2:
                    wait(gram_diag, NG, NG)
                    dve.tensor_reduce(norms[:, 0, :], st[:, :, :], AX_X, ALU.add).then_inc(norm_sum, 1)
                if m == G0:
                    wait(dec_diff, 1, 1)
                    guard = cst[:, CUP:CUP + P].rearrange("p (a c) -> p a c", a=2).unsqueeze(1).broadcast_to([P, NCH, 2, C])
                    tt(dec[:, :, :, :], dec[:, :, :, :], guard, ALU.min).then_inc(dec_arg, 1)
                if m == F0 + 1:
                    wait(norm_sqrt, 1, 1)
                    dve.reciprocal(rk[:, 1, :], rk[:, 0, :]).then_inc(rk_ready, 1)
                    wait(rk_ready, 2, 1)
                    tt(qd[:, 0, :], cur[:, BETA, :], rk[:, 1, :], ALU.mult).then_inc(rk_ready, 1)
                    wait(rk_ready, 2, 2)
                    tt(qd[:, 1, :], qd[:, 0, :], rk[:, 1, :], ALU.mult).then_inc(qd_ready, 1)
                    wait(qd_ready, 1, 1)
                    tt(st[:, :, :], cst[:, CI2:CI2 + C].unsqueeze(1).broadcast_to([P, NCH, C]), bc(qd[:, 1, :], C), ALU.mult).then_inc(s_init, 1)

                def twice(ap):
                    return ap.unsqueeze(2).broadcast_to([P, ap.shape[1], 2, C])

                if m == F0 + 2:
                    wait(decay_exp, 1, 1)
                    for g in range(NG):
                        kk = pg[g][:, 0:GC * 2 * C].rearrange("p (n a c) -> p n a c", a=2, c=C)[:, :, 0, :]
                        tt(mt[:, group(g), :, :], twice(kk), dec[:, group(g), :, :], ALU.mult).then_inc(mt_ready, 1)
                    wait(qd_shift, 1, 1)
                    tt(qd[:, 2, :], pt[:, 0:NCH], qd[:, 1, :], ALU.mult).then_inc(qd_pair, 1)
                if m == F0 + 3:
                    wait(dec_packed, 1, 1)
                    for g in range(NG):
                        kq_g = pg[g][:, 0:GC * 2 * C].rearrange("p (n a c) -> p n a c", a=2, c=C)[:, :, 1, :]
                        tt(qk[:, group(g), :], kq_g, tm[:, group(g), :], ALU.mult).then_inc(qk_ready, 1)
                if m == F0 + 4:
                    wait(pair_fac, 1, 1)
                    wait(s_init, 1, 1)
                    for g in range(NG):
                        kk = pg[g][:, 0:GC * 2 * C].rearrange("p (n a c) -> p n a c", a=2, c=C)[:, :, 0, :]
                        tt(px[:, group(g), :], kk, pw[:, group(g), :], ALU.mult).then_inc(pair_x, 1)
                    for g in range(NG):
                        wait(pair_x, NG, g + 1)
                        tt(st[:, group(g), :], st[:, group(g), :], px[:, group(g), :], ALU.subtract).then_inc(s_ready, 1)
                lv, stage = level_step(m)
                if stage in (0, 1):
                    for g in range(NG):
                        chunks = group(g, lv)
                        cols = slice(C * (chunks.start - GC * g) + 192 * stage, 192 + 192 * stage)
                        src = pg[g][:, cols].rearrange("p (n c) -> p n c", c=C)
                        if stage == 0:
                            wait(x_mm, NG * (LEVELS - 1), NG * (lv - 1) + g + 1)
                            pattern = lvm[:, lv, :, :].unsqueeze(1).broadcast_to([P, chunks.stop - chunks.start, 2, C])
                            tt(dec[:, chunks, :, :], twice(src), pattern, ALU.mult).then_inc(x_ready, 1)
                        else:
                            wait(y_mm, NG * (LEVELS - 1), NG * (lv - 1) + g + 1)
                            wait(s_ready, NG * LEVELS, NG * (lv - 1) + g + 1)
                            tt(st[:, chunks, :], st[:, chunks, :], src, ALU.subtract).then_inc(s_ready, 1)
                if R0 <= m < O0:
                    n, stage = (m - R0) // 3, (m - R0) % 3
                    if stage == 0 and n > 0:
                        wait(ks_mm, NCH - 1, n)
                        if n == 1:
                            wait(tok_done, ALL_TOK, V_TOK)
                        dve.scalar_tensor_tensor(rr[:, :], pg[0][:, 0:HD], cur[:, NEG_EG, n:n + 1], vtok[:, n, :],
                                                 ALU.mult, ALU.add).then_inc(r_ready, 1)
                    if stage == 2:
                        if n < NCH - 1:
                            wait(st_mm, NCH - 1, n + 1)
                            if n > 0:
                                wait(st_upd, 2 * (NCH - 1), 2 * n)
                            for hd in range(2):
                                if n == 0:
                                    dve.tensor_copy(state[:, hd, :], pg[1 + hd][:, 0:HD]).then_inc(st_upd, 1)
                                else:
                                    dve.scalar_tensor_tensor(state[:, hd, :], state[:, hd, :], cur[:, GLA + hd, n:n + 1],
                                                             pg[1 + hd][:, 0:HD], ALU.mult, ALU.add).then_inc(st_upd, 1)
                        if n > 0:
                            wait(qkv_mm, NCH - 1, n)
                            wait(o_inter, NCH - 1, n)
                            tt(oo[:, n - 1, :], oo[:, n - 1, :], pt[:, 128:128 + HD], ALU.add).then_inc(o_ready, 1)
                if m == O0 + 1:
                    wait(o_ssq, NCH - 1, NCH - 1)
                    wait(tok_done, ALL_TOK, ALL_TOK)
                    dve.tensor_scalar(oss[:, 3, :], norms[:, 1, 1:NCH], EPS, EPS * HD * HD, ALU.add, ALU.mult).then_inc(o_fac, 1)
                    wait(o_fac, 1, 1)
                    tt(oss[:, 1, :], oss[:, 0, :], oss[:, 3, :], ALU.add).then_inc(o_var, 1)
                if m == O0 + 2:
                    wait(o_sqrt, 1, 1)
                    dve.reciprocal(oss[:, 1, :], oss[:, 2, :]).then_inc(o_rstd, 1)
                    wait(o_rstd, 1, 1)
                    tt(oo[:, 0:4, :], oo[:, 0:4, :], bc(oss[:, 1, 0:4], HD), ALU.mult).then_inc(o_scaled, 1)
                if m == O0 + 3:
                    tt(oo[:, 4:8, :], oo[:, 4:8, :], bc(oss[:, 1, 4:8], HD), ALU.mult).then_inc(o_scaled, 1)
                for b in range(2):
                    if m == O0 + 5 + 2 * b:
                        wait(o_tr, 2, b + 1)
                        if b == 0:
                            wait(silu_done, 4, 4)
                        src = (pt if b == 0 else pg[0])[:, :].rearrange("p (n h c) -> p n h c", h=2, c=C)
                        for hd in range(2):
                            part = sz[:, hd, 256 * b:256 * (b + 1)].rearrange("p (n c) -> p n c", c=C)
                            dve.scalar_tensor_tensor(part, src[:, :, hd, :], dnw, part, ALU.mult, ALU.mult).then_inc(y_ready, 1)

            def pair_windows(p, d):
                for k in range(4):
                    for j in range(4):
                        def hook(q, k=k, j=j):
                            if k == 0 and j == 0 and q == 0:
                                dve.tensor_copy(convcur[:, :, :, :].rearrange("p t k h -> p (t k) h"),
                                                convc[:, :, :, bass.ds(2 * p, 2)].rearrange("p t k h -> p (t k) h")).then_inc(conv_cur, 1)
                            if d is not None:
                                delta(d, 16 * k + 4 * j + q)
                            if k < 3 and j == 2:
                                convolve(p, k, 0, q)
                            if k > 0 and j == 0:
                                convolve(p, k - 1, 1, q)
                        window(CP_PAIR0 + 4 * p + k, k % 2, j, hook)

            pair_windows(0, None)
            with dve.Fori(1, PAIRS) as p:
                pair_windows(p, p - 1)
            for k in range(4):
                for j in range(4):
                    window(CP_GATE0 + k, k % 2, j, lambda q, k=k, j=j: delta(PAIRS - 1, 16 * k + 4 * j + q))
            with dve.Fori(2, NGATE // 2 - 1) as i:
                for k in range(2):
                    for j in range(4):
                        window(CP_GATE0 + 2 * i + k, k, j, lambda q: None)
            for k in range(2):
                for j in range(4):
                    window(NCP - 2 + k, k, j, lambda q: None, last=(k == 1))

            def split_b(jp, j, q):
                c, u = j // 3, j % 3
                dve.wait_ge(hib, 24 * jp + 4 * j + q + 1)
                tt(bwl[:, u, 2 * q:2 * q + 2, :], rawb[:, u, 2 * q:2 * q + 2, c * P:(c + 1) * P],
                   bwh[:, u, 2 * q:2 * q + 2, :].bitcast(F32), ALU.subtract).then_inc(lob, 1)

            def y_lo_part(k):
                dve.wait_ge(y_hi, k + 1)
                tt(yl[:, k, :], yraw[:, k, :], yh[:, k, :].bitcast(F32), ALU.subtract).then_inc(y_lo, 1)

            for j in range(2):
                for q in range(4):
                    split_b(0, j, q)
                    y_lo_part(8 * j + 2 * q)
                    y_lo_part(8 * j + 2 * q + 1)

            def merge(jp, c):
                dve.wait_ge(peb, 6 * jp + 3 * c + 3)
                dve.wait_ge(gate_loaded[c], 32 * jp + 32)
                for i in range(2):
                    tt(gst[:, c, i, :], gst[:, c, i, :], pj[c][:, i, :], ALU.mult).then_inc(mg_step, 1)
                dve.wait_ge(mg_step, 4 * jp + 2 * c + 2)
                tt(merged[:, bass.ds(2 * jp + c, 1), :].rearrange("p a t -> p (a t)"), gst[:, c, 0, :], gst[:, c, 1, :],
                   ALU.add).then_inc(mg_done, 1)

            def window_b(jp, j, first, last):
                for q in range(4):
                    if j < 4:
                        split_b(jp, j + 2, q)
                    elif not last:
                        split_b(jp + 1, j - 4, q)
                    if first and j == 0:
                        y_lo_part(16 + 2 * q)
                        y_lo_part(16 + 2 * q + 1)
                if j % 3 == 2:
                    merge(jp, j // 3)

            for j in range(6):
                window_b(0, j, True, False)
            with dve.Fori(1, D // CW - 1) as jp:
                for j in range(6):
                    window_b(jp, j, False, False)
            for j in range(6):
                window_b(D // CW - 1, j, False, True)

            def split_c(cp, par, j, q):
                c, h = j // 2, j % 2
                dve.wait_ge(hic, 16 * cp + 4 * j + q + 1)
                tt(cwl[:, j, 2 * q:2 * q + 2, :], rawc[2 * par + h][:, 2 * q:2 * q + 2, c * P:(c + 1) * P],
                   cwh[:, j, 2 * q:2 * q + 2, :].bitcast(F32), ALU.subtract).then_inc(loc, 1)

            for j in range(2):
                for q in range(4):
                    split_c(0, 0, j, q)
                    for k in (8 * j + 2 * q, 8 * j + 2 * q + 1):
                        dve.wait_ge(m_hi, k + 1)
                        tt(ml[:, k, :], merged[:, k, :], mh[:, k, :].bitcast(F32), ALU.subtract).then_inc(m_lo, 1)

            def residual(count):
                dve.wait_ge(c_tr, count)
                if isinstance(count, int) and count == 1:
                    dve.wait_ge(xres_loaded, 16)
                col = (count - 1) * P
                tt(res[:, :, bass.ds(col, P)], pg[0][:, :].rearrange("p (n c) -> p n c", n=4),
                   xres[:, :, bass.ds(col, P)], ALU.add).then_inc(res_done, 1)

            def pair_c(cp, par, first, last=False):
                for j in range(4):
                    for q in range(4):
                        if not (last and j >= 2):
                            split_c(*target(cp, par, j), q)
                        if q == 3 and j == 0 and not first:
                            residual(2 * cp)
                        if q == 3 and j == 2:
                            residual(2 * cp + 1)

            pair_c(0, 0, True)
            pair_c(1, 1, False)
            with dve.Fori(1, D // CW // 2 - 1) as i:
                pair_c(2 * i, 0, False)
                pair_c(2 * i + 1, 1, False)
            pair_c(D // CW - 2, 0, False)
            pair_c(D // CW - 1, 1, False, last=True)
            residual(KT)
            dve.wait_ge(c_ssq, 4 * KT)
            dve.wait_ge(fnw_loaded, 16)
            dve.tensor_reduce(fin[:, 0, :], ssp[:, :, :], AX_X, ALU.add).then_inc(fin_sum, 1)
            dve.wait_ge(fin_sqrt, 1)
            dve.reciprocal(fin[:, 2, :], fin[:, 1, :]).then_inc(fin_rstd, 1)
            dve.wait_ge(fin_rstd, 1)
            for n in range(4):
                if n >= 2:
                    dve.wait_ge(fin_sqrt, n)
                for hf in range(2):
                    part = slice(hf * 1024, (hf + 1) * 1024)
                    if n < 2:
                        dve.scalar_tensor_tensor(res[:, n, part], res[:, n, part], fin[:, 2, n:n + 1], fnw[:, part],
                                                 ALU.mult, ALU.mult).then_inc(fin_done, 1)
                    else:
                        tt(res[:, n, part], res[:, n, part], fnw[:, part], ALU.mult).then_inc(fin_done, 1)

        @block.gpsimd
        def _(pool):
            def mix_load(g):
                need(pool, mix_mm, g)
                pool.dma_start(mixcur[:, :, :], pool_mix[0, bass.ds(g, 1), :, :].rearrange("g (c p) d -> p (g c) d", p=P)
                               ).then_inc(mix_loaded, 16)

            def branch_store(g):
                pool.wait_ge(yp_done, 2 * g + 2)
                pool.dma_start(y_d[bass.ds(g * GD, GD), :].rearrange("(c p) t -> p c t", p=P), yps[:, :, :]).then_inc(yp_stored, 16)

            for i in range(5):
                r, c0 = TILE_ROWS[i], TILE_COL[i]
                for b in range(4):
                    n = 4 * i + b
                    pool.wait_ge(x_hi, n + 1)
                    pool.tensor_tensor(xl[:, 4 * b:4 * b + 4, c0:c0 + r], fst[:, n % 4, :, 0:r],
                                       xh[:, 4 * b:4 * b + 4, c0:c0 + r].bitcast(F32), ALU.subtract).then_inc(x_lo, 1)
                if i == 3:
                    pool.wait_ge(x_sq, 5)
                    pool.memset(wbh[:, :, :].bitcast(F32), 0.0).then_inc(ba_zero, 1)
                    pool.memset(wbl[:, :, :].bitcast(F32), 0.0).then_inc(ba_zero, 1)
            pool.wait_ge(x_tr, 20)
            mix_load(0)
            branch_store(0)
            pool.wait_ge(gsum_row, 1)
            for h in range(2):
                pool.dma_start(g_d[:, h, :, :], grow[0:PAIRS * NCH, h * C:(h + 1) * C]).then_inc(gsum_stored, 16)
            with pool.Fori(1, GROUPS) as g:
                mix_load(g)
                branch_store(g)
            pool.wait_ge(yp_stored, 16 * GROUPS)
            pool.wait_ge(proj_evac, 4 * GROUPS)
            pool.memset(xin[:, 0:TAPS - 1], 0.0).then_inc(zeroed, 1)
            pool.memset(kq[:, :, 0, :, 0:PAD], 0.0).then_inc(zeroed, 1)
            pool.memset(vch[:, 0, :, 0:PAD], 0.0).then_inc(zeroed, 1)

            pool.dma_start(lvm[:, :, :, :], consts[:, CLEV:NCOLS].rearrange("p (l h c) -> p l h c", l=LEVELS, h=2)).then_inc(masks_loaded, 16)

            def row_load(d):
                for h in range(2):
                    src = g_d[bass.ds(d, 1), h, :, :].rearrange("a n c -> a (n c)").broadcast_to([64, NCH * C])
                    pool.dma_start(tm[64 * h:64 * h + 64, :, :].rearrange("p n c -> p (n c)"), src).then_inc(rowg_loaded, 16)

            pool.wait_ge(gsum_stored, 32)
            pool.sem_inc(work_free, 1)
            with pool.Fori(0, PAIRS) as d:
                row_load(d)
                pool.wait_ge(cur_ready, d + 1)
                pool.wait_ge(rowg_loaded, 32 * d + 32)
                pool.tensor_tensor(dec[:, :, :, :], tm.unsqueeze(2).broadcast_to([P, NCH, 2, C]),
                                   bc(cur[:, GCUM, :], 2 * C).rearrange("p n (h c) -> p n h c", h=2), ALU.subtract).then_inc(dec_diff, 1)
                pool.wait_ge(decay_exp, d + 1)
                pool.tensor_tensor(tm[:, :, :], dec[:, :, 0, :], dec[:, :, 1, :], ALU.add).then_inc(dec_packed, 1)
                pool.wait_ge(dec_packed, d + 1)
                pool.tensor_tensor(pw, tm[:, :, :], cst[:, CPAIR:CPAIR + C].unsqueeze(1).broadcast_to([P, NCH, C]), ALU.mult).then_inc(pair_dec, 1)
                pool.wait_ge(pair_dec, d + 1)
                pool.wait_ge(qd_pair, d + 1)
                pool.tensor_tensor(pw, pw, bc(qd[:, 2, :], C), ALU.mult).then_inc(pair_fac, 1)
                for lv in range(LEVELS):
                    for g in (0, 2):
                        chunks = group(g, lv)
                        n = chunks.stop - chunks.start
                        pool.wait_ge(s_ready, d * (NG * LEVELS) + NG * lv + g + 1)
                        pool.tensor_tensor(sq[:, chunks, :, :], st[:, chunks, :].unsqueeze(2).broadcast_to([P, n, 2, C]),
                                           cst[:, CHALF:CHALF + 2].unsqueeze(1).unsqueeze(3).broadcast_to([P, n, 2, C]),
                                           ALU.mult).then_inc(sq_pool, 1)
                pool.wait_ge(y_ready, 4 * d + 4)
                pool.dma_start(y_d[bass.ds(PW + CW * d, CW), :].rearrange("(h e) t -> e h t", e=P), sz[:, :, :]).then_inc(y_stored, 16)
                pool.wait_ge(y_stored, 16 * d + 16)
                pool.sem_inc(work_free, 1)

            def gate_load(jp, c, first):
                if first:
                    pool.wait_ge(y_lo, 24)
                    pool.wait_ge(gate_stored[0], 16 * NGATE)
                    pool.wait_ge(gate_stored[1], 16 * NGATE)
                else:
                    pool.wait_ge(mg_done, 2 * jp + c - 1)
                for i in range(2):
                    pool.dma_start(gst[:, c, i, :], gates_d[bass.ds(jp * CW + c * P + i * D, P), :]).then_inc(gate_loaded[c], 16)

            for c in range(2):
                gate_load(0, c, True)
            with pool.Fori(1, D // CW) as jp:
                for c in range(2):
                    gate_load(jp, c, False)


_INS = ["x", "meta_tokens", "norm_w", "w_in", "conv_w", "A_log", "dt_bias", "pool_mix", "pool_scale", "dn_norm_w",
        "w_pool_out", "w_dn_out", "w_o", "final_norm_w"]


def kernel(**inputs):
    import numpy as np
    import concourse.bacc as bacc
    from concourse.bass_utils import run_bass_kernel_spmd

    nc = bacc.Bacc("TRN2", target_bir_lowering=False, num_devices=1)
    arrays = {f"in_{n}": np.ascontiguousarray(inputs[n]) for n in _INS}
    arrays["in_consts"] = constants()
    args = [nc.dram_tensor(n, a.shape, mybir.dt.from_np(a.dtype), kind="ExternalInput").ap() for n, a in arrays.items()]
    out = nc.dram_tensor("out", (1, SEQ, D), F32, kind="ExternalOutput").ap()
    build(nc, *args, out)
    return run_bass_kernel_spmd(nc, [arrays], core_ids=[0]).results[0]["out"]
```

```python
from contextlib import ExitStack

import concourse.bass as bass
from concourse import mybir

F32 = mybir.dt.float32
F32R = mybir.dt.float32r
ALU = mybir.AluOpType
ACT = mybir.ActivationFunctionType
AX_X = mybir.AxisListType.X

P = 128
D = 2048
SEQ = 512
META = 16
T = SEQ + META
HALF = T // 2
QHALF = (SEQ + 4) // 2
KT = D // P
PW = 1024
GROUPS = 4
GD = PW // GROUPS
WINDOWS = (2, 4, 8, 16)
HEADS = 16
PAIRS = HEADS // 2
HD = 128
DNW = HEADS * HD
TAPS = 4
C = 64
PAD = C - META
NCH = (T + PAD) // C
LEVELS = 6
SHORT = 4
GC = 3
NG = NCH // GC
EPS = 1e-6
NEG = -3.0e4

COL_U, COL_ZP = 0, PW
COL_Q, COL_K, COL_V, COL_Z = 2 * PW, 2 * PW + DNW, 2 * PW + 2 * DNW, 2 * PW + 3 * DNW
COL_BA = 2 * PW + 4 * DNW
COL_GATE = COL_BA + 2 * HEADS
CW = 256
UK = 8
CP_PAIR0 = 2 * GROUPS
CP_GATE0 = CP_PAIR0 + 4 * PAIRS
NGATE = 2 * D // CW
NCP = CP_GATE0 + NGATE

CI, CI2 = 0, 128
CUP = 192
CHALF = 256
CPAIR = 258
CEPS = 322
NCONST = CEPS + 1
CU, CONES, CHA, CHB = (NCONST + P * i for i in range(4))
CLEV = CHB + P
NCOLS = CLEV + C * LEVELS
NTILE_CONV = 3 * HEADS
ROW_NORM, ROW_PS, ROW_DN = 2 * NTILE_CONV, 2 * NTILE_CONV + KT, 2 * NTILE_CONV + KT + PW // P
NROW_A, NROW_B = ROW_DN + 1, 2 * NTILE_CONV
BETA, GCUM, NEG_EG, EG, EDEC, GLA, GLB = range(7)
NKIND = 7


def constants():
    import numpy as np

    c = np.zeros((P, NCOLS), np.float32)
    c[:, CI:CI + P] = np.eye(P)
    s = np.arange(P) % C
    half = np.arange(P) // C
    col = np.arange(C)
    c[:, CI2:CI2 + C] = s[:, None] == col[None]
    c[:, CUP:CUP + C] = np.where(s[:, None] <= col[None], 0.0, NEG)
    c[:, CPAIR:CPAIR + C] = (s[:, None] % 2 == 0) & (col[None] == s[:, None] + 1)
    for h in range(2):
        c[:, CHALF + h] = half == h
    for lv in range(LEVELS):
        a, b = s[:, None] >> lv, col[None] >> lv
        c[:, CLEV + C * lv:CLEV + C * (lv + 1)] = (b % 2 == 0) & (a == b + 1)
    same = half[:, None] == half[None]
    c[:, CU:CU + P] = same & (s[:, None] <= s[None])
    c[:, CONES:CONES + P] = same
    c[:, CHA:CHA + P] = (half == 0)[:, None]
    c[:, CHB:CHB + P] = (half == 1)[:, None]
    c[:, CEPS] = EPS
    return c


def need(engine, semaphore, value):
    if isinstance(value, int) and value < 1:
        return
    engine.wait_ge(semaphore, value)


def build(nc, x, meta_tokens, norm_w, w_in, conv_w, A_log, dt_bias, pool_mix, pool_scale, dn_norm_w,
          w_pool_out, w_dn_out, w_o, final_norm_w, consts, out):
    gates_d = nc.dram_tensor("gates_scratch", (2 * D, SEQ), F32, kind="Internal").ap()
    y_d = nc.dram_tensor("branch_scratch", (PW + DNW, SEQ), F32, kind="Internal").ap()
    g_d = nc.dram_tensor("gate_sum_scratch", (PAIRS, 2, NCH, C), F32, kind="Internal").ap()

    outer = ExitStack()
    with outer:
        def tensors(stack):
            def sb(name, shape, dt=F32):
                return stack.enter_context(nc.sbuf_tensor(name, shape, dt))
            return sb

        def sem(name):
            return outer.enter_context(nc.semaphore(name))

        sb = tensors(outer)
        cst = sb("cst", [P, NCONST])
        vcol = sb("vcol", [P, NROW_A - ROW_NORM])
        convc = sb("convc", [P, TAPS, 3, HEADS])
        table = sb("table", [P, PAIRS, NKIND, NCH])
        ident = cst[:, CI:CI + P]
        eps = cst[:, CEPS:CEPS + 1]
        normw = vcol[:, 0:KT]
        pscale = vcol[:, KT:KT + PW // P]
        dnw = vcol[:, KT + PW // P:KT + PW // P + 1]

        WORK = 24 * SEQ + 3 * UK * CW + 320

        class Layout:

            def __init__(self):
                self.stack, self.at = ExitStack(), 0

            def tensor(self, name, shape, dt=F32):
                n = 1
                for k in shape:
                    n *= k
                self.at += -(-n // 8) * 8
                return self.stack.enter_context(nc.sbuf_tensor(name, [P] + list(shape), dt))

            def skip_to(self, column):
                assert column >= self.at, (column, self.at)
                if column > self.at:
                    self.tensor(f"skip{self.stack_id}_{self.at}", [column - self.at])

            def close(self):
                self.stack.close()

        def layout(number):
            made = Layout()
            made.stack_id = number
            return made

        lay = layout(0)
        kq = lay.tensor("kq", [2, NCH, 2, C])
        vch = lay.tensor("vch", [NCH, 2, C])
        sz = lay.tensor("sz", [2, SEQ])
        dec = lay.tensor("dec", [NCH, C])
        xm = lay.tensor("xm", [NCH, C])
        mq = lay.tensor("mq", [NCH, 2, C])
        st = lay.tensor("st", [NCH, C])
        tm = lay.tensor("tm", [NCH, C])
        sq = lay.tensor("sq", [NCH, 2, C])
        ktok = lay.tensor("ktok", [NCH, HD])
        oo = lay.tensor("oo", [NCH - 1, HD])
        gates_at = lay.at
        stg = lay.tensor("stg", [3, 2, T])
        vtok = lay.tensor("vtok", [NCH, HD])
        pw, px = (vtok[:, :, i * C:(i + 1) * C] for i in range(2))
        xin = lay.tensor("xin", [TAPS - 1 + T])
        zst = lay.tensor("zst", [2, SEQ])
        convcur = lay.tensor("convcur", [TAPS, 3, 2])
        cur = lay.tensor("cur", [NKIND, NCH])
        state = lay.tensor("state", [2, HD])
        rr = lay.tensor("rr", [HD])
        vn = lay.tensor("vn", [HD])
        junk = lay.tensor("junk", [HD])
        norms = lay.tensor("norms", [2, NCH])
        rk = lay.tensor("rk", [2, NCH])
        qd = lay.tensor("qd", [3, NCH])
        lvm = lay.tensor("lvm", [LEVELS, C])
        oss = lay.tensor("oss", [4, NCH - 1])
        lay.skip_to(WORK)
        raw = lay.tensor("raw", [4, UK, CW])
        xh = lay.tensor("xh", [KT, T], F32R)
        xl = lay.tensor("xl", [KT, T], F32R)
        wh = lay.tensor("wh", [4, UK, P], F32R)
        wl = lay.tensor("wl", [4, UK, P], F32R)
        lay.close()
        assert gates_at == 22 * SEQ
        gates_sb = [stg[:, 0, :, :].rearrange("p a t -> p (a t)")[:, i * SEQ:(i + 1) * SEQ] for i in range(2)]

        lay = layout(1)
        prow = lay.tensor("prow", [2, P])
        al = lay.tensor("al", [2, HEADS])
        wba = lay.tensor("wba", [KT, 2 * HEADS])
        sums = lay.tensor("sums", [4, P])
        at_xt = lay.at
        xt = lay.tensor("xt", [5, D])
        fst = lay.tensor("fst", [4, 4, P])
        stat = lay.tensor("stat", [3, 5])
        at_square = lay.at
        xsquare = lay.tensor("xsquare", [D])
        lay.close()
        lay = layout(2)
        lay.skip_to(at_xt)
        ba = lay.tensor("ba", [NCH * C])
        ba2 = lay.tensor("ba2", [NCH, 2, C])
        tb = lay.tensor("tb", [2, PAIRS, NCH])
        tq = lay.tensor("tq", [8, PAIRS, NCH])
        grow = lay.tensor("grow", [P])
        mixcur = lay.tensor("mixcur", [2, GD])
        ub = lay.tensor("ub", [2, T])
        pa = lay.tensor("pa", [2, T])
        pooled = lay.tensor("pooled", [2, SEQ])
        szp = lay.tensor("szp", [2, SEQ])
        yps = lay.tensor("yps", [2, SEQ])
        lay.skip_to(at_square)
        wbh = lay.tensor("wbh", [KT, P], F32R)
        wbl = lay.tensor("wbl", [KT, P], F32R)
        assert lay.at <= WORK
        lay.close()

        lay = layout(3)
        yraw = lay.tensor("yraw", [24, SEQ])
        rawb = lay.tensor("rawb", [3, UK, CW])
        lay.skip_to(WORK)
        yh = lay.tensor("yh", [24, SEQ], F32R)
        mh0 = lay.tensor("mh0", [UK, SEQ], F32R)
        merged = lay.tensor("merged", [KT, SEQ])
        ot = lay.tensor("ot", [SEQ])
        lay.tensor("bwh", [3, UK, P], F32R)
        gst0 = lay.tensor("gst0", [2, SEQ])
        lay.tensor("bwl", [3, UK, P], F32R)
        gst1 = lay.tensor("gst1", [2, SEQ])
        lay.close()
        gst = [gst0, gst1]
        lay = layout(4)
        yl = lay.tensor("yl", [24, SEQ], F32R)
        lay.skip_to(WORK + (24 + UK) * SEQ)
        ml = lay.tensor("ml", [KT, SEQ], F32R)
        lay.close()
        lay = layout(5)
        xres = lay.tensor("xres", [4, D])
        fnw = lay.tensor("fnw", [D])
        rawc3 = lay.tensor("rawc3", [UK, CW])
        lay.skip_to(WORK)
        mh1 = lay.tensor("mh1", [KT - UK, SEQ], F32R)
        res = lay.tensor("res", [4, D])
        lay.close()
        bwh, bwl, cwh, cwl = wh, wl, wh, wl
        rawc = [rawb[:, 0], rawb[:, 1], rawb[:, 2], rawc3[:, :, :]]
        spare = table[:, :, :, :].rearrange("p a k n -> p (a k n)")
        ssp = spare[:, 0:4 * KT].rearrange("p (n k) -> p n k", n=4)
        fin = spare[:, 4 * KT:4 * KT + 12].rearrange("p (a n) -> p a n", a=3)

        pj = [outer.enter_context(nc.psum_tensor(f"pj{i}", [P, 2, 512], F32)) for i in range(2)]
        pg = [outer.enter_context(nc.psum_tensor(f"pg{i}", [P, 512], F32)) for i in range(NG)]
        pt = outer.enter_context(nc.psum_tensor("pt", [P, 512], F32))
        banks = [pj[0][:, 0, :], pj[0][:, 1, :], pj[1][:, 0, :], pj[1][:, 1, :]]

        cst_loaded, par_loaded, ba_loaded = sem("cst_loaded"), sem("par_loaded"), sem("ba_loaded")
        mix_loaded = sem("mix_loaded")
        xt_loaded = [sem(f"xt_loaded{i}") for i in range(5)]
        raw_loaded = [sem(f"raw_loaded{i}") for i in range(4)]
        rawb_loaded = [sem(f"rawb_loaded{i}") for i in range(3)]
        rawc_loaded = [sem(f"rawc_loaded{i}") for i in range(4)]
        par_tr, par_cols = sem("par_tr"), sem("par_cols")
        x_sq, x_rms, x_rstd, x_scaled = sem("x_sq"), sem("x_rms"), sem("x_rstd"), sem("x_scaled")
        x_tr, x_f, x_hi, x_lo, x_lo3 = sem("x_tr"), sem("x_f"), sem("x_hi"), sem("x_lo"), sem("x_lo3")
        ba_zero, ba_hi, ba_lo, ba_mm, ba_row = sem("ba_zero"), sem("ba_hi"), sem("ba_lo"), sem("ba_mm"), sem("ba_row")
        ba_tr = sem("ba_tr")
        tab_act, tab_dve, tab_mid, tab_mm = sem("tab_act"), sem("tab_dve"), sem("tab_mid"), sem("tab_mm")
        zeroed = sem("zeroed")
        hi_done, lo_done, pe_piece, proj_evac = sem("hi_done"), sem("lo_done"), sem("pe_piece"), sem("proj_evac")
        pool_add, pool_step, mix_mm, yp_done, yp_stored = sem("pool_add"), sem("pool_step"), sem("mix_mm"), sem("yp_done"), sem("yp_stored")
        conv_cur, conv_step = sem("conv_cur"), sem("conv_step")
        gate_stored = [sem("gate_stored0"), sem("gate_stored1")]
        silu_done, cur_ready = sem("silu_done"), sem("cur_ready")
        gsum_tr, gsum_row, gsum_stored, rowg_loaded = sem("gsum_tr"), sem("gsum_row"), sem("gsum_stored"), sem("rowg_loaded")
        masks_loaded = sem("masks_loaded")
        dec_diff, dec_arg, decay_exp = sem("dec_diff"), sem("dec_arg"), sem("decay_exp")
        gram_mm, gram_diag, norm_sum, norm_sqrt = sem("gram_mm"), sem("gram_diag"), sem("norm_sum"), sem("norm_sqrt")
        rk_ready, qd_ready, s_init, mq_ready = sem("rk_ready"), sem("qd_ready"), sem("s_init"), sem("mq_ready")
        qd_shift, qd_pair, pair_dec, pair_fac, pair_x = sem("qd_shift"), sem("qd_pair"), sem("pair_dec"), sem("pair_fac"), sem("pair_x")
        tok_tr, tok_done = sem("tok_tr"), sem("tok_done")
        x_mm, x_ready, y_mm, s_ready = sem("x_mm"), sem("x_ready"), sem("y_mm"), sem("s_ready")
        t_tr, t_ready = sem("t_tr"), sem("t_ready")
        sq_ready = sem("sq_ready")
        ks_mm, qs_mm, r_ready, tr_mm, vn_ready = sem("ks_mm"), sem("qs_mm"), sem("r_ready"), sem("tr_mm"), sem("vn_ready")
        st_mm, st_upd, qkv_mm, o_inter, o_ready = sem("st_mm"), sem("st_upd"), sem("qkv_mm"), sem("o_inter"), sem("o_ready")
        o_ssq, o_var, o_sqrt, o_rstd, o_fac = sem("o_ssq"), sem("o_var"), sem("o_sqrt"), sem("o_rstd"), sem("o_fac")
        o_scaled, o_tr, y_ready, y_stored = sem("o_scaled"), sem("o_tr"), sem("y_ready"), sem("y_stored")
        work_free = sem("work_free")
        pe_gate = sem("pe_gate")
        yraw_tail, yraw_loaded, y_hi, y_lo = sem("yraw_tail"), sem("yraw_loaded"), sem("y_hi"), sem("y_lo")
        hib, lob, peb = sem("hib"), sem("lob"), sem("peb")
        gate_loaded = [sem("gate_loaded0"), sem("gate_loaded1")]
        mg_step, mg_done = sem("mg_step"), sem("mg_done")
        m_hi, m_lo = sem("m_hi"), sem("m_lo")
        hic, loc, pec, c_evac, c_tr, res_done = sem("hic"), sem("loc"), sem("pec"), sem("c_evac"), sem("c_tr"), sem("res_done")
        xres_loaded, xrest_loaded, fnw_loaded, c_ssq = sem("xres_loaded"), sem("xrest_loaded"), sem("fnw_loaded"), sem("c_ssq")
        weighed, fin_last = sem("weighed"), sem("fin_last")
        fin_sum, fin_sqrt, fin_rstd, fin_done, out_stored = (
            sem("fin_sum"), sem("fin_sqrt"), sem("fin_rstd"), sem("fin_done"), sem("out_stored"))

        TILE_ROWS = [META] + [P] * 4
        TILE_COL = [0] + [META + P * i for i in range(4)]

        def chunk(t, n):
            return t[:, n * C:(n + 1) * C]

        def bc(ap, n):
            return ap.unsqueeze(2).broadcast_to([ap.shape[0], ap.shape[1], n])

        HALVES = [slice(0, 64), slice(64, 128)]
        QUARTERS = [(slice(64 * h, 64 * h + 32), slice(64 * h + 32, 64 * h + 64)) for h in range(2)]

        def group(g, lv=0):
            return slice(GC * g + (1 if g == 0 and lv >= SHORT else 0), GC * (g + 1))

        G0 = 3
        F0 = G0 + GC
        L0 = F0 + 7
        TOK_ROUNDS = {G0: [("k", n) for n in range(0, 4)], G0 + 1: [("k", n) for n in range(4, 8)], G0 + 2: [("k", 8)]}
        for i in range(3):
            TOK_ROUNDS[L0 + 3 * i] = [("v", n) for n in range(3 * i, 3 * i + 3)]
            TOK_ROUNDS[L0 + 9 + 3 * i] = [("q", n) for n in range(3 * i + 1, min(3 * i + 4, NCH))]
        TOK_STEPS = sorted(TOK_ROUNDS)
        K_TOK, V_TOK, ALL_TOK = NCH, 2 * NCH, 3 * NCH - 1

        def tok_before(m):
            return sum(len(TOK_ROUNDS[i]) for i in TOK_STEPS if i < m)

        def level_step(m):
            return ((m - L0 + 2) // 3, (m - L0 + 2) % 3) if L0 <= m < R0 else (None, None)

        R0 = L0 + 3 * LEVELS - 3
        O0 = R0 + 3 * NCH

        block = outer.enter_context(nc.Block())

        @block.sync
        def _(sp):
            sp.dma_start(cst[:, :], consts[:, 0:NCONST]).then_inc(cst_loaded, 16)
            for i in range(5):
                src = meta_tokens if i == 0 else x[0, (i - 1) * P:i * P, :]
                sp.dma_start(xt[0:TILE_ROWS[i], i, :], src).then_inc(xt_loaded[i], 16)
                if i == 1:
                    cv = conv_w[0].rearrange("t (n c) -> t n c", c=P)
                    n = NTILE_CONV
                    sp.dma_start(prow[0:n, 0, :], cv[0]).then_inc(par_loaded, 16)
                    sp.dma_start(prow[n:2 * n, 0, :], cv[1]).then_inc(par_loaded, 16)
                    sp.dma_start(prow[0:n, 1, :], cv[2]).then_inc(par_loaded, 16)
                    sp.dma_start(prow[n:2 * n, 1, :], cv[3]).then_inc(par_loaded, 16)
                    sp.dma_start(prow[ROW_NORM:ROW_PS, 0, :], norm_w[0].rearrange("(k p) -> k p", p=P)).then_inc(par_loaded, 16)
                    sp.dma_start(prow[ROW_PS:ROW_DN, 0, :], pool_scale[0].rearrange("(k p) -> k p", p=P)).then_inc(par_loaded, 16)
                    sp.dma_start(prow[ROW_DN:ROW_DN + 1, 0, :], dn_norm_w).then_inc(par_loaded, 16)
            sp.dma_start(wba[:, :, :], w_in[0, :, COL_BA:COL_GATE].rearrange("(k p) c -> p k c", p=P)).then_inc(ba_loaded, 16)
            sp.dma_start(sums[:, :, :], consts[:, CU:CU + 4 * P].rearrange("p (i c) -> p i c", i=4)).then_inc(ba_loaded, 16)
            sp.dma_start(al[:, 0, :], A_log.broadcast_to([P, HEADS])).then_inc(ba_loaded, 16)
            sp.dma_start(al[:, 1, :], dt_bias.broadcast_to([P, HEADS])).then_inc(ba_loaded, 16)

            def load_cp(cp, par, col):
                for h in range(2):
                    need(sp, lo_done, 16 * cp + 4 * h - 20)
                    sp.dma_start(raw[:, 2 * par + h, :, :],
                                 w_in[0, h * UK * P:(h + 1) * UK * P, bass.ds(col, CW)].rearrange("(k p) c -> p k c", p=P)
                                 ).then_inc(raw_loaded[2 * par + h], 16)

            load_cp(0, 0, COL_U)
            load_cp(1, 1, COL_ZP)
            with sp.Fori(1, GROUPS) as g:
                load_cp(2 * g, 0, COL_U + g * CW)
                load_cp(2 * g + 1, 1, COL_ZP + g * CW)
            with sp.Fori(0, PAIRS) as p:
                for k, col in enumerate((COL_K, COL_Q, COL_V, COL_Z)):
                    load_cp(CP_PAIR0 + 4 * p + k, k % 2, col + p * CW)
            with sp.Fori(0, NGATE // 2) as i:
                load_cp(CP_GATE0 + 2 * i, 0, COL_GATE + i * (2 * CW))
                load_cp(CP_GATE0 + 2 * i + 1, 1, COL_GATE + CW + i * (2 * CW))

            sp.wait_ge(y_stored, 16 * PAIRS)
            sp.wait_ge(yp_stored, 16 * GROUPS)
            y_rows = y_d.rearrange("(k p) t -> p k t", p=P)
            sp.dma_start(yraw[:, 0:22, :], y_rows[:, 0:22, :]).then_inc(yraw_loaded, 16)

            def load_b(jp, first):
                for u in range(3):
                    if not first:
                        need(sp, lob, 24 * jp + 4 * u - 8)
                    w = w_pool_out if u == 0 else w_dn_out
                    r = 0 if u < 2 else UK * P
                    sp.dma_start(rawb[:, u, :, :],
                                 w[0, r:r + UK * P, bass.ds(jp * CW, CW)].rearrange("(k p) c -> p k c", p=P)
                                 ).then_inc(rawb_loaded[u], 16)

            load_b(0, True)
            for c in range(2):
                sp.wait_ge(gate_stored[c], 16 * NGATE)
            sp.dma_start(yraw[:, 22:24, :], y_rows[:, 22:24, :]).then_inc(yraw_tail, 16)
            with sp.Fori(1, D // CW) as jp:
                load_b(jp, False)

            def load_c(cp, par, first):
                for h in range(2):
                    slot = 2 * par + h
                    if first:
                        if slot < 3:
                            sp.wait_ge(lob, 24 * (D // CW) + 4 * slot - 8)
                        else:
                            sp.wait_ge(peb, 6 * (D // CW))
                    else:
                        need(sp, loc, 16 * cp + 4 * h - 20)
                    sp.dma_start(rawc[slot],
                                 w_o[0, h * UK * P:(h + 1) * UK * P, bass.ds(cp * CW, CW)].rearrange("(k p) c -> p k c", p=P)
                                 ).then_inc(rawc_loaded[slot], 16)

            load_c(0, 0, True)
            load_c(1, 1, True)
            x_rows = x[0].rearrange("(n p) d -> p n d", p=P)
            sp.dma_start(xres[:, :, 0:CW], x_rows[:, :, 0:CW]).then_inc(xres_loaded, 16)
            sp.dma_start(xres[:, :, CW:D], x_rows[:, :, CW:D]).then_inc(xrest_loaded, 16)
            sp.dma_start(fnw[:, :], final_norm_w.unsqueeze(0).broadcast_to([P, D])).then_inc(fnw_loaded, 16)
            with sp.Fori(1, D // CW // 2) as i:
                load_c(2 * i, 0, False)
                load_c(2 * i + 1, 1, False)
            for n in (0, 3, 1, 2):
                for hf in range(2):
                    if n == 3:
                        sp.wait_ge(fin_last, hf + 1)
                    else:
                        sp.wait_ge(fin_done, 2 * n + hf + 1)
                    sp.dma_start(out[0, n * P:(n + 1) * P, hf * 1024:(hf + 1) * 1024],
                                 res[:, n, hf * 1024:(hf + 1) * 1024]).then_inc(out_stored, 16)
            sp.wait_ge(out_stored, 16 * 8)

        @block.tensor
        def _(pe):
            def product(dst, lhs, rhs, start, stop):
                return pe.matmul(dst, lhs, rhs, start=start, stop=stop)

            def window(cp, c, h, half, hook):
                early = isinstance(cp, int) and cp == 0 and c == 0
                if not early:
                    pe.wait_ge(lo_done, 16 * cp + 8 * c + 4 * h + 4)
                if h == 0:
                    need(pe, proj_evac, 2 * cp + c - 1)
                halves = [(pj[c][:, i, 0:half], T - (2 - i) * half, half) for i in range(2)] if half else \
                    [(pj[c][:, 0, 0:SEQ], META, SEQ)]
                slot = 2 * c + h
                for k in range(UK):
                    kt = h * UK + k
                    if early and k % 2 == 0:
                        pe.wait_ge(lo_done, 4 * h + k // 2 + 1)
                    if early and k % 4 == 0:
                        pe.wait_ge(*((x_lo, 13), (x_lo, 14), (x_lo, 15), (x_lo3, 5))[kt // 4])
                    for w, xx, first, last in ((wh, xh, True, False), (wh, xl, False, False), (wl, xh, False, True)):
                        for dst, c0, n in halves:
                            mm = product(dst, w[:, slot, k, :], xx[:, kt, c0:c0 + n],
                                         first and kt == 0, last and kt == KT - 1)
                    if k == UK - 1:
                        mm.then_inc(pe_piece, 1)
                    if k % 2 == 1:
                        hook(k // 2)

            pe.wait_ge(cst_loaded, 16)
            pe.wait_ge(par_loaded, 16 * 7)
            pe.transpose(pt[:, 0:NROW_A], prow[0:NROW_A, 0, :], cst[0:NROW_A, CI:CI + NROW_A])
            pe.transpose(pt[:, 128:128 + NROW_B], prow[0:NROW_B, 1, :], cst[0:NROW_B, CI:CI + NROW_B]).then_inc(par_tr, 1)
            for i in range(5):
                r = TILE_ROWS[i]
                pe.wait_ge(x_scaled, i + 1)
                for b in range(4):
                    n = 4 * i + b
                    if n >= 4:
                        pe.wait_ge(x_f, n - 3)
                    for k in range(4):
                        kt = 4 * b + k
                        mm = pe.transpose(banks[n % 4][:, k * P:k * P + r], xt[0:r, i, kt * P:(kt + 1) * P],
                                          cst[0:r, CI:CI + r])
                    mm.then_inc(x_tr, 1)

            def no_hook(q):
                return None

            def table_steps(cp, j, q):
                if (cp, j, q) == (0, 1, 3):
                    pe.wait_ge(ba_lo, 2)
                    for kt in range(KT):
                        for w, xx, first, last in ((wbh, xh, True, False), (wbh, xl, False, False), (wbl, xh, False, True)):
                            for i in range(2):
                                mm = product(pg[i][:, 0:HALF], w[:, kt, :], xx[:, kt, i * HALF:(i + 1) * HALF],
                                             first and kt == 0, last and kt == KT - 1)
                    mm.then_inc(ba_mm, 1)
                if (cp, j, q) == (0, 3, 0):
                    pe.wait_ge(ba_row, 4)
                    for n in range(NCH):
                        lhs = ba2[0:48, n, :, :].rearrange("p a c -> p (a c)")
                        mm = pe.transpose(pg[2][:, 48 * n:48 * (n + 1)], lhs, cst[0:48, CI:CI + 48])
                    mm.then_inc(ba_tr, 1)
                if (cp, j, q) == (1, 1, 0):
                    pe.wait_ge(tab_dve, 3)
                    g = tq[:, 5, :, :].rearrange("p a n -> p (a n)")
                    w = PAIRS * NCH
                    pe.wait_ge(ba_loaded, 64)
                    for i in range(4):
                        mm = product(pg[2][:, i * w:(i + 1) * w], sums[:, i, :], g, True, True)
                    mm.then_inc(tab_mm, 1)
                if (cp, j, q) == (1, 2, 0):
                    pe.wait_ge(tab_dve, 5)
                    w = PAIRS * NCH
                    pe.transpose(pg[2][0:w, 0:P], tq[:, 5, :, :].rearrange("p a n -> p (a n)"), ident).then_inc(gsum_tr, 1)

            def pool_windows(g, first):
                for z in range(2):
                    for j in range(4):
                        def hook(q, z=z, j=j):
                            if first:
                                table_steps(z, j, q)
                            if (z, j, q) == (1, 2, 3):
                                pe.wait_ge(mix_loaded, 16 * g + 16)
                                pe.wait_ge(pool_step, 2 * g + 2)
                                need(pe, yp_done, 2 * g)
                                for d in range(2):
                                    for cc in range(2):
                                        mm = product(pg[d][:, 0:SEQ], mixcur[:, cc, d * P:(d + 1) * P],
                                                     pooled[:, cc, :], cc == 0, cc == 1)
                                mm.then_inc(mix_mm, 1)
                        window(2 * g + z, j // 2, j % 2, (HALF, None)[z], hook)

            pool_windows(0, True)
            with pe.Fori(1, GROUPS) as g:
                pool_windows(g, False)

            def delta(d, m):
                def wait(semaphore, per_pair, count):
                    need(pe, semaphore, d * per_pair + count)

                def alone():
                    pe.sem_inc(pe_gate, 1)

                if G0 <= m < G0 + NG:
                    g = m - G0
                    if g == 0:
                        wait(silu_done, 4, 2)
                        wait(cur_ready, 1, 1)
                        pe.wait_ge(yp_done, 2 * GROUPS)
                        pe.wait_ge(tab_dve, 6)
                        alone()
                    for n in range(GC * g, GC * (g + 1)):
                        i = n - GC * g
                        for hd in range(2):
                            ph = slice(64 * hd, 64 * hd + 64)
                            mm = product(pg[g][ph, 128 * i:128 * (i + 1)].rearrange("p (a c) -> p a c", a=2),
                                         kq[:, 0, n, hd, :], kq[:, :, n, hd, :], True, True)
                    mm.then_inc(gram_mm, 1)
                if m in TOK_ROUNDS:
                    if m > TOK_STEPS[0]:
                        wait(tok_done, ALL_TOK, tok_before(m))
                    if TOK_ROUNDS[m][0] == ("v", 0):
                        wait(silu_done, 4, 3)
                        wait(qd_pair, 1, 1)
                    for i, (what, n) in enumerate(TOK_ROUNDS[m]):
                        src = vch[:, n] if what == "v" else kq[:, "kq".index(what), n]
                        mm = pe.transpose(pt[:, i * P:(i + 1) * P], src.rearrange("p h c -> p (h c)"), ident)
                    mm.then_inc(tok_tr, 1)
                if m == F0 + 2:
                    wait(qd_ready, 1, 1)
                    wait(tok_done, ALL_TOK, K_TOK)
                    pe.wait_ge(masks_loaded, 16)
                    alone()
                    for ph in HALVES:
                        mm = product(pt[ph, 0:NCH], lvm[ph, 0, :], qd[ph, 1, :], True, True)
                    mm.then_inc(qd_shift, 1)
                lv, stage = level_step(m)
                if lv is not None:
                    for g in range(NG):
                        chunks = group(g, lv)
                        if stage == 0:
                            wait(t_ready, NG * (LEVELS - 1), NG * (lv - 1) + g + 1)
                            alone()
                        if stage == 1:
                            wait(x_ready, NG * (LEVELS - 1), NG * (lv - 1) + g + 1)
                            alone()
                        if stage == 2:
                            wait(s_ready, NG * LEVELS, NG * lv + g + 1)
                            if lv == 0 and g == 0:
                                wait(mq_ready, NG, NG)
                            alone()
                        for n in range(chunks.start, chunks.stop):
                            i = n - GC * g
                            if stage == 2:
                                mm = pe.transpose(pg[g][0:C, P * i:P * (i + 1)], st[:, n, :], ident)
                                continue
                            if lv == LEVELS - 1:
                                for low, high in QUARTERS:
                                    if stage == 0:
                                        mm = product(pg[g][high, C * i:C * i + 32], mq[low, n, 0, 32:C], tm[low, n, 0:32], True, True)
                                    else:
                                        mm = product(pg[g][low, 224 + C * i:256 + C * i], xm[high, n, 0:32], st[high, n, 32:C], True, True)
                                continue
                            for ph in HALVES:
                                if stage == 0:
                                    mm = product(pg[g][ph, C * i:C * (i + 1)], mq[ph, n, 0, :], tm[ph, n, :], True, True)
                                if stage == 1:
                                    mm = product(pg[g][ph, 192 + C * i:192 + C * (i + 1)], xm[ph, n, :], st[ph, n, :], True, True)
                        mm.then_inc((x_mm, y_mm, t_tr)[stage], 1)
                if R0 <= m < O0:
                    n, stage = (m - R0) // 3, (m - R0) % 3
                    if stage == 0 and n > 0:
                        wait(st_upd, 2 * (NCH - 1), 2 * n)
                        if n == 1:
                            wait(vn_ready, NCH, 1)
                        for hd in range(2):
                            mm = product(pg[0][64 * hd:64 * hd + 64, 0:HD], kq[:, 0, n, hd, :], state[:, hd, :], True, True)
                        mm.then_inc(ks_mm, 1)
                        if n > 1:
                            wait(o_ready, NCH - 1, n - 1)
                        else:
                            wait(tok_done, ALL_TOK, ALL_TOK)
                        for hd in range(2):
                            mm = product(pt[64 * hd:64 * hd + 64, 0:HD], kq[:, 1, n, hd, :], state[:, hd, :], True, True)
                        mm.then_inc(qs_mm, 1)
                    if stage == 1:
                        if n == 0:
                            wait(sq_ready, NG, NG)
                            wait(tok_done, ALL_TOK, V_TOK)
                            rhs = vtok[:, 0, :]
                        else:
                            wait(r_ready, NCH - 1, n)
                            rhs = rr[:, :]
                        mm = product(pg[0][:, 128:128 + HD], sq[:, n, :, :].rearrange("p h c -> p (h c)"), rhs, True, True)
                        mm.then_inc(tr_mm, 1)
                    if stage == 2:
                        wait(vn_ready, NCH, n + 1)
                        if n < NCH - 1:
                            for hd in range(2):
                                ph = slice(64 * hd, 64 * hd + 64)
                                mm = product(pg[1 + hd][:, 0:HD], ktok[ph, n, :], vn[ph, :], True, True)
                            mm.then_inc(st_mm, 1)
                        if n > 0:
                            wait(o_inter, NCH - 1, n)
                            alone()
                            for hd in range(2):
                                ph = slice(64 * hd, 64 * hd + 64)
                                mm = product(pt[ph, 128:128 + HD], mq[ph, n, 1, :], vn[ph, :], True, True)
                            mm.then_inc(qkv_mm, 1)
                for b in range(2):
                    if m == O0 + 4 + 2 * b:
                        wait(o_scaled, 2, b + 1)
                        if b == 0:
                            wait(o_ready, NCH - 1, NCH - 1)
                        for i in range(4):
                            mm = pe.transpose((pt if b == 0 else pg[0])[:, i * P:(i + 1) * P], oo[:, 4 * b + i, :], ident)
                        mm.then_inc(o_tr, 1)

            def pair_windows(p, d):
                for k in range(4):
                    for j in range(4):
                        def hook(q, k=k, j=j):
                            if d is not None:
                                delta(d, 16 * k + 4 * j + q)
                        window(CP_PAIR0 + 4 * p + k, j // 2, j % 2, (HALF, QHALF, HALF, None)[k], hook)

            pair_windows(0, None)
            with pe.Fori(1, PAIRS) as p:
                pair_windows(p, p - 1)
            for k in range(4):
                for j in range(4):
                    window(CP_GATE0 + k, j // 2, j % 2, None, lambda q, k=k, j=j: delta(PAIRS - 1, 16 * k + 4 * j + q))
            with pe.Fori(2, NGATE // 2) as i:
                for k in range(2):
                    for j in range(4):
                        window(CP_GATE0 + 2 * i + k, j // 2, j % 2, None, no_hook)

            def window_b(jp, c, u, first):
                pe.wait_ge(lob, 24 * jp + 12 * c + 4 * u + 4)
                if u == 0:
                    if first:
                        pe.wait_ge(proj_evac, 2 * NCP - 1 + c)
                    else:
                        pe.wait_ge(mg_done, 2 * jp + c - 1)
                dst = pj[c][:, 0 if u == 0 else 1, :]
                for k in range(UK):
                    kt = u * UK + k
                    if first and c == 0:
                        pe.wait_ge(y_lo, kt + 1)
                    for w, yy, one, last in ((bwh, yh, True, False), (bwh, yl, False, False), (bwl, yh, False, True)):
                        mm = product(dst, w[:, u, k, :], yy[:, kt, :], one and k == 0 and u < 2,
                                     last and k == UK - 1 and u != 1)
                mm.then_inc(peb, 1)

            for c in range(2):
                for u in range(3):
                    window_b(0, c, u, True)
            with pe.Fori(1, D // CW) as jp:
                for c in range(2):
                    for u in range(3):
                        window_b(jp, c, u, False)

            mhs = [mh0[:, k, :] for k in range(UK)] + [mh1[:, k, :] for k in range(KT - UK)]
            mls = [ml[:, k, :] for k in range(KT)]

            def back(count):
                pe.wait_ge(c_evac, count)
                need(pe, c_ssq, 4 * (count - 1))
                for n in range(4):
                    mm = pe.transpose(pg[0][:, n * P:(n + 1) * P], ot[:, n * P:(n + 1) * P], ident)
                mm.then_inc(c_tr, 1)

            def window_c(cp, c, h, first):
                pe.wait_ge(loc, 16 * cp + 8 * c + 4 * h + 4)
                if h == 0:
                    if first:
                        pe.wait_ge(mg_done, KT - 1 + c)
                    else:
                        need(pe, c_evac, 2 * cp + c - 1)
                for k in range(UK):
                    kt = h * UK + k
                    if first and c == 0:
                        pe.wait_ge(m_lo, kt + 1)
                    for w, yy, one, last in ((cwh, mhs, True, False), (cwh, mls, False, False), (cwl, mhs, False, True)):
                        mm = product(pj[c][:, 0, :], w[:, 2 * c + h, k, :], yy[kt], one and kt == 0, last and kt == KT - 1)
                mm.then_inc(pec, 1)

            def pair_c(cp, first):
                for j in range(4):
                    window_c(cp, j // 2, j % 2, first)
                    if j == 0 and not first:
                        back(2 * cp)
                    if j == 2:
                        back(2 * cp + 1)

            pair_c(0, True)
            pair_c(1, False)
            with pe.Fori(1, D // CW // 2) as i:
                pair_c(2 * i, False)
                pair_c(2 * i + 1, False)
            back(2 * (D // CW))

        def target(cp, par, j):
            return (cp, par, j + 2) if j < 2 else (cp + 1, 1 - par, j - 2)

        @block.scalar
        def _(act):
            def copy(dst, src):
                return act.activation(dst, src, ACT.Copy)

            def split_hi(cp, par, j, q):
                c, h = j // 2, j % 2
                if q == 0:
                    if c == 0:
                        act.wait_ge(raw_loaded[2 * par + h], 8 * cp + 16 - 8 * par)
                    need(act, pe_piece, 4 * cp + j - 3)
                copy(wh[:, j, 2 * q:2 * q + 2, :],
                     raw[:, 2 * par + h, 2 * q:2 * q + 2, c * P:(c + 1) * P]).then_inc(hi_done, 1)

            def window(cp, par, j, hook, evac, last=False):
                for q in range(4):
                    if not (last and j >= 2):
                        split_hi(*target(cp, par, j), q)
                    hook(q)
                if j % 2 == 1:
                    act.wait_ge(pe_piece, 4 * cp + j + 1)
                    evac(j // 2)

            def x_hi_part(i):
                r, c0 = TILE_ROWS[i], TILE_COL[i]
                for b in range(4):
                    n = 4 * i + b
                    act.wait_ge(x_f, n + 1)
                    copy(xh[:, 4 * b:4 * b + 4, c0:c0 + r], fst[:, n % 4, :, 0:r]).then_inc(x_hi, 1)

            act.wait_ge(cst_loaded, 16)
            for i in range(5):
                r = TILE_ROWS[i]
                act.wait_ge(xt_loaded[i], 16)
                act.activation(xsquare[0:r, :], xt[0:r, i, :], ACT.Square, accum_out=stat[0:r, 0, i:i + 1]).then_inc(x_sq, 1)
                act.wait_ge(x_sq, i + 1)
                act.activation(stat[0:r, 1, i:i + 1], stat[0:r, 0, i:i + 1], ACT.Sqrt, bias=eps[0:r, :], scale=1.0 / D).then_inc(x_rms, 1)
                if i >= 2:
                    x_hi_part(i - 2)
            x_hi_part(3)
            for q in range(4):
                split_hi(0, 0, 0, q)
            x_hi_part(4)
            for q in range(4):
                split_hi(0, 0, 1, q)

            def nothing(q):
                return None

            def table_acts(z, j, q):
                if (z, j, q) == (0, 3, 3):
                    act.wait_ge(tab_dve, 2)
                    act.activation(tq[:, 1], tq[:, 0], ACT.Abs).then_inc(tab_act, 1)
                    act.wait_ge(tab_act, 1)
                    act.activation(tq[:, 2], tq[:, 1], ACT.Exp, scale=-1.0).then_inc(tab_act, 1)
                    act.wait_ge(tab_act, 2)
                    act.activation(tq[:, 3], tq[:, 2], ACT.Ln, bias=1.0).then_inc(tab_act, 1)
                    act.activation(al[:, 0, :], al[:, 0, :], ACT.Exp).then_inc(tab_act, 1)
                    act.activation(table[:, :, BETA, :], tb[:, 0], ACT.Sigmoid).then_inc(tab_act, 1)
                if (z, j, q) == (1, 2, 0):
                    act.wait_ge(tab_dve, 5)
                    act.activation(table[:, :, EG, :], table[:, :, GCUM, :], ACT.Exp).then_inc(tab_act, 1)
                    act.activation(table[:, :, EDEC, :], tq[:, 4], ACT.Exp).then_inc(tab_act, 1)
                    act.activation(table[:, :, GLA, :], tq[:, 6], ACT.Exp).then_inc(tab_act, 1)
                    act.activation(table[:, :, GLB, :], tq[:, 7], ACT.Exp).then_inc(tab_act, 1)

            def pool_windows(g, first):
                for z in range(2):
                    def evac(c, z=z):
                        if z == 0:
                            need(act, pool_step, 2 * g)
                            copy(ub[:, c, :].rearrange("p (a t) -> p a t", a=2), pj[c][:, :, 0:HALF]).then_inc(proj_evac, 1)
                        else:
                            need(act, yp_done, 2 * g)
                            act.activation(szp[:, c, :], pj[c][:, 0, :], ACT.Silu).then_inc(proj_evac, 1)
                    for j in range(4):
                        hook = (lambda q, z=z, j=j: table_acts(z, j, q)) if first else nothing
                        window(2 * g + z, z, j, hook, evac)

            pool_windows(0, True)
            with act.Fori(1, GROUPS) as g:
                pool_windows(g, False)

            def silu_chunks(dst, src):
                act.activation(dst[:, 0, :, PAD:], src[:, :, 0:META], ACT.Silu)
                act.activation(dst[:, 1:NCH].rearrange("p n h c -> p h n c"),
                               src[:, :, META:T].rearrange("p h (n c) -> p h n c", c=C), ACT.Silu).then_inc(silu_done, 1)

            def delta(d, m):
                def wait(semaphore, per_pair, count):
                    need(act, semaphore, d * per_pair + count)

                if m == 0:
                    wait(conv_step, 4 * 6, 4 * 6)
                    for kk in range(2):
                        silu_chunks(kq[:, kk], stg[:, kk])
                if m == 1:
                    silu_chunks(vch, stg[:, 2])
                if m == R0:
                    wait(work_free, 1, 1)
                    act.wait_ge(proj_evac, 2 * CP_PAIR0 + 8 * d + 8)
                    act.activation(sz[:, :, :], zst[:, :, :], ACT.Silu).then_inc(silu_done, 1)
                if m == F0:
                    wait(norm_sum, 1, 1)
                    act.activation(rk[:, 0, :], norms[:, 0, :], ACT.Sqrt, bias=eps).then_inc(norm_sqrt, 1)
                if m == G0 + 1:
                    wait(dec_arg, 1, 1)
                    act.activation(dec[:, :, :], dec[:, :, :], ACT.Exp).then_inc(decay_exp, 1)
                if m in TOK_ROUNDS:
                    if m == TOK_STEPS[0]:
                        wait(cur_ready, 1, 1)
                    if TOK_ROUNDS[m][0] == ("v", 0):
                        wait(norm_sqrt, 1, 1)
                        wait(s_ready, NG * LEVELS, NG)
                    wait(tok_tr, len(TOK_STEPS), TOK_STEPS.index(m) + 1)
                    for i, (what, n) in enumerate(TOK_ROUNDS[m]):
                        src = pt[:, i * P:(i + 1) * P]
                        if what == "k":
                            act.activation(ktok[:, n, :], src, ACT.Copy, scale=cur[:, EDEC, n:n + 1]).then_inc(tok_done, 1)
                        elif what == "v":
                            act.activation(vtok[:, n, :], src, ACT.Copy, scale=rk[:, 0, n:n + 1]).then_inc(tok_done, 1)
                        else:
                            act.activation(src, src, ACT.Square, accum_out=norms[:, 1, n:n + 1]).then_inc(tok_done, 1)
                lv, stage = level_step(m)
                if stage == 2:
                    for g in range(NG):
                        chunks = group(g, lv)
                        wait(t_tr, NG * (LEVELS - 1), NG * lv + g + 1)
                        for hd in range(2):
                            src = pg[g][0:C, 0:GC * P].rearrange("p (n h c) -> p n h c", h=2, c=C)[:, chunks.start - GC * g:, hd, :]
                            ins = copy(tm[HALVES[hd], chunks, :], src)
                        ins.then_inc(t_ready, 1)
                if R0 <= m < O0:
                    n, stage = (m - R0) // 3, (m - R0) % 3
                    if stage == 0 and n > 0:
                        wait(qs_mm, NCH - 1, n)
                        act.activation(oo[:, n - 1, :], pt[:, 0:HD], ACT.Copy, scale=cur[:, EG, n:n + 1]).then_inc(o_inter, 1)
                    if stage == 1:
                        wait(tr_mm, NCH, n + 1)
                        copy(vn[:, :], pg[0][:, 128:128 + HD]).then_inc(vn_ready, 1)
                    if stage == 1 and n > 1:
                        wait(o_ready, NCH - 1, n - 1)
                        act.activation(junk[:, :], oo[:, n - 2, :], ACT.Square, accum_out=oss[:, 0, n - 2:n - 1]).then_inc(o_ssq, 1)
                if m == O0:
                    wait(o_ready, NCH - 1, NCH - 1)
                    act.activation(junk[:, :], oo[:, NCH - 2, :], ACT.Square, accum_out=oss[:, 0, NCH - 2:NCH - 1]).then_inc(o_ssq, 1)
                if m == O0 + 1:
                    wait(o_var, 1, 1)
                    act.activation(oss[:, 2, :], oss[:, 1, :], ACT.Sqrt, bias=eps, scale=1.0 / HD).then_inc(o_sqrt, 1)

            def pair_windows(p, d):
                for k in range(4):
                    def evac(c, k=k):
                        if k < 3:
                            need(act, conv_step, (p * 6 + 2 * k + c) * 4)
                            if k == 0 and c == 0 and isinstance(p, int) and p == 0:
                                act.wait_ge(zeroed, 3)
                            half = QHALF if k == 1 else HALF
                            copy(xin[:, TAPS - 1 + T - 2 * half:].rearrange("p (a t) -> p a t", a=2), pj[c][:, :, 0:half]).then_inc(proj_evac, 1)
                        else:
                            copy(zst[:, c, :], pj[c][:, 0, :]).then_inc(proj_evac, 1)
                    for j in range(4):
                        hook = nothing if d is None else (lambda q, k=k, j=j: delta(d, 16 * k + 4 * j + q))
                        window(CP_PAIR0 + 4 * p + k, k % 2, j, hook, evac)

            pair_windows(0, None)
            with act.Fori(1, PAIRS) as p:
                pair_windows(p, p - 1)

            def gate_evac(i):
                def evac(c):
                    need(act, gate_stored[c], 16 * i)
                    act.activation(gates_sb[c], pj[c][:, 0, :], ACT.Sigmoid).then_inc(proj_evac, 1)
                    act.wait_ge(proj_evac, 2 * CP_GATE0 + 2 * i + c + 1)
                    act.dma_start(gates_d[bass.ds((2 * i + c) * P, P), :], gates_sb[c]).then_inc(gate_stored[c], 16)
                return evac

            for k in range(4):
                for j in range(4):
                    window(CP_GATE0 + k, k % 2, j, lambda q, k=k, j=j: delta(PAIRS - 1, 16 * k + 4 * j + q), gate_evac(k))
            with act.Fori(2, NGATE // 2 - 1) as i:
                for k in range(2):
                    for j in range(4):
                        window(CP_GATE0 + 2 * i + k, k, j, nothing, gate_evac(2 * i + k))
            def split_b(jp, j, q):
                c, u = j // 3, j % 3
                if q == 0:
                    if c == 0:
                        act.wait_ge(rawb_loaded[u], 16 * jp + 16)
                    if isinstance(jp, int) and jp == 0 and j < 3:
                        act.wait_ge(pe_piece, 4 * NCP - 3 + j)
                    else:
                        need(act, peb, 6 * jp + j - 2)
                copy(bwh[:, u, 2 * q:2 * q + 2, :], rawb[:, u, 2 * q:2 * q + 2, c * P:(c + 1) * P]).then_inc(hib, 1)

            def y_hi_part(k):
                copy(yh[:, k, :], yraw[:, k, :]).then_inc(y_hi, 1)

            def into_b(j, q):
                if (j, q) == (0, 0):
                    act.wait_ge(yraw_loaded, 16)
                    act.wait_ge(lo_done, 16 * (NCP - 1))
                if (j, q) == (2, 0):
                    act.wait_ge(lo_done, 16 * NCP)
                if j >= 2:
                    split_b(0, j - 2, q)
                y_hi_part(4 * j + q)

            for j in range(4):
                window(NCP - 2, 0, j, nothing, gate_evac(NGATE - 2))
            for j in range(4):
                window(NCP - 1, 1, j, lambda q, j=j: into_b(j, q), gate_evac(NGATE - 1), last=True)

            def mh_tile(k):
                return mh0[:, k, :] if k < UK else mh1[:, k - UK, :]

            def split_c(cp, par, j, q):
                c, h = j // 2, j % 2
                if q == 0:
                    if c == 0:
                        act.wait_ge(rawc_loaded[2 * par + h], 8 * cp + 16 - 8 * par)
                    if isinstance(cp, int) and cp == 0:
                        if j < 3:
                            act.wait_ge(peb, 6 * (D // CW) - 2 + j)
                        else:
                            act.wait_ge(mg_done, KT)
                    else:
                        need(act, pec, 4 * cp + j - 3)
                copy(cwh[:, j, 2 * q:2 * q + 2, :], rawc[2 * par + h][:, 2 * q:2 * q + 2, c * P:(c + 1) * P]).then_inc(hic, 1)

            def m_hi_part(k):
                act.wait_ge(mg_done, k + 1)
                if isinstance(k, int):
                    copy(mh_tile(k), merged[:, k, :]).then_inc(m_hi, 1)
                else:
                    copy(mh0[:, bass.ds(k, 1), :], merged[:, bass.ds(k, 1), :]).then_inc(m_hi, 1)

            def window_b(jp, j, mode):
                for q in range(4):
                    if j < 4:
                        split_b(jp, j + 2, q)
                    elif mode != "last":
                        split_b(jp + 1, j - 4, q)
                    else:
                        split_c(0, 0, j - 4, q)
                        if j == 4:
                            m_hi_part(UK + q)
                        elif q < 3:
                            m_hi_part(UK + 4 + q)
                    if mode == "first" and j < 2:
                        if (j, q) == (0, 0):
                            act.wait_ge(pe_piece, 4 * NCP)
                        if (j, q) == (1, 2):
                            act.wait_ge(yraw_tail, 16)
                        y_hi_part(16 + 4 * j + q)
                if mode in ("low", "turn") and j == 1:
                    m_hi_part(2 * jp - 1)
                if mode in ("first", "low") and j == 4:
                    m_hi_part(2 * jp)

            for j in range(6):
                window_b(0, j, "first")
            with act.Fori(1, UK // 2) as jp:
                for j in range(6):
                    window_b(jp, j, "low")
            for j in range(6):
                window_b(UK // 2, j, "turn")
            with act.Fori(UK // 2 + 1, D // CW - 1) as jp:
                for j in range(6):
                    window_b(jp, j, "high")
            for j in range(6):
                window_b(D // CW - 1, j, "last")
            m_hi_part(KT - 1)

            def squares(count):
                act.wait_ge(res_done, count)
                need(act, c_ssq, 4 * (count - 1))
                for n in range(4):
                    col = (count - 1) * P
                    act.activation(pt[:, n * P:(n + 1) * P], res[:, n, bass.ds(col, P)], ACT.Square,
                                   accum_out=ssp[:, n, bass.ds(count - 1, 1)]).then_inc(c_ssq, 1)

            def pair_c(cp, par, first, last=False):
                for j in range(4):
                    for q in range(4):
                        if not (last and j >= 2):
                            split_c(*target(cp, par, j), q)
                        if q == 3 and j == 0 and not first:
                            squares(2 * cp)
                        if q == 3 and j == 2:
                            squares(2 * cp + 1)
                    if j % 2 == 1:
                        act.wait_ge(pec, 4 * cp + j + 1)
                        need(act, c_tr, 2 * cp + j // 2)
                        copy(ot[:, :], pj[j // 2][:, 0, :]).then_inc(c_evac, 1)

            pair_c(0, 0, True)
            pair_c(1, 1, False)
            with act.Fori(1, D // CW // 2 - 1) as i:
                pair_c(2 * i, 0, False)
                pair_c(2 * i + 1, 1, False)
            pair_c(D // CW - 2, 0, False)
            pair_c(D // CW - 1, 1, False, last=True)
            act.activation(spare[:, 80:81], eps, ACT.Sqrt)
            squares(KT)
            act.wait_ge(fin_sum, 1)
            act.activation(fin[:, 1, :], fin[:, 0, :], ACT.Sqrt, bias=eps, scale=1.0 / D).then_inc(fin_sqrt, 1)
            act.wait_ge(fin_rstd, 1)
            act.wait_ge(weighed, KT)
            for hf in range(2):
                part = slice(hf * 1024, (hf + 1) * 1024)
                act.activation(res[:, 3, part], res[:, 3, part], ACT.Copy, scale=fin[:, 2, 3:4]).then_inc(fin_last, 1)

        @block.vector
        def _(dve):
            tt = dve.tensor_tensor

            def split_lo(cp, par, j, q):
                c, h = j // 2, j % 2
                dve.wait_ge(hi_done, 16 * cp + 4 * j + q + 1)
                tt(wl[:, j, 2 * q:2 * q + 2, :], raw[:, 2 * par + h, 2 * q:2 * q + 2, c * P:(c + 1) * P],
                   wh[:, j, 2 * q:2 * q + 2, :].bitcast(F32), ALU.subtract).then_inc(lo_done, 1)

            def window(cp, par, j, hook, last=False):
                for q in range(4):
                    if not (last and j >= 2):
                        split_lo(*target(cp, par, j), q)
                    hook(q)

            dve.wait_ge(par_tr, 1)
            dve.tensor_copy(convc[:, 0:2, :, :].rearrange("p a b c -> p (a b c)"), pt[:, 0:2 * NTILE_CONV]).then_inc(par_cols, 1)
            dve.tensor_copy(vcol[:, :], pt[:, ROW_NORM:NROW_A]).then_inc(par_cols, 1)
            dve.tensor_copy(convc[:, 2:4, :, :].rearrange("p a b c -> p (a b c)"), pt[:, 128:128 + NROW_B]).then_inc(par_cols, 1)
            dve.wait_ge(par_cols, 3)

            def x_f_part(i):
                r = TILE_ROWS[i]
                for b in range(4):
                    n = 4 * i + b
                    dve.wait_ge(x_tr, n + 1)
                    if i > 0 and b < 3:
                        dve.wait_ge(x_lo, 3 * i + b - 2)
                    if i > 0 and b == 3:
                        dve.wait_ge(x_lo3, i)
                    tt(fst[:, n % 4, :, 0:r], banks[n % 4].rearrange("p (k t) -> p k t", k=4)[:, :, 0:r],
                       bc(normw[:, 4 * b:4 * b + 4], r), ALU.mult).then_inc(x_f, 1)

            def x_lo_part(i):
                r, c0 = TILE_ROWS[i], TILE_COL[i]
                dve.wait_ge(x_hi, 4 * i + 4)
                tt(xl[:, 12:16, c0:c0 + r], fst[:, 3, :, 0:r], xh[:, 12:16, c0:c0 + r].bitcast(F32), ALU.subtract).then_inc(x_lo3, 1)

            for i in range(5):
                r = TILE_ROWS[i]
                dve.wait_ge(x_rms, i + 1)
                dve.reciprocal(stat[0:r, 2, i:i + 1], stat[0:r, 1, i:i + 1]).then_inc(x_rstd, 1)
                dve.wait_ge(x_rstd, i + 1)
                dve.tensor_scalar(xt[0:r, i, :], xt[0:r, i, :], stat[0:r, 2, i:i + 1], None, ALU.mult).then_inc(x_scaled, 1)
                if i >= 2:
                    x_lo_part(i - 2)
                if i >= 1:
                    x_f_part(i - 1)
            x_lo_part(3)
            x_f_part(4)
            for q in range(4):
                split_lo(0, 0, 0, q)
            x_lo_part(4)
            for q in range(4):
                split_lo(0, 0, 1, q)
            dve.wait_ge(ba_loaded, 64)
            dve.wait_ge(ba_zero, 2)

            def parity(t, e):
                return t[:, :, 32 * e:32 * e + 16].rearrange("p k (b h) -> p k b h", b=2)

            for e in range(2):
                src = wba[:, :, :].rearrange("p k (b h e) -> p k b h e", b=2, e=2)[:, :, :, :, e]
                dve.tensor_copy(parity(wbh, e), src).then_inc(ba_hi, 1)
            dve.wait_ge(ba_hi, 2)
            for e in range(2):
                src = wba[:, :, :].rearrange("p k (b h e) -> p k b h e", b=2, e=2)[:, :, :, :, e]
                tt(parity(wbl, e), src, parity(wbh, e).bitcast(F32), ALU.subtract).then_inc(ba_lo, 1)
            dve.memset(ba[0:48, 0:PAD], 0.0).then_inc(ba_row, 1)

            def table_dves(z, j, q):
                if (z, j, q) == (0, 2, 0):
                    dve.wait_ge(ba_mm, 1)
                    for i in range(2):
                        dve.tensor_copy(ba[0:48, PAD + i * HALF:PAD + (i + 1) * HALF], pg[i][0:48, 0:HALF]).then_inc(ba_row, 1)
                    dve.wait_ge(ba_row, 3)
                    dve.tensor_copy(ba2[0:48], ba[0:48].rearrange("p (n c) -> p n c", c=C).unsqueeze(2).broadcast_to([48, NCH, 2, C])).then_inc(ba_row, 1)
                if (z, j, q) == (0, 3, 0):
                    dve.wait_ge(ba_tr, 1)
                    for e in range(2):
                        ph = slice(64 * e, 64 * e + 64)
                        src = pg[2][ph, 0:48 * NCH].rearrange("p (n r) -> p n r", r=48)[:, :, 32 * e:32 * e + 16]
                        dst = tb[ph, :, :, :].rearrange("p b a n -> p n (b a)")
                        ins = dve.tensor_copy(dst, src)
                    ins.then_inc(tab_dve, 1)
                    dve.wait_ge(tab_dve, 1)
                    for e in range(2):
                        ph = slice(64 * e, 64 * e + 64)
                        dtb = al[ph, 1, :].rearrange("p (h e) -> p h e", e=2)[:, :, e]
                        ins = tt(tq[ph, 0], tb[ph, 1], bc(dtb, NCH), ALU.add)
                    ins.then_inc(tab_dve, 1)
                if (z, j, q) == (1, 0, 0):
                    dve.wait_ge(tab_act, 5)
                    dve.scalar_tensor_tensor(tq[:, 4].rearrange("p a n -> p (a n)"), tq[:, 0].rearrange("p a n -> p (a n)"), 0.0,
                                             tq[:, 3].rearrange("p a n -> p (a n)"), ALU.max, ALU.add).then_inc(tab_mid, 1)
                    dve.wait_ge(tab_mid, 1)
                    for e in range(2):
                        ph = slice(64 * e, 64 * e + 64)
                        ea = al[ph, 0, :].rearrange("p (h e) -> p h e", e=2)[:, :, e]
                        ins = dve.scalar_tensor_tensor(tq[ph, 5], tq[ph, 4], -1.0, bc(ea, NCH), ALU.mult, ALU.mult)
                    ins.then_inc(tab_dve, 1)
                if (z, j, q) == (1, 1, 1):
                    dve.wait_ge(tab_mm, 1)
                    w = PAIRS * NCH
                    sums = pg[2][:, 0:4 * w].rearrange("p (i a n) -> p i a n", i=4, a=PAIRS)
                    dve.tensor_copy(table[:, :, GCUM, :], sums[:, 0]).then_inc(tab_mid, 1)
                    dve.tensor_copy(tq[:, 5], sums[:, 0])
                    dve.tensor_copy(tq[:, 6:8], sums[:, 2:4]).then_inc(tab_dve, 1)
                    dve.wait_ge(tab_mid, 2)
                    tt(tq[:, 4], sums[:, 1], table[:, :, GCUM, :], ALU.subtract).then_inc(tab_dve, 1)
                if (z, j, q) == (1, 2, 3):
                    dve.wait_ge(tab_act, 9)
                    dve.tensor_scalar(table[:, :, NEG_EG, :], table[:, :, EG, :], -1.0, None, ALU.mult).then_inc(tab_dve, 1)
                    dve.wait_ge(gsum_tr, 1)
                    dve.tensor_copy(grow[0:PAIRS * NCH, :], pg[2][0:PAIRS * NCH, 0:P]).then_inc(gsum_row, 1)

            steps = [0]

            def pooling(g, c):
                dve.wait_ge(proj_evac, 4 * g + c + 1)
                need(dve, mix_mm, g)
                need(dve, pool_step, 2 * g + c)
                src, lag, n = ub[:, c, :], 1, 0
                while lag < WINDOWS[g]:
                    if n:
                        dve.wait_ge(pool_add, steps[0])
                    lo = 2 * lag - 1
                    tt(pa[:, n % 2, lo:T], src[:, lo:T], src[:, lo - lag:T - lag], ALU.add).then_inc(pool_add, 1)
                    steps[0] += 1
                    src, lag, n = pa[:, n % 2, :], 2 * lag, n + 1
                dve.wait_ge(pool_add, steps[0])
                dve.scalar_tensor_tensor(pooled[:, c, :], src[:, META:T], 1.0 / WINDOWS[g], ub[:, c, META:T],
                                         ALU.mult, ALU.subtract).then_inc(pool_step, 1)

            for g in range(GROUPS):
                for z in range(2):
                    for j in range(4):
                        def hook(q, z=z, j=j):
                            if g == 0:
                                table_dves(z, j, q)
                            if q == 0 and (z, j) == (0, 2):
                                pooling(g, 0)
                            if q == 0 and (z, j) == (1, 0):
                                pooling(g, 1)
                        window(2 * g + z, z, j, hook)
                dve.wait_ge(mix_mm, g + 1)
                dve.wait_ge(proj_evac, 4 * g + 4)
                need(dve, yp_stored, 16 * g)
                for d in range(2):
                    dve.scalar_tensor_tensor(yps[:, d, :], pg[d][:, :], pscale[:, 2 * g + d:2 * g + d + 1], szp[:, d, :],
                                             ALU.mult, ALU.mult).then_inc(yp_done, 1)

            def convolve(p, k, c, tap):
                n = (p * 6 + 2 * k + c) * 4
                which = (1, 0, 2)[k]
                acc = stg[:, k, c, :]
                src_tap = (3, 0, 1, 2)[tap]
                w = convcur[:, src_tap, which, c:c + 1]
                if tap == 0:
                    dve.wait_ge(proj_evac, 2 * CP_PAIR0 + 8 * p + 2 * k + c + 1)
                    need(dve, silu_done, p * 4 if k == 2 else p * 4 - 2)
                    dve.wait_ge(conv_cur, p + 1)
                    dve.tensor_scalar(acc, xin[:, src_tap:src_tap + T], w, None, ALU.mult).then_inc(conv_step, 1)
                else:
                    dve.wait_ge(conv_step, n + tap)
                    dve.scalar_tensor_tensor(acc, xin[:, src_tap:src_tap + T], w, acc, ALU.mult, ALU.add).then_inc(conv_step, 1)

            def delta(d, m):
                def wait(semaphore, per_pair, count):
                    need(dve, semaphore, d * per_pair + count)

                if m == 0:
                    wait(silu_done, 4, 1)
                    dve.tensor_copy(cur[:, :, :], table[:, bass.ds(d, 1), :, :].rearrange("p a k n -> p (a k) n")).then_inc(cur_ready, 1)
                if G0 <= m < G0 + NG:
                    g = m - G0
                    wait(gram_mm, NG, g + 1)
                    kk = pg[g][:, 0:GC * 2 * C].rearrange("p (n a c) -> p n a c", a=2, c=C)[:, :, 0, :]
                    tt(st[:, group(g), :], kk, cst[:, CI2:CI2 + C].unsqueeze(1).broadcast_to([P, GC, C]), ALU.mult).then_inc(gram_diag, 1)
                if m == G0 + 2:
                    wait(gram_diag, NG, NG)
                    dve.tensor_reduce(norms[:, 0, :], st[:, :, :], AX_X, ALU.add).then_inc(norm_sum, 1)
                if m == G0:
                    wait(dec_diff, 1, 1)
                    guard = cst[:, CUP:CUP + C].unsqueeze(1).broadcast_to([P, NCH, C])
                    tt(dec[:, :, :], dec[:, :, :], guard, ALU.min).then_inc(dec_arg, 1)
                if m == F0 + 1:
                    wait(norm_sqrt, 1, 1)
                    dve.reciprocal(rk[:, 1, :], rk[:, 0, :]).then_inc(rk_ready, 1)
                    wait(rk_ready, 2, 1)
                    tt(qd[:, 0, :], cur[:, BETA, :], rk[:, 1, :], ALU.mult).then_inc(rk_ready, 1)
                    wait(rk_ready, 2, 2)
                    tt(qd[:, 1, :], qd[:, 0, :], rk[:, 1, :], ALU.mult).then_inc(qd_ready, 1)
                    wait(qd_ready, 1, 1)
                    tt(st[:, :, :], cst[:, CI2:CI2 + C].unsqueeze(1).broadcast_to([P, NCH, C]), bc(qd[:, 1, :], C), ALU.mult).then_inc(s_init, 1)

                if m == F0 + 2:
                    wait(qd_shift, 1, 1)
                    tt(qd[:, 2, :], pt[:, 0:NCH], qd[:, 1, :], ALU.mult).then_inc(qd_pair, 1)
                if m == F0 + 4:
                    wait(pair_fac, 1, 1)
                    wait(s_init, 1, 1)
                    for g in range(NG):
                        kk = pg[g][:, 0:GC * 2 * C].rearrange("p (n a c) -> p n a c", a=2, c=C)[:, :, 0, :]
                        tt(px[:, group(g), :], kk, pw[:, group(g), :], ALU.mult).then_inc(pair_x, 1)
                    for g in range(NG):
                        wait(pair_x, NG, g + 1)
                        tt(st[:, group(g), :], st[:, group(g), :], px[:, group(g), :], ALU.subtract).then_inc(s_ready, 1)
                if m == F0 + 3:
                    wait(decay_exp, 1, 1)
                    for g in range(NG):
                        both = pg[g][:, 0:GC * 2 * C].rearrange("p (n a c) -> p n a c", a=2, c=C)
                        tt(mq[:, group(g), :, :], both, dec[:, group(g), :].unsqueeze(2).broadcast_to([P, GC, 2, C]),
                           ALU.mult).then_inc(mq_ready, 1)
                lv, stage = level_step(m)
                if stage in (0, 1):
                    for g in range(NG):
                        chunks = group(g, lv)
                        cols = slice(C * (chunks.start - GC * g) + 192 * stage, 192 + 192 * stage)
                        src = pg[g][:, cols].rearrange("p (n c) -> p n c", c=C)
                        if stage == 0:
                            wait(x_mm, NG * (LEVELS - 1), NG * (lv - 1) + g + 1)
                            pattern = lvm[:, lv, :].unsqueeze(1).broadcast_to([P, chunks.stop - chunks.start, C])
                            tt(xm[:, chunks, :], src, pattern, ALU.mult).then_inc(x_ready, 1)
                        else:
                            wait(y_mm, NG * (LEVELS - 1), NG * (lv - 1) + g + 1)
                            wait(s_ready, NG * LEVELS, NG * (lv - 1) + g + 1)
                            if lv == LEVELS - 1:
                                for low, high in QUARTERS:
                                    part = st[low, chunks, 32:C]
                                    ins = tt(part, part, src[low, :, 32:C], ALU.subtract)
                                ins.then_inc(s_ready, 1)
                            else:
                                tt(st[:, chunks, :], st[:, chunks, :], src, ALU.subtract).then_inc(s_ready, 1)
                if R0 <= m < O0:
                    n, stage = (m - R0) // 3, (m - R0) % 3
                    if stage == 0 and n > 0:
                        wait(ks_mm, NCH - 1, n)
                        if n == 1:
                            wait(tok_done, ALL_TOK, V_TOK)
                        dve.scalar_tensor_tensor(rr[:, :], pg[0][:, 0:HD], cur[:, NEG_EG, n:n + 1], vtok[:, n, :],
                                                 ALU.mult, ALU.add).then_inc(r_ready, 1)
                    if stage == 2:
                        if n < NCH - 1:
                            wait(st_mm, NCH - 1, n + 1)
                            if n > 0:
                                wait(st_upd, 2 * (NCH - 1), 2 * n)
                            for hd in range(2):
                                if n == 0:
                                    dve.tensor_copy(state[:, hd, :], pg[1 + hd][:, 0:HD]).then_inc(st_upd, 1)
                                else:
                                    dve.scalar_tensor_tensor(state[:, hd, :], state[:, hd, :], cur[:, GLA + hd, n:n + 1],
                                                             pg[1 + hd][:, 0:HD], ALU.mult, ALU.add).then_inc(st_upd, 1)
                        if n > 0:
                            wait(qkv_mm, NCH - 1, n)
                            wait(o_inter, NCH - 1, n)
                            tt(oo[:, n - 1, :], oo[:, n - 1, :], pt[:, 128:128 + HD], ALU.add).then_inc(o_ready, 1)
                if m == O0 + 1:
                    wait(o_ssq, NCH - 1, NCH - 1)
                    wait(tok_done, ALL_TOK, ALL_TOK)
                    dve.tensor_scalar(oss[:, 3, :], norms[:, 1, 1:NCH], EPS, EPS * HD * HD, ALU.add, ALU.mult).then_inc(o_fac, 1)
                    wait(o_fac, 1, 1)
                    tt(oss[:, 1, :], oss[:, 0, :], oss[:, 3, :], ALU.add).then_inc(o_var, 1)
                if m == O0 + 2:
                    wait(o_sqrt, 1, 1)
                    dve.reciprocal(oss[:, 1, :], oss[:, 2, :]).then_inc(o_rstd, 1)
                    wait(o_rstd, 1, 1)
                    tt(oo[:, 0:4, :], oo[:, 0:4, :], bc(oss[:, 1, 0:4], HD), ALU.mult).then_inc(o_scaled, 1)
                if m == O0 + 3:
                    tt(oo[:, 4:8, :], oo[:, 4:8, :], bc(oss[:, 1, 4:8], HD), ALU.mult).then_inc(o_scaled, 1)
                for b in range(2):
                    if m == O0 + 5 + 2 * b:
                        wait(o_tr, 2, b + 1)
                        if b == 0:
                            wait(silu_done, 4, 4)
                        src = (pt if b == 0 else pg[0])[:, :].rearrange("p (n h c) -> p n h c", h=2, c=C)
                        for hd in range(2):
                            part = sz[:, hd, 256 * b:256 * (b + 1)].rearrange("p (n c) -> p n c", c=C)
                            dve.scalar_tensor_tensor(part, src[:, :, hd, :], dnw, part, ALU.mult, ALU.mult).then_inc(y_ready, 1)

            def pair_windows(p, d):
                for k in range(4):
                    for j in range(4):
                        def hook(q, k=k, j=j):
                            if k == 0 and j == 0 and q == 0:
                                dve.tensor_copy(convcur[:, :, :, :].rearrange("p t k h -> p (t k) h"),
                                                convc[:, :, :, bass.ds(2 * p, 2)].rearrange("p t k h -> p (t k) h")).then_inc(conv_cur, 1)
                            if d is not None:
                                delta(d, 16 * k + 4 * j + q)
                            if k < 3 and j == 2:
                                convolve(p, k, 0, q)
                            if k > 0 and j == 0:
                                convolve(p, k - 1, 1, q)
                        window(CP_PAIR0 + 4 * p + k, k % 2, j, hook)

            pair_windows(0, None)
            with dve.Fori(1, PAIRS) as p:
                pair_windows(p, p - 1)
            for k in range(4):
                for j in range(4):
                    window(CP_GATE0 + k, k % 2, j, lambda q, k=k, j=j: delta(PAIRS - 1, 16 * k + 4 * j + q))
            with dve.Fori(2, NGATE // 2 - 1) as i:
                for k in range(2):
                    for j in range(4):
                        window(CP_GATE0 + 2 * i + k, k, j, lambda q: None)
            def split_b(jp, j, q):
                c, u = j // 3, j % 3
                dve.wait_ge(hib, 24 * jp + 4 * j + q + 1)
                tt(bwl[:, u, 2 * q:2 * q + 2, :], rawb[:, u, 2 * q:2 * q + 2, c * P:(c + 1) * P],
                   bwh[:, u, 2 * q:2 * q + 2, :].bitcast(F32), ALU.subtract).then_inc(lob, 1)

            def y_lo_part(k):
                dve.wait_ge(y_hi, k + 1)
                tt(yl[:, k, :], yraw[:, k, :], yh[:, k, :].bitcast(F32), ALU.subtract).then_inc(y_lo, 1)

            def into_b(j, q):
                if j >= 2:
                    split_b(0, j - 2, q)
                y_lo_part(4 * j + q)

            for j in range(4):
                window(NCP - 2, 0, j, lambda q: None)
            for j in range(4):
                window(NCP - 1, 1, j, lambda q, j=j: into_b(j, q), last=True)

            def merge(jp, c):
                dve.wait_ge(peb, 6 * jp + 3 * c + 3)
                dve.wait_ge(gate_loaded[c], 32 * jp + 32)
                for i in range(2):
                    tt(gst[c][:, i, :], gst[c][:, i, :], pj[c][:, i, :], ALU.mult).then_inc(mg_step, 1)
                dve.wait_ge(mg_step, 4 * jp + 2 * c + 2)
                tt(merged[:, bass.ds(2 * jp + c, 1), :].rearrange("p a t -> p (a t)"), gst[c][:, 0, :], gst[c][:, 1, :],
                   ALU.add).then_inc(mg_done, 1)

            def split_c(cp, par, j, q):
                c, h = j // 2, j % 2
                dve.wait_ge(hic, 16 * cp + 4 * j + q + 1)
                tt(cwl[:, j, 2 * q:2 * q + 2, :], rawc[2 * par + h][:, 2 * q:2 * q + 2, c * P:(c + 1) * P],
                   cwh[:, j, 2 * q:2 * q + 2, :].bitcast(F32), ALU.subtract).then_inc(loc, 1)

            def m_lo_part(k):
                dve.wait_ge(m_hi, k + 1)
                if isinstance(k, int):
                    high = mh0[:, k, :] if k < UK else mh1[:, k - UK, :]
                    tt(ml[:, k, :], merged[:, k, :], high.bitcast(F32), ALU.subtract).then_inc(m_lo, 1)
                else:
                    one = bass.ds(k, 1)
                    tt(ml[:, one, :], merged[:, one, :], mh0[:, one, :].bitcast(F32), ALU.subtract).then_inc(m_lo, 1)

            def window_b(jp, j, mode):
                for q in range(4):
                    if j < 4:
                        split_b(jp, j + 2, q)
                    elif mode != "last":
                        split_b(jp + 1, j - 4, q)
                    else:
                        split_c(0, 0, j - 4, q)
                        if j == 4:
                            m_lo_part(UK + q)
                        elif q < 3:
                            m_lo_part(UK + 4 + q)
                    if mode == "first" and j < 2:
                        y_lo_part(16 + 4 * j + q)
                if mode in ("low", "turn") and j == 1:
                    m_lo_part(2 * jp - 1)
                if mode in ("first", "low") and j == 4:
                    m_lo_part(2 * jp)
                if j % 3 == 2:
                    merge(jp, j // 3)

            for j in range(6):
                window_b(0, j, "first")
            with dve.Fori(1, UK // 2) as jp:
                for j in range(6):
                    window_b(jp, j, "low")
            for j in range(6):
                window_b(UK // 2, j, "turn")
            with dve.Fori(UK // 2 + 1, D // CW - 1) as jp:
                for j in range(6):
                    window_b(jp, j, "high")
            for j in range(6):
                window_b(D // CW - 1, j, "last")
            m_lo_part(KT - 1)

            def weigh(count):
                dve.wait_ge(c_ssq, 4 * count)
                if isinstance(count, int) and count == 1:
                    dve.wait_ge(fnw_loaded, 16)
                cols = bass.ds((count - 1) * P, P)
                tt(res[:, :, cols], res[:, :, cols], fnw[:, cols].unsqueeze(1).broadcast_to([P, 4, P]), ALU.mult).then_inc(weighed, 1)

            def residual(count):
                dve.wait_ge(c_tr, count)
                if isinstance(count, int) and count == 1:
                    dve.wait_ge(xres_loaded, 16)
                if isinstance(count, int) and count == 3:
                    dve.wait_ge(xrest_loaded, 16)
                col = (count - 1) * P
                tt(res[:, :, bass.ds(col, P)], pg[0][:, :].rearrange("p (n c) -> p n c", n=4),
                   xres[:, :, bass.ds(col, P)], ALU.add).then_inc(res_done, 1)

            def pair_c(cp, par, first, last=False):
                for j in range(4):
                    for q in range(4):
                        if not (last and j >= 2):
                            split_c(*target(cp, par, j), q)
                        if q == 3 and j == 0 and not first:
                            residual(2 * cp)
                        if q == 3 and j == 2:
                            residual(2 * cp + 1)
                        if q == 3 and j == 1 and not first:
                            weigh(2 * cp)
                        if q == 3 and j == 3:
                            weigh(2 * cp + 1)

            pair_c(0, 0, True)
            pair_c(1, 1, False)
            with dve.Fori(1, D // CW // 2 - 1) as i:
                pair_c(2 * i, 0, False)
                pair_c(2 * i + 1, 1, False)
            pair_c(D // CW - 2, 0, False)
            pair_c(D // CW - 1, 1, False, last=True)
            residual(KT)
            weigh(KT)
            dve.tensor_reduce(fin[:, 0, :], ssp[:, :, :], AX_X, ALU.add).then_inc(fin_sum, 1)
            dve.wait_ge(fin_sqrt, 1)
            dve.reciprocal(fin[:, 2, :], fin[:, 1, :]).then_inc(fin_rstd, 1)
            dve.wait_ge(fin_rstd, 1)
            for n in range(3):
                for hf in range(2):
                    part = slice(hf * 1024, (hf + 1) * 1024)
                    dve.tensor_scalar(res[:, n, part], res[:, n, part], fin[:, 2, n:n + 1], None, ALU.mult).then_inc(fin_done, 1)

        @block.gpsimd
        def _(pool):
            def mix_load(g):
                need(pool, mix_mm, g)
                pool.dma_start(mixcur[:, :, :], pool_mix[0, bass.ds(g, 1), :, :].rearrange("g (c p) d -> p (g c) d", p=P)
                               ).then_inc(mix_loaded, 16)

            def branch_store(g):
                pool.wait_ge(yp_done, 2 * g + 2)
                pool.dma_start(y_d[bass.ds(g * GD, GD), :].rearrange("(c p) t -> p c t", p=P), yps[:, :, :]).then_inc(yp_stored, 16)

            for i in range(5):
                r, c0 = TILE_ROWS[i], TILE_COL[i]
                for b in range(3):
                    n = 4 * i + b
                    pool.wait_ge(x_hi, n + 1)
                    pool.tensor_tensor(xl[:, 4 * b:4 * b + 4, c0:c0 + r], fst[:, n % 4, :, 0:r],
                                       xh[:, 4 * b:4 * b + 4, c0:c0 + r].bitcast(F32), ALU.subtract).then_inc(x_lo, 1)
            pool.wait_ge(x_sq, 5)
            pool.memset(wbh[:, :, :].bitcast(F32), 0.0).then_inc(ba_zero, 1)
            pool.memset(wbl[:, :, :].bitcast(F32), 0.0).then_inc(ba_zero, 1)
            pool.wait_ge(x_tr, 20)
            mix_load(0)
            branch_store(0)
            pool.wait_ge(gsum_row, 1)
            for h in range(2):
                pool.dma_start(g_d[:, h, :, :], grow[0:PAIRS * NCH, h * C:(h + 1) * C]).then_inc(gsum_stored, 16)
            with pool.Fori(1, GROUPS) as g:
                mix_load(g)
                branch_store(g)
            pool.wait_ge(yp_stored, 16 * GROUPS)
            pool.wait_ge(proj_evac, 4 * GROUPS)
            pool.memset(xin[:, 0:TAPS - 1], 0.0).then_inc(zeroed, 1)
            pool.memset(kq[:, :, 0, :, 0:PAD], 0.0).then_inc(zeroed, 1)
            pool.memset(vch[:, 0, :, 0:PAD], 0.0).then_inc(zeroed, 1)

            pool.dma_start(lvm[:, :, :], consts[:, CLEV:NCOLS].rearrange("p (l c) -> p l c", l=LEVELS)).then_inc(masks_loaded, 16)

            def row_load(d):
                for h in range(2):
                    src = g_d[bass.ds(d, 1), h, :, :].rearrange("a n c -> a (n c)").broadcast_to([64, NCH * C])
                    pool.dma_start(tm[64 * h:64 * h + 64, :, :].rearrange("p n c -> p (n c)"), src).then_inc(rowg_loaded, 16)

            pool.wait_ge(gsum_stored, 32)
            pool.sem_inc(work_free, 1)
            with pool.Fori(0, PAIRS) as d:
                row_load(d)
                pool.wait_ge(cur_ready, d + 1)
                pool.wait_ge(rowg_loaded, 32 * d + 32)
                pool.tensor_tensor(dec[:, :, :], tm[:, :, :], bc(cur[:, GCUM, :], C), ALU.subtract).then_inc(dec_diff, 1)
                pool.wait_ge(decay_exp, d + 1)
                pool.tensor_tensor(pw, dec[:, :, :], cst[:, CPAIR:CPAIR + C].unsqueeze(1).broadcast_to([P, NCH, C]), ALU.mult).then_inc(pair_dec, 1)
                pool.wait_ge(pair_dec, d + 1)
                pool.wait_ge(qd_pair, d + 1)
                pool.tensor_tensor(pw, pw, bc(qd[:, 2, :], C), ALU.mult).then_inc(pair_fac, 1)
                for g in range(NG):
                    pool.wait_ge(s_ready, d * (NG * LEVELS) + NG * (LEVELS - 1) + g + 1)
                    pool.tensor_tensor(sq[:, group(g), :, :], st[:, group(g), :].unsqueeze(2).broadcast_to([P, GC, 2, C]),
                                       cst[:, CHALF:CHALF + 2].unsqueeze(1).unsqueeze(3).broadcast_to([P, GC, 2, C]),
                                       ALU.mult).then_inc(sq_ready, 1)
                pool.wait_ge(y_ready, 4 * d + 4)
                pool.dma_start(y_d[bass.ds(PW + CW * d, CW), :].rearrange("(h e) t -> e h t", e=P), sz[:, :, :]).then_inc(y_stored, 16)
                pool.wait_ge(y_stored, 16 * d + 16)
                pool.sem_inc(work_free, 1)

            def gate_load(jp, c, first):
                if first:
                    pool.wait_ge(pe_piece, 4 * NCP)
                    pool.wait_ge(gate_stored[0], 16 * NGATE)
                    pool.wait_ge(gate_stored[1], 16 * NGATE)
                else:
                    pool.wait_ge(mg_done, 2 * jp + c - 1)
                for i in range(2):
                    pool.dma_start(gst[c][:, i, :], gates_d[bass.ds(jp * CW + c * P + i * D, P), :]).then_inc(gate_loaded[c], 16)

            for c in range(2):
                gate_load(0, c, True)
            with pool.Fori(1, D // CW) as jp:
                for c in range(2):
                    gate_load(jp, c, False)


_INS = ["x", "meta_tokens", "norm_w", "w_in", "conv_w", "A_log", "dt_bias", "pool_mix", "pool_scale", "dn_norm_w",
        "w_pool_out", "w_dn_out", "w_o", "final_norm_w"]


def kernel(**inputs):
    import numpy as np
    import concourse.bacc as bacc
    from concourse.bass_utils import run_bass_kernel_spmd

    nc = bacc.Bacc("TRN2", target_bir_lowering=False, num_devices=1)
    arrays = {f"in_{n}": np.ascontiguousarray(inputs[n]) for n in _INS}
    arrays["in_consts"] = constants()
    args = [nc.dram_tensor(n, a.shape, mybir.dt.from_np(a.dtype), kind="ExternalInput").ap() for n, a in arrays.items()]
    out = nc.dram_tensor("out", (1, SEQ, D), F32, kind="ExternalOutput").ap()
    build(nc, *args, out)
    return run_bass_kernel_spmd(nc, [arrays], core_ids=[0]).results[0]["out"]
```
